# Optimizing a Trainium2 kernel written in Bass

```python
import jax, jax.numpy as jnp
from jax import lax
import numpy as np

D_MODEL = 1024
BATCH = 1
SEQ = 2048
DEPTH = 1

H_DN = 4
DK_DN = 128
DV_DN = 128
SHORT_CONV = 4
CHUNK = 64
H_FOX = 4
D_FOX = 128
Q_BLOCK = 128
C_CONV = 512
CONV_WIDTH = 31
N_GROUPS = 4
EXPERTS_PER_GROUP = 8
N_EXPERTS = N_GROUPS * EXPERTS_PER_GROUP
TOP_K = 2
D_EXPERT = 256
EXPERT_BLOCK = 128

EPS = 1e-6

IN_SIZES = (H_DN * DK_DN, H_DN * DK_DN, H_DN * DV_DN, H_DN * DV_DN, H_DN, H_DN,
            H_FOX * D_FOX, H_FOX * D_FOX, H_FOX * D_FOX, H_FOX,
            2 * C_CONV, D_MODEL, D_MODEL, D_MODEL)
D_IN = sum(IN_SIZES)

kernel_name = "hybrid_deltanet_fox_conformer_hmoe"

def rms_norm(x, g):
    xf = x.astype(jnp.float32)
    y = xf * lax.rsqrt(jnp.mean(xf * xf, axis=-1, keepdims=True) + EPS)
    return (y * g.astype(jnp.float32)).astype(x.dtype)

def l2_normalize(x):
    xf = x.astype(jnp.float32)
    return (xf * lax.rsqrt(jnp.sum(xf * xf, axis=-1, keepdims=True) + EPS)).astype(x.dtype)

def causal_depthwise_conv(x, w):
    k = w.shape[0]
    return lax.conv_general_dilated(
        x, w[:, None, :].astype(x.dtype), window_strides=(1,), padding=[(k - 1, 0)],
        dimension_numbers=("NWC", "WIO", "NWC"), feature_group_count=x.shape[-1])

def _to_chunks(a):
    b, t, hh = a.shape[:3]
    a = a.reshape(b, t // CHUNK, CHUNK, hh, *a.shape[3:])
    return jnp.moveaxis(a, 3, 1)

def gated_delta_rule(q, k, v, beta, g):
    out_dtype = v.dtype
    f32 = jnp.float32
    b, t, hh, dk = q.shape
    dv = v.shape[-1]
    q, k, v = (_to_chunks(a.astype(f32)) for a in (q, k, v))
    beta = _to_chunks(beta.astype(f32))
    g = _to_chunks(g.astype(f32))
    q = q * dk ** -0.5
    kb = k * beta[..., None]
    vb = v * beta[..., None]
    gc = jnp.cumsum(g, axis=-1)
    causal = jnp.tril(jnp.ones((CHUNK, CHUNK), bool))
    strict = jnp.tril(jnp.ones((CHUNK, CHUNK), bool), -1)
    diff = gc[..., :, None] - gc[..., None, :]
    decay = jnp.where(causal, jnp.exp(jnp.where(causal, diff, 0.0)), 0.0)
    a_mat = jnp.where(strict, jnp.einsum("bhncd,bhnsd->bhncs", kb, k) * decay, 0.0)
    lhs = a_mat + jnp.eye(CHUNK, dtype=f32)
    rhs = jnp.concatenate([vb, kb * jnp.exp(gc)[..., None]], axis=-1)
    sol = lax.linalg.triangular_solve(lhs, rhs, left_side=True, lower=True, unit_diagonal=True)
    u, w = sol[..., :dv], sol[..., dv:]
    qk = jnp.where(causal, jnp.einsum("bhncd,bhnsd->bhncs", q, k) * decay, 0.0)

    def step(state, xs):
        qi, ki, ui, wi, gi, ai = xs
        v_new = ui - jnp.einsum("bhck,bhkv->bhcv", wi, state)
        o = (jnp.einsum("bhck,bhkv->bhcv", qi * jnp.exp(gi)[..., None], state)
             + jnp.einsum("bhcs,bhsv->bhcv", ai, v_new))
        g_last = gi[..., -1]
        state = (state * jnp.exp(g_last)[..., None, None]
                 + jnp.einsum("bhck,bhcv->bhkv", ki * jnp.exp(g_last[..., None] - gi)[..., None], v_new))
        return state, o

    xs = tuple(jnp.moveaxis(a, 2, 0) for a in (q, k, u, w, gc, qk))
    s0 = jnp.zeros((b, hh, dk, dv), f32)
    _, o = lax.scan(step, s0, xs)
    o = jnp.moveaxis(o, 0, 2).reshape(b, hh, t, dv)
    return o.transpose(0, 2, 1, 3).astype(out_dtype)

def forgetting_attention(q, k, v, log_f):
    out_dtype = v.dtype
    f32 = jnp.float32
    b, t, hh, d = q.shape
    nb = t // Q_BLOCK
    c = jnp.cumsum(log_f.astype(f32), axis=1)
    qb = q.astype(f32).reshape(b, nb, Q_BLOCK, hh, d).transpose(1, 0, 3, 2, 4)
    cq = c.reshape(b, nb, Q_BLOCK, hh).transpose(1, 0, 3, 2)
    kt = k.astype(f32).transpose(0, 2, 1, 3)
    vt = v.astype(f32).transpose(0, 2, 1, 3)
    ck = c.transpose(0, 2, 1)
    kpos = jnp.arange(t)
    scale = d ** -0.5

    def block(args):
        qi, ci, start = args
        s = jnp.einsum("bhqd,bhkd->bhqk", qi, kt) * scale + (ci[..., :, None] - ck[:, :, None, :])
        qpos = start + jnp.arange(Q_BLOCK)
        s = jnp.where(kpos[None, :] <= qpos[:, None], s, -jnp.inf)
        return jnp.einsum("bhqk,bhkd->bhqd", jax.nn.softmax(s, axis=-1), vt)

    o = lax.map(block, (qb, cq, jnp.arange(nb) * Q_BLOCK))
    return o.transpose(1, 0, 3, 2, 4).reshape(b, t, hh, d).astype(out_dtype)

def conformer_conv_module(u, dw_w, dw_b, ln_g, ln_b):
    a, gate = jnp.split(u, 2, axis=-1)
    z = a * jax.nn.sigmoid(gate)
    z = causal_depthwise_conv(z, dw_w) + dw_b
    zf = z.astype(jnp.float32)
    mu = jnp.mean(zf, axis=-1, keepdims=True)
    var = jnp.mean(jnp.square(zf - mu), axis=-1, keepdims=True)
    zf = (zf - mu) * lax.rsqrt(var + EPS) * ln_g.astype(jnp.float32) + ln_b.astype(jnp.float32)
    return jax.nn.silu(zf).astype(u.dtype)

def hierarchical_moe(h, wg, bg, we, be, w1, w3, w2):
    bsz, t, d = h.shape
    n = bsz * t
    xf = h.reshape(n, d)
    glog = (xf @ wg + bg).astype(jnp.float32)
    gprob = jax.nn.softmax(glog, axis=-1)
    grp = jnp.argmax(glog, axis=-1)
    p_grp = jnp.take_along_axis(gprob, grp[:, None], axis=-1)
    elog = (xf @ we + be).astype(jnp.float32).reshape(n, N_GROUPS, EXPERTS_PER_GROUP)
    elog_g = jnp.take_along_axis(elog, grp[:, None, None], axis=1)[:, 0]
    top_v, top_i = lax.top_k(elog_g, TOP_K)
    gate = p_grp * jax.nn.softmax(top_v, axis=-1)
    eid = (grp[:, None] * EXPERTS_PER_GROUP + top_i).astype(jnp.int32)

    a = n * TOP_K
    eid_f = eid.reshape(a)
    tok_f = jnp.repeat(jnp.arange(n, dtype=jnp.int32), TOP_K)
    gate_f = gate.reshape(a)
    order = jnp.argsort(eid_f)
    s_eid, s_tok, s_gate = eid_f[order], tok_f[order], gate_f[order]
    counts = jnp.bincount(eid_f, length=N_EXPERTS).astype(jnp.int32)
    start = jnp.cumsum(counts) - counts
    padded = ((counts + EXPERT_BLOCK - 1) // EXPERT_BLOCK) * EXPERT_BLOCK
    pend = jnp.cumsum(padded)
    pstart = pend - padded
    dest = pstart[s_eid] + (jnp.arange(a, dtype=jnp.int32) - start[s_eid])
    nb = -(-a // EXPERT_BLOCK) + N_EXPERTS
    p = nb * EXPERT_BLOCK
    buf_tok = jnp.zeros((p,), jnp.int32).at[dest].set(s_tok)
    buf_gate = jnp.zeros((p,), jnp.float32).at[dest].set(s_gate)
    blk_eid = jnp.minimum(jnp.searchsorted(pend, jnp.arange(nb, dtype=jnp.int32) * EXPERT_BLOCK, side="right"),
                          N_EXPERTS - 1)

    def expert_block(args):
        toks, e = args
        xb = xf[toks]
        return (jax.nn.silu(xb @ w1[e]) * (xb @ w3[e])) @ w2[e]

    yb = lax.map(expert_block, (buf_tok.reshape(nb, EXPERT_BLOCK), blk_eid))
    y = jnp.zeros((n, d), h.dtype).at[buf_tok].add(yb.reshape(p, d) * buf_gate[:, None].astype(h.dtype))
    return y.reshape(bsz, t, d)

def setup_inputs(seed: int = 0) -> dict:
    key = jax.random.key(seed)
    ks = jax.random.split(key, 24)
    L, D = DEPTH, D_MODEL
    f32 = jnp.float32
    nrm = lambda k, shape, scale: jax.random.normal(k, shape, f32) * scale
    qkv_dn = 2 * H_DN * DK_DN + H_DN * DV_DN
    dt = jnp.exp(jax.random.uniform(ks[5], (L, H_DN), f32, np.log(1e-3), np.log(1e-1)))
    return {
        "x": jax.random.normal(ks[0], (BATCH, SEQ, D), f32),
        "norm_mix": 1.0 + nrm(ks[1], (L, D), 0.02),
        "w_in": nrm(ks[2], (L, D, D_IN), D ** -0.5),
        "conv_qkv": nrm(ks[3], (L, SHORT_CONV, qkv_dn), SHORT_CONV ** -0.5),
        "dn_a_log": jnp.log(jax.random.uniform(ks[4], (L, H_DN), f32, 1.0, 16.0)),
        "dn_dt_bias": dt + jnp.log(-jnp.expm1(-dt)),
        "dn_norm": 1.0 + nrm(ks[6], (L, DV_DN), 0.02),
        "fox_bias": jax.random.uniform(ks[7], (L, H_FOX), f32, 1.0, 6.0),
        "conv_dw": nrm(ks[8], (L, CONV_WIDTH, C_CONV), CONV_WIDTH ** -0.5),
        "conv_dw_b": nrm(ks[9], (L, C_CONV), 0.02),
        "conv_ln_g": 1.0 + nrm(ks[10], (L, C_CONV), 0.02),
        "conv_ln_b": nrm(ks[11], (L, C_CONV), 0.02),
        "w_a": nrm(ks[12], (L, H_DN * DV_DN, D), (H_DN * DV_DN) ** -0.5),
        "w_b": nrm(ks[13], (L, H_FOX * D_FOX, D), (H_FOX * D_FOX) ** -0.5),
        "w_c": nrm(ks[14], (L, C_CONV, D), C_CONV ** -0.5),
        "w_out": nrm(ks[15], (L, D, D), D ** -0.5),
        "norm_ffn": 1.0 + nrm(ks[16], (L, D), 0.02),
        "router_group_w": nrm(ks[17], (L, D, N_GROUPS), D ** -0.5),
        "router_group_b": nrm(ks[18], (L, N_GROUPS), 0.01),
        "router_expert_w": nrm(ks[19], (L, D, N_EXPERTS), D ** -0.5),
        "router_expert_b": nrm(ks[20], (L, N_EXPERTS), 0.01),
        "expert_w1": nrm(ks[21], (L, N_EXPERTS, D, D_EXPERT), D ** -0.5),
        "expert_w3": nrm(ks[22], (L, N_EXPERTS, D, D_EXPERT), D ** -0.5),
        "expert_w2": nrm(ks[23], (L, N_EXPERTS, D_EXPERT, D), D_EXPERT ** -0.5),
        "norm_final": 1.0 + nrm(jax.random.fold_in(key, 99), (D,), 0.02),
    }

def reference(x, norm_mix, w_in, conv_qkv, dn_a_log, dn_dt_bias, dn_norm, fox_bias,
              conv_dw, conv_dw_b, conv_ln_g, conv_ln_b, w_a, w_b, w_c, w_out,
              norm_ffn, router_group_w, router_group_b, router_expert_w, router_expert_b,
              expert_w1, expert_w3, expert_w2, norm_final):
    b, t, _ = x.shape
    split_idx = np.cumsum(IN_SIZES)[:-1].tolist()
    qk_w = H_DN * DK_DN
    for l in range(DEPTH):
        h = rms_norm(x, norm_mix[l])
        proj = h @ w_in[l]
        (qa, ka, va, za, ba, aa, qb, kb, vb, fb, uc, ga, gb, gc) = jnp.split(proj, split_idx, axis=-1)

        qkv = jax.nn.silu(causal_depthwise_conv(jnp.concatenate([qa, ka, va], axis=-1), conv_qkv[l]))
        qa, ka, va = qkv[..., :qk_w], qkv[..., qk_w:2 * qk_w], qkv[..., 2 * qk_w:]
        qa = l2_normalize(qa.reshape(b, t, H_DN, DK_DN))
        ka = l2_normalize(ka.reshape(b, t, H_DN, DK_DN))
        va = va.reshape(b, t, H_DN, DV_DN)
        beta = jax.nn.sigmoid(ba.astype(jnp.float32))
        g_log = -jnp.exp(dn_a_log[l].astype(jnp.float32)) * jax.nn.softplus(
            aa.astype(jnp.float32) + dn_dt_bias[l].astype(jnp.float32))
        oa = gated_delta_rule(qa, ka, va, beta, g_log)
        oa = rms_norm(oa, dn_norm[l]) * jax.nn.silu(za.reshape(b, t, H_DN, DV_DN))
        ya = oa.reshape(b, t, H_DN * DV_DN) @ w_a[l]

        log_f = jax.nn.log_sigmoid(fb.astype(jnp.float32) + fox_bias[l].astype(jnp.float32))
        ob = forgetting_attention(qb.reshape(b, t, H_FOX, D_FOX), kb.reshape(b, t, H_FOX, D_FOX),
                                  vb.reshape(b, t, H_FOX, D_FOX), log_f)
        yb = ob.reshape(b, t, H_FOX * D_FOX) @ w_b[l]

        yc = conformer_conv_module(uc, conv_dw[l], conv_dw_b[l], conv_ln_g[l], conv_ln_b[l]) @ w_c[l]

        merged = jax.nn.sigmoid(ga) * ya + jax.nn.sigmoid(gb) * yb + jax.nn.sigmoid(gc) * yc
        x = x + merged @ w_out[l]

        h2 = rms_norm(x, norm_ffn[l])
        x = x + hierarchical_moe(h2, router_group_w[l], router_group_b[l], router_expert_w[l],
                                 router_expert_b[l], expert_w1[l], expert_w3[l], expert_w2[l])
    return rms_norm(x, norm_final)


_drawn_inputs = setup_inputs


def setup_inputs(seed=0):
    import zlib

    import numpy as np

    out = dict(_drawn_inputs(seed))
    spreads = {}
    factors = {'dn_norm': 11.005,
     'conv_dw_b': 2.728,
     'conv_ln_g': 9.216,
     'conv_ln_b': 9.453,
     'router_group_b': 11.127,
     'router_expert_b': 12.132,
     'norm_final': 8.161,
     'norm_ffn': 3.306}
    for name, (base, spread) in spreads.items():
        noise = np.random.default_rng([zlib.crc32(name.encode()), seed]).standard_normal(out[name].shape)
        drawn = base * np.exp(spread * noise) if base else spread * noise
        out[name] = __import__('jax').numpy.asarray(drawn.astype(out[name].dtype))
    for name, factor in factors.items():
        out[name] = (out[name] * factor).astype(out[name].dtype)
    return out
```

```python
from contextlib import ExitStack

import numpy as np

import concourse.bass as bass
from concourse import mybir

ALU = mybir.AluOpType
ACT = mybir.ActivationFunctionType
AX = mybir.AxisListType
F32 = mybir.dt.float32
I32 = mybir.dt.int32
U8 = mybir.dt.uint8
U32 = mybir.dt.uint32

P = 128
T = 2048
D = 1024
KD = D // P
NT = T // P
G = 512
NG = T // G
GT = G // P
H = 4
KC = 4
NPAD = 64
N_EXP = 32
N_GRP = 4
PER_GRP = N_EXP // N_GRP
DE = 256
BLK = 128
NB = 2 * T // BLK + N_EXP
SLOTS = 4
W_CONV = 31
LEVELS = 7
W_SHORT = 4
EPS = 1e-6
BIG = 1e30
Q_A, K_A, V_A, Z_A, Q_B, K_B, V_B, C_A, C_G, GATE_A, GATE_B, GATE_C = 0, 4, 8, 12, 16, 20, 24, 28, 32, 36, 44, 52
N_BLOCKS = 60
R_BETA, R_DECAY, R_FORGET, R_ALL = 0, 32, 64, 96


class Phase:

    def __init__(self, nc, name):
        self.nc, self.name, self.ctx, self.used = nc, name, ExitStack(), []

    def __enter__(self):
        self.ctx.__enter__()
        return self

    def __exit__(self, *a):
        self.ctx.__exit__(*a)
        if a[0] is None:
            self.nc.clear_and_free_semaphores(self.used)
            self.nc.all_engine_barrier()

    def sb(self, name, shape, dt=F32):
        return self.ctx.enter_context(self.nc.sbuf_tensor(f"{self.name}_{name}", shape, dt))

    def ps(self, name, shape, dt=F32):
        return self.ctx.enter_context(self.nc.psum_tensor(f"{self.name}_{name}", shape, dt))

    def sem(self, name):
        self.used.append(self.nc.alloc_semaphore(f"{self.name}_{name}"))
        return self.used[-1]

    def sems(self, name, n):
        return [self.sem(f"{name}{i}") for i in range(n)]

    def block(self):
        return self.ctx.enter_context(self.nc.Block())


class Chain:

    def __init__(self, eng, sem, per=0, round_=None):
        self.eng, self.sem, self.per, self.round, self.n = eng, sem, per, round_, 0

    def did(self, ins):
        ins.then_inc(self.sem, 1)
        self.n += 1
        return self.n

    def wait(self, n=None):
        n = self.n if n is None else n
        self.eng.wait_ge(self.sem, n if self.round is None else self.round * self.per + n)

    def end(self):
        assert self.n == self.per, (self.n, self.per)


def rounds(eng, n, first, both, last, ahead=1):
    first()
    loop = (n - ahead) // 2
    with eng.Fori(0, loop) as i:
        both(i * 2, 0)
        both(i * 2 + 1, 1)
    if (n - ahead) % 2:
        both(2 * loop, 0)
    last()


def tile_of(ap, t):
    return ap[:, t] if isinstance(t, int) else ap[:, bass.ds(t, 1)]


def constants(nc, c):
    with Phase(nc, "const") as ph:
        made = ph.sem("made")
        block = ph.block()

        @block.gpsimd
        def _(pool):
            st = Chain(pool, made)
            st.did(pool.memset(c.ones[:, :], 1.0))
            for m in (c.below, c.above):
                st.did(pool.memset(m[:, :, :], 1.0))
            st.did(pool.memset(c.eps[:, :], EPS))
            st.did(pool.memset(c.ident[:, :], 0.0))
            st.did(pool.memset(c.negtri[:, :], 0.0))
            st.did(pool.memset(c.upper[:, :], 1.0))
            st.did(pool.memset(c.uppereq[:, :], 1.0))
            st.wait()
            st.did(pool.affine_select(out=c.ident[:, :], in_=c.ident[:, :], compare_op=ALU.not_equal, fill=1.0,
                                      base=0, pattern=[[-1, P]], channel_multiplier=1))
            st.did(pool.affine_select(out=c.negtri[:, :], in_=c.negtri[:, :], compare_op=ALU.is_ge, fill=-BIG,
                                      base=0, pattern=[[-1, P]], channel_multiplier=1))
            st.did(pool.affine_select(out=c.upper[:, :], in_=c.upper[:, :], compare_op=ALU.is_gt, fill=0.0,
                                      base=0, pattern=[[1, P]], channel_multiplier=-1))
            st.did(pool.affine_select(out=c.uppereq[:, :], in_=c.uppereq[:, :], compare_op=ALU.is_ge, fill=0.0,
                                      base=0, pattern=[[1, P]], channel_multiplier=-1))
            for l in range(LEVELS):
                n = 1 << l
                for m, row_lo, row_hi, col in ((c.below, n, 2 * n, (n - 1, -1)), (c.above, 0, n, (-n, 1))):
                    v = m[:, l, :].rearrange("p (b s) -> p b s", s=2 * n)
                    nb = P // (2 * n)
                    for base, pat, mult in ((-row_lo, [[-2 * n, nb], [0, 2 * n]], 1),
                                            (row_hi - 1, [[2 * n, nb], [0, 2 * n]], -1),
                                            (col[0], [[0, nb], [col[1], 2 * n]], 0)):
                        st.did(pool.affine_select(out=v, in_=v, compare_op=ALU.is_ge, fill=0.0, base=base,
                                                  pattern=pat, channel_multiplier=mult))
                        st.wait()
            st.wait()


def norm_and_transpose(nc, c, x, gain):
    with Phase(nc, "norm") as ph:
        xt = ph.sb("xt", [P, 2, D])
        xn = ph.sb("xn", [P, 2, D])
        junk = ph.sb("junk", [P, 2, D])
        ss = ph.sb("ss", [P, 2])
        sd = ph.sb("sd", [P, 2])
        rs = ph.sb("rs", [P, 2])
        gcol = ph.sb("gcol", [P, KD])
        tp = ph.ps("tp", [P, 2, D])
        x_in = ph.sems("x_in", 2)
        g_in = ph.sem("g_in")
        x_free, xn_free, tp_free = ph.sem("x_free"), ph.sem("xn_free"), ph.sem("tp_free")
        squares, sd_ready, recip, xn_ready, turned = (ph.sem(n) for n in ("squares", "sd_ready", "recip", "xn_ready", "turned"))
        block = ph.block()

        @block.sync
        def _(sp):
            sp.dma_start(gcol[:, :], gain).then_inc(g_in, 16)
            with sp.Fori(0, NT // 2) as i:
                for p in range(2):
                    sp.wait_ge(x_free, i * 2 + (p + 1))
                    sp.dma_start(xt[:, p, :], x[i * 2 + p]).then_inc(x_in[p], 16)

        @block.scalar
        def _(act):
            with act.Fori(0, NT // 2) as i:
                for p in range(2):
                    act.wait_ge(x_in[p], i * 16 + 16)
                    act.activation(junk[:, p, :], xt[:, p, :], ACT.Square, accum_out=ss[:, p:p + 1]).then_inc(squares, 1)
                for p in range(2):
                    act.wait_ge(squares, i * 2 + (p + 1))
                    act.wait_ge(x_free, i * 2 + (p + 1))
                    act.activation(sd[:, p:p + 1], ss[:, p:p + 1], ACT.Sqrt, scale=1.0 / D, bias=c.eps[:, 0:1]).then_inc(sd_ready, 1)

        @block.vector
        def _(dve):
            dve.sem_inc(x_free, 2)
            dve.wait_ge(g_in, 16)
            with dve.Fori(0, NT // 2) as i:
                for p in range(2):
                    dve.wait_ge(sd_ready, i * 2 + (p + 1))
                    dve.reciprocal(rs[:, p:p + 1], sd[:, p:p + 1]).then_inc(recip, 1)
                for p in range(2):
                    dve.wait_ge(recip, i * 2 + (p + 1))
                    dve.wait_ge(xn_free, i * 2 + (p + 1))
                    dve.tensor_scalar(xn[:, p, :], xt[:, p, :], rs[:, p:p + 1], None, ALU.mult).then_inc(x_free, 1)
                    dve.wait_ge(x_free, i * 2 + (p + 3))
                    dve.sem_inc(xn_ready, 1)
                for p in range(2):
                    dve.wait_ge(turned, i * 2 + (p + 1))
                    dve.tensor_tensor(c.hT[:, :, bass.ds(i * (2 * P) + p * P, P)], tp[:, p, :].rearrange("p (k t) -> p k t", t=P),
                                      gcol[:, :].unsqueeze(2).to_broadcast([P, KD, P]), ALU.mult).then_inc(tp_free, 1)

        @block.tensor
        def _(pe):
            pe.sem_inc(xn_free, 2)
            pe.sem_inc(tp_free, 2)
            with pe.Fori(0, NT // 2) as i:
                for p in range(2):
                    pe.wait_ge(xn_ready, i * 2 + (p + 1))
                    pe.wait_ge(tp_free, i * 2 + (p + 1))
                    for k in range(KD):
                        last = pe.transpose(tp[:, p, k * P:(k + 1) * P], xn[:, p, k * P:(k + 1) * P], c.ident[:, :])
                    last.then_inc(turned, 1)
                    pe.wait_ge(turned, i * 2 + (p + 1))
                    pe.sem_inc(xn_free, 1)


def narrow_rows(nc, c, w_narrow, sm_bias, a_log, rows_dram):
    with Phase(nc, "narrow") as ph:
        w = ph.sb("w", [P, KD, R_ALL])
        bias, coef, sign = ph.sb("bias", [R_ALL, 1]), ph.sb("coef", [R_ALL, 1]), ph.sb("sign", [R_ALL, 1])
        u, mag, sp, keep, cum = (ph.sb(n, [R_ALL, T]) for n in ("u", "mag", "sp", "keep", "cum"))
        out = ph.ps("out", [P, NG, G])
        turned = ph.ps("turned", [P, NT, P])
        w_in, b_in, stored = ph.sem("w_in"), ph.sem("b_in"), ph.sem("stored")
        projected, dve_done, act_done, cols_turned = (ph.sem(n) for n in ("projected", "dve_done", "act_done", "cols_turned"))
        block = ph.block()

        @block.sync
        def _(sp_):
            sp_.dma_start(w[:, :, :], w_narrow).then_inc(w_in, 16)
            sp_.dma_start(bias[:, :], sm_bias).then_inc(b_in, 16)
            sp_.dma_start(coef[:, :], a_log).then_inc(b_in, 16)
            sp_.wait_ge(act_done, 5)
            sp_.dma_start(rows_dram, cum[:, :]).then_inc(stored, 16)
            sp_.wait_ge(stored, 16)

        @block.tensor
        def _(pe):
            pe.wait_ge(w_in, 16)
            for g in range(NG):
                for k in range(KD):
                    last = pe.matmul(out[0:R_ALL, g, :], w[:, k, :], c.hT[:, k, g * G:(g + 1) * G], start=(k == 0), stop=(k == KD - 1))
            last.then_inc(projected, 1)
            pe.wait_ge(act_done, 5)
            for t in range(NT):
                last = pe.transpose(turned[:, t, 0:R_ALL], cum[:, t * P:(t + 1) * P], c.ident[0:R_ALL, 0:R_ALL])
            last.then_inc(cols_turned, 1)

        @block.scalar
        def _(act):
            act.wait_ge(b_in, 32)
            act.activation(coef[R_DECAY:R_DECAY + 32, :], coef[R_DECAY:R_DECAY + 32, :], ACT.Exp).then_inc(act_done, 1)
            act.wait_ge(dve_done, 3)
            act.activation(mag[:, :], u[:, :], ACT.Abs).then_inc(act_done, 1)
            act.wait_ge(act_done, 2)
            act.activation(mag[:, :], mag[:, :], ACT.Exp, scale=-1.0).then_inc(act_done, 1)
            act.wait_ge(act_done, 3)
            act.activation(sp[:, :], mag[:, :], ACT.Ln, bias=c.ones[0:R_ALL, 0:1]).then_inc(act_done, 1)
            act.wait_ge(dve_done, 6)
            act.activation(cum[R_BETA:R_BETA + H, :], out[R_BETA:R_BETA + H, :, :].rearrange("p g t -> p (g t)"), ACT.Sigmoid).then_inc(act_done, 1)

        @block.vector
        def _(dve):
            st = Chain(dve, dve_done)
            dve.wait_ge(b_in, 32)
            dve.wait_ge(act_done, 1)
            dve.memset(sign[:, :], 1.0)
            dve.memset(keep[:, :], 1.0)
            st.did(dve.tensor_scalar(coef[R_DECAY:R_DECAY + 32, :], coef[R_DECAY:R_DECAY + 32, :], -1.0, None, ALU.mult))
            st.wait()
            dve.memset(coef[R_FORGET:R_ALL, :], -1.0)
            dve.memset(sign[R_FORGET:R_ALL, :], -1.0)
            dve.memset(coef[0:32, :], -1.0)
            st.did(dve.memset(keep[R_DECAY:R_DECAY + 32, :].rearrange("p (t c) -> p t c", c=P)[:, :, 0:1], 0.0))
            st.wait()
            dve.wait_ge(projected, 1)
            st.did(dve.tensor_scalar(u[:, :], out[0:R_ALL, :, :].rearrange("p g t -> p (g t)"), bias[:, 0:1], sign[:, 0:1], ALU.add, ALU.mult))
            st.wait()
            dve.wait_ge(act_done, 4)
            st.did(dve.scalar_tensor_tensor(out=u[:, :], in0=u[:, :], scalar=0.0, in1=sp[:, :], op0=ALU.max, op1=ALU.add))
            st.wait()
            st.did(dve.tensor_scalar(u[:, :], u[:, :], coef[:, 0:1], None, ALU.mult))
            st.wait()
            st.did(dve.tensor_tensor_scan(cum[:, :], keep[:, :], u[:, :], 0.0, ALU.mult, ALU.add))
            dve.wait_ge(cols_turned, 1)
            st.did(dve.tensor_copy(c.cols[:, :, :], turned[:, :, 0:R_ALL]))
            st.wait()


def conformer(nc, c, oT, w_blocks, dw_w, dw_b, ln_g, ln_b):
    PAD = W_CONV - 1
    with Phase(nc, "conf") as ph:
        w_a, w_g = ph.sb("w_a", [P, 2, KD, P]), ph.sb("w_g", [P, 2, KD, P])
        taps, tap_b = ph.sb("taps", [P, KC, W_CONV]), ph.sb("tap_b", [P, KC])
        sg = ph.sb("sg", [P, NG, G])
        z = ph.sb("z", [P, PAD + T])
        acc = ph.sb("acc", [P, T])
        pa, pg = ph.ps("pa", [P, NG, G]), ph.ps("pg", [P, NG, G])
        w_in = ph.sems("w_in", 2)
        taps_in = ph.sem("taps_in")
        w_free, gate_done, a_done, gate_free, a_free, sg_ready, dve_done = (
            ph.sem(n) for n in ("w_free", "gate_done", "a_done", "gate_free", "a_free", "sg_ready", "dve_done"))
        block = ph.block()

        @block.sync
        def _(sp):
            sp.dma_start(taps[:, :, :], dw_w).then_inc(taps_in, 16)
            sp.dma_start(tap_b[:, :], dw_b).then_inc(taps_in, 16)
            with sp.Fori(0, KC // 2) as i:
                for p in range(2):
                    sp.wait_ge(w_free, i * 2 + (p + 1))
                    sp.dma_start(w_g[:, p, :, :], w_blocks[i * 2 + (C_G + p)]).then_inc(w_in[p], 16)
                    sp.dma_start(w_a[:, p, :, :], w_blocks[i * 2 + (C_A + p)]).then_inc(w_in[p], 16)

        @block.tensor
        def _(pe):
            pe.sem_inc(w_free, 2)
            with pe.Fori(0, KC // 2) as i:
                for p in range(2):
                    pe.wait_ge(w_in[p], i * 32 + 32)
                    for g in range(NG):
                        tok = slice(g * G, (g + 1) * G)
                        pe.wait_ge(gate_free, i * (2 * NG) + (p * NG + g + 1))
                        for k in range(KD):
                            last = pe.matmul(pg[:, g, :], w_g[:, p, k, :], c.hT[:, k, tok], start=(k == 0), stop=(k == KD - 1))
                        last.then_inc(gate_done, 1)
                        pe.wait_ge(a_free, i * (2 * NG) + (p * NG + g + 1))
                        for k in range(KD):
                            last = pe.matmul(pa[:, g, :], w_a[:, p, k, :], c.hT[:, k, tok], start=(k == 0), stop=(k == KD - 1))
                        last.then_inc(a_done, 1)
                    pe.wait_ge(a_done, i * (2 * NG) + (p + 1) * NG)
                    pe.sem_inc(w_free, 1)

        @block.scalar
        def _(act):
            act.sem_inc(gate_free, NG)
            with act.Fori(0, KC) as j:
                for g in range(NG):
                    act.wait_ge(gate_done, j * NG + (g + 1))
                    act.wait_ge(a_free, j * NG + (g + 1))
                    act.activation(sg[:, g, :], pg[:, g, :], ACT.Sigmoid).then_inc(sg_ready, 1)
                    act.wait_ge(sg_ready, j * NG + (g + 1))
                    act.sem_inc(gate_free, 1)

        @block.vector
        def _(dve):
            dve.sem_inc(a_free, NG)
            dve.memset(z[:, 0:PAD], 0.0)
            dve.wait_ge(taps_in, 32)
            with dve.Fori(0, KC) as j:
                st = Chain(dve, dve_done, NG + W_CONV, j)
                for g in range(NG):
                    dve.wait_ge(a_done, j * NG + (g + 1))
                    dve.wait_ge(sg_ready, j * NG + (g + 1))
                    st.did(dve.tensor_tensor(z[:, PAD + g * G:PAD + (g + 1) * G], pa[:, g, :], sg[:, g, :], ALU.mult))
                    st.wait()
                    dve.sem_inc(a_free, 1)
                for k in range(W_CONV):
                    tap, src = taps[:, bass.ds(j, 1), k:k + 1].rearrange("p a b -> p (a b)"), z[:, k:k + T]
                    dst = acc[:, :] if k < W_CONV - 1 else oT[:, bass.ds(j, 1), :].rearrange("p a t -> p (a t)")
                    if k == 0:
                        st.did(dve.tensor_scalar(dst, src, tap, tap_b[:, bass.ds(j, 1)], ALU.mult, ALU.add))
                    else:
                        st.did(dve.scalar_tensor_tensor(out=dst, in0=src, scalar=tap, in1=acc[:, :], op0=ALU.mult, op1=ALU.add))
                    st.wait()
                st.end()

    with Phase(nc, "ln") as ph:
        mean_w = ph.sb("mean_w", [P, P])
        g_col, b_col = ph.sb("g_col", [P, KC]), ph.sb("b_col", [P, KC])
        sq = ph.sb("sq", [P, KC, G])
        sd, rs = ph.sb("sd", [P, 2, G]), ph.sb("rs", [P, 2, G])
        mu, var = ph.ps("mu", [P, NG, G]), ph.ps("var", [P, NG, G])
        cols_in, w_ready, mu_done, var_done, centred, squared, sd_ready, scaled, rs_ready, act_done = (
            ph.sem(n) for n in ("cols_in", "w_ready", "mu_done", "var_done", "centred", "squared", "sd_ready", "scaled", "rs_ready", "act_done"))
        block = ph.block()

        @block.sync
        def _(sp):
            sp.dma_start(g_col[:, :], ln_g).then_inc(cols_in, 16)
            sp.dma_start(b_col[:, :], ln_b).then_inc(cols_in, 16)

        @block.gpsimd
        def _(pool):
            pool.memset(mean_w[:, :], 1.0 / (KC * P)).then_inc(w_ready, 1)

        @block.tensor
        def _(pe):
            pe.wait_ge(w_ready, 1)
            for g in range(NG):
                for j in range(KC):
                    last = pe.matmul(mu[:, g, :], mean_w[:, :], oT[:, j, g * G:(g + 1) * G], start=(j == 0), stop=(j == KC - 1))
                last.then_inc(mu_done, 1)
            for g in range(NG):
                pe.wait_ge(squared, g + 1)
                for j in range(KC):
                    last = pe.matmul(var[:, g, :], mean_w[:, :], sq[:, j, :], start=(j == 0), stop=(j == KC - 1))
                last.then_inc(var_done, 1)

        @block.scalar
        def _(act):
            act.wait_ge(cols_in, 32)
            for g in range(NG):
                act.wait_ge(centred, g + 1)
                if g:
                    act.wait_ge(var_done, g)
                act.activation(sq[:, :, :], oT[:, :, g * G:(g + 1) * G], ACT.Square).then_inc(squared, 1)
                act.wait_ge(var_done, g + 1)
                if g >= 2:
                    act.wait_ge(rs_ready, g - 1)
                act.activation(sd[:, g % 2, :], var[:, g, :], ACT.Sqrt, bias=c.eps[:, 0:1]).then_inc(sd_ready, 1)
            for g in range(NG):
                act.wait_ge(scaled, g + 1)
                for j in range(KC):
                    part = oT[:, j, g * G:(g + 1) * G]
                    act.activation(part, part, ACT.Silu, scale=g_col[:, j:j + 1], bias=b_col[:, j:j + 1])

        @block.vector
        def _(dve):
            for g in range(NG):
                part = oT[:, :, g * G:(g + 1) * G]
                dve.wait_ge(mu_done, g + 1)
                dve.tensor_tensor(part, part, mu[:, g, :].unsqueeze(1).to_broadcast([P, KC, G]), ALU.subtract).then_inc(centred, 1)
            for g in range(NG):
                part = oT[:, :, g * G:(g + 1) * G]
                dve.wait_ge(sd_ready, g + 1)
                if g >= 2:
                    dve.wait_ge(scaled, g - 1)
                dve.reciprocal(rs[:, g % 2, :], sd[:, g % 2, :]).then_inc(rs_ready, 1)
                dve.wait_ge(rs_ready, g + 1)
                dve.wait_ge(centred, g + 1)
                dve.wait_ge(squared, g + 1)
                dve.tensor_tensor(part, part, rs[:, g % 2, :].unsqueeze(1).to_broadcast([P, KC, G]), ALU.mult).then_inc(scaled, 1)


def gated_merge(nc, c, oT, w_blocks, gate, w_mix, mix, merged, first):
    with Phase(nc, f"merge{mix}") as ph:
        w_g, w_y = ph.sb("w_g", [P, 2, KD, P]), ph.sb("w_y", [P, 2, KC, P])
        sg = ph.sb("sg", [P, NG, G])
        res = ph.sb("res", [P, 2, NG, G])
        old = None if first else ph.sb("old", [P, 2, NG, G])
        pg, py = ph.ps("pg", [P, NG, G]), ph.ps("py", [P, NG, G])
        w_in, old_in, stored = ph.sems("w_in", 2), ph.sems("old_in", 2), ph.sems("stored", 2)
        w_free, gate_done, y_done, gate_free, y_free, sg_ready, gated, summed, res_free = (
            ph.sem(n) for n in ("w_free", "gate_done", "y_done", "gate_free", "y_free", "sg_ready", "gated", "summed", "res_free"))
        block = ph.block()

        @block.sync
        def _(sp):
            with sp.Fori(0, KD // 2) as i:
                for p in range(2):
                    sp.wait_ge(w_free, i * 2 + (p + 1))
                    sp.dma_start(w_g[:, p, :, :], w_blocks[i * 2 + (gate + p)]).then_inc(w_in[p], 16)
                    sp.dma_start(w_y[:, p, :, :], w_mix[i * 2 + (mix * KD + p)]).then_inc(w_in[p], 16)
                    if not first:
                        sp.wait_ge(summed, i * 2 + (p + 1))
                        sp.dma_start(old[:, p, :, :].rearrange("p g t -> p (g t)"), merged[i * 2 + p]).then_inc(old_in[p], 16)

        @block.tensor
        def _(pe):
            pe.sem_inc(w_free, 2)
            with pe.Fori(0, KD // 2) as i:
                for p in range(2):
                    pe.wait_ge(w_in[p], i * 32 + 32)
                    for g in range(NG):
                        tok = slice(g * G, (g + 1) * G)
                        pe.wait_ge(gate_free, i * (2 * NG) + (p * NG + g + 1))
                        for k in range(KD):
                            last = pe.matmul(pg[:, g, :], w_g[:, p, k, :], c.hT[:, k, tok], start=(k == 0), stop=(k == KD - 1))
                        last.then_inc(gate_done, 1)
                        pe.wait_ge(y_free, i * (2 * NG) + (p * NG + g + 1))
                        for k in range(KC):
                            last = pe.matmul(py[:, g, :], w_y[:, p, k, :], oT[:, k, tok], start=(k == 0), stop=(k == KC - 1))
                        last.then_inc(y_done, 1)
                    pe.wait_ge(y_done, i * (2 * NG) + (p + 1) * NG)
                    pe.sem_inc(w_free, 1)

        @block.scalar
        def _(act):
            act.sem_inc(gate_free, NG)
            with act.Fori(0, KD) as j:
                for g in range(NG):
                    act.wait_ge(gate_done, j * NG + (g + 1))
                    act.wait_ge(y_free, j * NG + (g + 1))
                    act.activation(sg[:, g, :], pg[:, g, :], ACT.Sigmoid).then_inc(sg_ready, 1)
                    act.wait_ge(sg_ready, j * NG + (g + 1))
                    act.sem_inc(gate_free, 1)

        @block.vector
        def _(dve):
            dve.sem_inc(y_free, NG)
            with dve.Fori(0, KD // 2) as i:
                for p in range(2):
                    dve.wait_ge(res_free, i * 2 + (p + 1))
                    for g in range(NG):
                        n = i * (2 * NG) + (p * NG + g + 1)
                        dve.wait_ge(sg_ready, n)
                        dve.wait_ge(y_done, n)
                        dve.tensor_tensor(res[:, p, g, :], py[:, g, :], sg[:, g, :], ALU.mult).then_inc(gated, 1)
                        dve.wait_ge(gated, n)
                        dve.sem_inc(y_free, 1)

        @block.gpsimd
        def _(pool):
            pool.sem_inc(res_free, 2)
            if not first:
                pool.sem_inc(summed, 2)
            with pool.Fori(0, KD // 2) as i:
                for p in range(2):
                    pool.wait_ge(gated, i * (2 * NG) + (p + 1) * NG)
                    if not first:
                        pool.wait_ge(old_in[p], i * 16 + 16)
                        pool.tensor_tensor(res[:, p, :, :], res[:, p, :, :], old[:, p, :, :], ALU.add).then_inc(summed, 1)
                        pool.wait_ge(summed, i * 2 + (p + 3))
                    pool.dma_start(merged[i * 2 + p], res[:, p, :, :].rearrange("p g t -> p (g t)")).then_inc(stored[p], 16)
                    pool.wait_ge(stored[p], i * 16 + 16)
                    pool.sem_inc(res_free, 1)


def forgetting_attention(nc, c, oT, w_blocks, rows_dram):
    with Phase(nc, "fox") as ph:
        w = ph.sb("w", [P, 3, KD, P])
        lost = ph.sb("lost", [P, T])
        qT, kT, v = ph.sb("qT", [P, T]), ph.sb("kT", [P, T]), ph.sb("v", [P, T])
        logits, probs = ph.sb("logits", [P, T]), ph.sb("probs", [P, 2, T])
        mx, nm = ph.sb("mx", [P, 2, NG]), ph.sb("nm", [P, 2])
        den, rden = ph.sb("den", [P, 2]), ph.sb("rden", [P, 2])
        pT = ph.sb("pT", [P, 2, GT, P])
        on = ph.sb("on", [P, 2, P])
        big = ph.ps("big", [P, NG, G])
        flat = big[:, :, :].rearrange("p g t -> p (g t)")
        turn = ph.ps("turn", [P, 2, GT, P])
        po = ph.ps("po", [P, G])
        pot = ph.ps("pot", [P, G])
        w_in, lost_in = ph.sem("w_in"), ph.sem("lost_in")
        names = ("filled", "emptied", "w_free", "scored", "biased", "nm_ready", "exped", "turned", "t_copied",
                 "pv_done", "on_ready", "o_turned", "o_stored", "v_chain", "heads_done", "t_pv", "lost_free", "waited")
        (filled, emptied, w_free, scored, biased, nm_ready, exped, turned, t_copied,
         pv_done, on_ready, o_turned, o_stored, v_chain, heads_done, t_pv, lost_free, waited) = (ph.sem(n) for n in names)
        segs = [i // GT + 1 for i in range(NT)]
        before = [sum(segs[:i]) for i in range(NT + 1)]
        ALL = before[NT]
        block = ph.block()

        @block.sync
        def _(sp):
            with sp.Fori(0, H) as h:
                sp.wait_ge(w_free, h + 1)
                for n, blk in enumerate((Q_B, K_B, V_B)):
                    sp.dma_start(w[:, n, :, :], w_blocks[h + blk]).then_inc(w_in, 16)
                sp.wait_ge(lost_free, h + 1)
                sp.dma_start(lost[:, :], rows_dram[bass.ds(h + R_FORGET, 1), :].to_broadcast([P, T])).then_inc(lost_in, 16)

        @block.tensor
        def _(pe):
            pe.sem_inc(w_free, 1)
            with pe.Fori(0, H) as h:
                pe.wait_ge(w_in, h * 48 + 48)
                pe.wait_ge(biased, h * ALL + 1)
                for n in range(2):
                    for g in range(NG):
                        if n:
                            pe.wait_ge(emptied, h * 12 + (g + 1))
                        for k in range(KD):
                            last = pe.matmul(big[:, g, :], w[:, n, k, :], c.hT[:, k, g * G:(g + 1) * G], start=(k == 0), stop=(k == KD - 1))
                        last.then_inc(filled, 1)
                for g in range(NG):
                    pe.wait_ge(emptied, h * 12 + (4 + g + 1))
                    for t in range(GT * g, GT * (g + 1)):
                        for k in range(KD):
                            last = pe.matmul(flat[:, t * P:(t + 1) * P], c.hT[:, k, t * P:(t + 1) * P], w[:, 2, k, :], start=(k == 0), stop=(k == KD - 1))
                    last.then_inc(filled, 1)
                pe.wait_ge(filled, h * 12 + 12)
                pe.sem_inc(w_free, 1)
                pe.wait_ge(emptied, h * 12 + 12)

                def score(i):
                    pe.wait_ge(biased, h * ALL + (before[i] + 1))
                    for s in range(segs[i]):
                        n = min(G, (i + 1) * P - s * G)
                        diag = s == segs[i] - 1
                        last = pe.matmul(big[:, s, 0:n], qT[:, i * P:(i + 1) * P], kT[:, s * G:s * G + n], start=True, stop=not diag)
                        if diag:
                            last = pe.matmul(big[:, s, n - P:n], c.ident[:, :], c.negtri[:, :], start=False, stop=True)
                        last.then_inc(scored, 1)

                def turn_group(i, s):
                    m = before[i] + s
                    if s == 0:
                        pe.wait_ge(exped, h * NT + (i + 1))
                    pe.wait_ge(t_copied, h * ALL + (m + 1))
                    for b in range(min(GT, i + 1 - s * GT)):
                        j = s * GT + b
                        last = pe.transpose(turn[:, m % 2, b, :], probs[:, i % 2, j * P:(j + 1) * P], c.ident[:, :])
                    last.then_inc(turned, 1)

                def weigh_group(i, s):
                    m = before[i] + s
                    pe.wait_ge(t_copied, h * ALL + (m + 3))
                    if s == 0:
                        pe.wait_ge(on_ready, h * NT + (i + 1))
                    for b in range(min(GT, i + 1 - s * GT)):
                        j = s * GT + b
                        last = pe.matmul(po[:, 0:P], pT[:, m % 2, b, :], v[:, j * P:(j + 1) * P], start=(j == 0), stop=(j == i))
                    last.then_inc(t_pv, 1)
                    if s == segs[i] - 1:
                        pe.wait_ge(t_pv, h * ALL + (m + 3))
                        pe.sem_inc(pv_done, 1)

                def turn_out(i):
                    pe.wait_ge(on_ready, h * NT + (i + 2))
                    pe.wait_ge(o_stored, h * NT + (i + 1))
                    pe.transpose(pot[:, 0:P], on[:, i % 2, :], c.ident[:, :]).then_inc(o_turned, 1)

                score(0)
                for i in range(NT):
                    if i + 1 < NT:
                        score(i + 1)
                    turn_group(i, 0)
                    for s in range(segs[i]):
                        if s + 1 < segs[i]:
                            turn_group(i, s + 1)
                        weigh_group(i, s)
                    if i:
                        turn_out(i - 1)
                turn_out(NT - 1)

        @block.scalar
        def _(act):
            act.sem_inc(t_copied, 2)
            with act.Fori(0, H) as h:
                act.wait_ge(heads_done, h + 1)
                for n, (dst, scale) in enumerate(((qT, float(P) ** -0.5), (kT, 1.0), (v, 1.0))):
                    for g in range(NG):
                        act.wait_ge(filled, h * 12 + (n * NG + g + 1))
                        act.activation(dst[:, g * G:(g + 1) * G], big[:, g, :], ACT.Copy, scale=scale).then_inc(emptied, 1)

                def soften(i):
                    act.wait_ge(nm_ready, h * NT + (i + 1))
                    if i >= 2:
                        act.wait_ge(turned, h * ALL + before[i - 1])
                    n = (i + 1) * P
                    act.activation(probs[:, i % 2, 0:n], logits[:, 0:n], ACT.Exp, bias=nm[:, i % 2:i % 2 + 1],
                                   accum_out=den[:, i % 2:i % 2 + 1]).then_inc(exped, 1)

                soften(0)
                for i in range(NT):
                    for s in range(segs[i]):
                        m = before[i] + s
                        act.wait_ge(turned, h * ALL + (m + 1))
                        act.wait_ge(t_pv, h * ALL + (m + 1))
                        b = min(GT, i + 1 - s * GT)
                        act.activation(pT[:, m % 2, 0:b, :], turn[:, m % 2, 0:b, :], ACT.Copy).then_inc(t_copied, 1)
                        if s == 0 and i + 1 < NT:
                            soften(i + 1)

        @block.vector
        def _(dve):
            dve.sem_inc(biased, 1)
            dve.sem_inc(heads_done, 1)
            dve.sem_inc(on_ready, 1)
            dve.sem_inc(o_stored, 1)
            dve.sem_inc(lost_free, 1)
            dve.sem_inc(t_pv, 2)
            with dve.Fori(0, H) as h:
                st = Chain(dve, v_chain, NT, h)

                def bias(i):
                    if i:
                        dve.wait_ge(exped, h * NT + i)
                    for s in range(segs[i]):
                        n = min(G, (i + 1) * P - s * G)
                        dve.wait_ge(scored, h * ALL + (before[i] + s + 1))
                        dve.sem_inc(waited, 1)
                        dve.tensor_tensor_reduce(logits[:, s * G:s * G + n], big[:, s, 0:n], lost[:, s * G:s * G + n], 1.0, -3e38,
                                                 ALU.subtract, ALU.max, mx[:, i % 2, s:s + 1]).then_inc(biased, 1)
                    dve.wait_ge(biased, h * ALL + (before[i + 1] + 1))
                    dve.tensor_reduce(nm[:, i % 2:i % 2 + 1], mx[:, i % 2, 0:segs[i]], AX.X, ALU.max, negate=True).then_inc(nm_ready, 1)

                def finish(i):
                    dve.wait_ge(exped, h * NT + (i + 1))
                    st.did(dve.reciprocal(rden[:, i % 2:i % 2 + 1], den[:, i % 2:i % 2 + 1]))
                    st.wait()
                    dve.wait_ge(pv_done, h * NT + (i + 1))
                    if i >= 2:
                        dve.wait_ge(o_turned, h * NT + (i - 1))
                    dve.tensor_scalar(on[:, i % 2, :], po[:, 0:P], rden[:, i % 2:i % 2 + 1], None, ALU.mult).then_inc(on_ready, 1)

                def store(i):
                    dve.wait_ge(o_turned, h * NT + (i + 1))
                    dve.tensor_copy(oT[:, bass.ds(h, 1), i * P:(i + 1) * P].rearrange("p a t -> p (a t)"), pot[:, 0:P]).then_inc(o_stored, 1)

                dve.wait_ge(lost_in, h * 16 + 16)
                bias(0)
                for i in range(NT):
                    if i + 1 < NT:
                        bias(i + 1)
                    if i:
                        store(i - 1)
                    finish(i)
                store(NT - 1)
                st.end()
                dve.wait_ge(biased, h * ALL + (ALL + 1))
                dve.sem_inc(lost_free, 1)
                dve.sem_inc(heads_done, 1)


def short_conv(nc, c, w_blocks, short_w, base, n, kept, conv, norm):
    PAD = W_SHORT - 1
    assert n % 2 == 0
    with Phase(nc, f"short{base}") as ph:
        w = ph.sb("w", [P, 2, KD, P])
        taps = ph.sb("taps", [P, 12, W_SHORT])
        z = ph.sb("z", [P, 2, PAD + T])
        acc, act_out = ph.sb("acc", [P, T]), ph.sb("act_out", [P, 2, T])
        sq, sd = ph.sb("sq", [P, T]), ph.sb("sd", [P, NG, G])
        pp, pn = ph.ps("pp", [P, NG, G]), ph.ps("pn", [P, NG, G])
        w_in, stored = ph.sems("w_in", 2), ph.sems("stored", 2)
        names = ("taps_in", "w_free", "projected", "copied", "conv_done", "dve_done", "silu_done", "squared", "lengths_done",
                 "sd_ready", "sd_free", "done", "z_free", "out_free", "lengths_free", "pad_ready")
        (taps_in, w_free, projected, copied, conv_done, dve_done, silu_done, squared, lengths_done,
         sd_ready, sd_free, done, z_free, out_free, lengths_free, pad_ready) = (ph.sem(x) for x in names)
        block = ph.block()

        @block.sync
        def _(sp):
            sp.dma_start(taps[:, :, :], short_w).then_inc(taps_in, 16)
            with sp.Fori(0, n // 2) as i:
                for p in range(2):
                    sp.wait_ge(w_free, i * 2 + (p + 1))
                    sp.dma_start(w[:, p, :, :], w_blocks[i * 2 + (base + p)]).then_inc(w_in[p], 16)

        @block.gpsimd
        def _(pool):
            pool.sem_inc(out_free, 2)
            with pool.Fori(0, n // 2) as i:
                for p in range(2):
                    pool.wait_ge(done, i * 2 + (p + 1))
                    pool.dma_start(kept[i * 2 + (base + p)], act_out[:, p, :]).then_inc(stored[p], 16)
                    pool.wait_ge(stored[p], i * 16 + 16)
                    pool.sem_inc(out_free, 1)

        @block.tensor
        def _(pe):
            pe.sem_inc(w_free, 2)

            def project_block(j, p, i):
                pe.wait_ge(w_in[p], i * 16 + 16)
                for g in range(NG):
                    pe.wait_ge(copied, j * NG + (g + 1))
                    for k in range(KD):
                        last = pe.matmul(pp[:, g, :], w[:, p, k, :], c.hT[:, k, g * G:(g + 1) * G], start=(k == 0), stop=(k == KD - 1))
                    last.then_inc(projected, 1)
                pe.wait_ge(projected, j * NG + NG)
                pe.sem_inc(w_free, 1)

            def lengths(j):
                pe.wait_ge(squared, j + 1)
                pe.wait_ge(lengths_free, j + 1)
                for g in range(NG):
                    last = pe.matmul(pn[:, g, :], c.ones[:, :], sq[:, g * G:(g + 1) * G], start=True, stop=True)
                last.then_inc(lengths_done, 1)

            if not norm:
                with pe.Fori(0, n // 2) as i:
                    for p in range(2):
                        project_block(i * 2 + p, p, i)
            else:
                project_block(0, 0, 0)
                with pe.Fori(0, n // 2 - 1) as i:
                    project_block(i * 2 + 1, 1, i)
                    lengths(i * 2)
                    project_block(i * 2 + 2, 0, i + 1)
                    lengths(i * 2 + 1)
                project_block(n - 1, 1, n // 2 - 1)
                lengths(n - 2)
                lengths(n - 1)

        @block.scalar
        def _(act):
            act.sem_inc(copied, NG)
            act.sem_inc(lengths_free, 1)

            def copy(j, p):
                act.wait_ge(z_free, j + 1)
                for g in range(NG):
                    act.wait_ge(projected, j * NG + (g + 1))
                    act.activation(z[:, p, PAD + g * G:PAD + (g + 1) * G], pp[:, g, :], ACT.Copy).then_inc(copied, 1)

            def silu(j, p):
                act.wait_ge(conv_done, j + 1)
                act.wait_ge(out_free, j + 1)
                act.activation(act_out[:, p, :], acc[:, :] if conv else z[:, p, PAD:], ACT.Silu).then_inc(silu_done, 1)
                if norm:
                    act.wait_ge(silu_done, j + 1)
                    act.wait_ge(lengths_free, j + 1)
                    act.activation(sq[:, :], act_out[:, p, :], ACT.Square).then_inc(squared, 1)
                    act.wait_ge(lengths_done, j + 1)
                    act.wait_ge(sd_free, j + 1)
                    act.activation(sd[:, :, :], pn[:, :, :], ACT.Sqrt, bias=c.eps[:, 0:1]).then_inc(sd_ready, 1)
                    act.wait_ge(sd_ready, j + 1)
                    act.sem_inc(lengths_free, 1)

            copy(0, 0)
            with act.Fori(0, n // 2 - 1) as i:
                copy(i * 2 + 1, 1)
                silu(i * 2, 0)
                copy(i * 2 + 2, 0)
                silu(i * 2 + 1, 1)
            copy(n - 1, 1)
            silu(n - 2, 0)
            silu(n - 1, 1)

        @block.vector
        def _(dve):
            dve.sem_inc(z_free, 2)
            dve.sem_inc(sd_free, 1)
            PER = (W_SHORT if conv else 0) + (2 if norm else 0)
            dve.memset(z[:, :, 0:PAD], 0.0).then_inc(pad_ready, 1)
            dve.wait_ge(pad_ready, 1)
            dve.wait_ge(taps_in, 16)

            with dve.Fori(0, n // 2) as i:
                for p in range(2):
                    j = i * 2 + p
                    st = Chain(dve, dve_done, PER, j)
                    dve.wait_ge(copied, j * NG + 2 * NG)
                    if conv:
                        for k in range(W_SHORT):
                            tap, src = taps[:, bass.ds(j + base, 1), k:k + 1].rearrange("p a b -> p (a b)"), z[:, p, k:k + T]
                            if k == 0:
                                st.did(dve.tensor_scalar(acc[:, :], src, tap, None, ALU.mult))
                            else:
                                st.did(dve.scalar_tensor_tensor(out=acc[:, :], in0=src, scalar=tap, in1=acc[:, :], op0=ALU.mult, op1=ALU.add))
                            st.wait()
                        dve.sem_inc(z_free, 1)
                    dve.sem_inc(conv_done, 1)
                    if norm:
                        dve.wait_ge(sd_ready, j + 1)
                        st.did(dve.reciprocal(sd[:, :, :], sd[:, :, :]))
                        st.wait()
                        out = act_out[:, p, :]
                        st.did(dve.tensor_tensor(out, out, sd[:, :, :].rearrange("p g t -> p (g t)"), ALU.mult))
                        st.wait()
                        dve.sem_inc(sd_free, 1)
                    else:
                        dve.wait_ge(silu_done, j + 1)
                        if not conv:
                            dve.sem_inc(z_free, 1)
                    dve.sem_inc(done, 1)
                    st.end()


def delta_rule(nc, c, oT, kept, rows_dram, dn_norm):
    SCALE = float(P) ** -0.5
    ND = LEVELS - 1
    XY = 2 * LEVELS - 1
    with Phase(nc, "delta") as ph:
        four = [P, H, P]
        qkvz = ph.sb("qkvz", [P, 2, 4, H, P])
        g_row, b_row = ph.sb("g_row", [P, 2, H, P]), ph.sb("b_row", [P, 2, H, P])
        small, smallx = ph.sb("small", [P, 2, 3 * H]), ph.sb("smallx", [P, 2, 3 * H])
        beta, nbeg, qscale = ph.sb("beta", [P, 2, H]), ph.sb("nbeg", [P, 2, H]), ph.sb("qscale", [P, 2, H])
        dif, E, Em, W, W1, nAT, X, M, R, Rt, v_new, S, Sdec, oq, o, osq, on = (
            ph.sb(n, four) for n in ("dif", "E", "Em", "W", "W1", "nAT", "X", "M", "R", "Rt", "v_new", "S", "Sdec", "oq", "o", "osq", "on"))
        PT, Kd, Vb, Y = (ph.sb(n, [P, 2, H, P]) for n in ("PT", "Kd", "Vb", "Y"))
        ssq, sd, rs = (ph.sb(n, [P, H]) for n in ("ssq", "sd", "rs"))
        dn = ph.sb("dn", [P, 1])
        p0, p1, p2, p3, q0, q1, q2, q3 = (ph.ps(f"bank{n}", four) for n in range(8))
        ins, dn_in = ph.sems("ins", 2), ph.sem("dn_in")
        names = ("in_free", "gram", "turned", "small_in", "dif_done", "expd", "masked", "w1_done", "init", "v_step", "nat", "kvb", "nA", "xy",
                 "m_done", "m_copied", "t_done", "S_ready", "ks", "r_half", "r", "vn", "vn_copied", "pv", "s_decayed", "oq_done",
                 "o_done", "alone", "osq_done", "ssq_done", "sd_done", "rs_done", "on_done", "o_turned", "stored", "nbeg_done")
        e = {n: ph.sem(n) for n in names}
        block = ph.block()

        def each(eng, out, lhs, rhs):
            for h in range(H):
                last = eng.matmul(out[:, h, :], lhs[:, h, :], rhs[:, h, :], start=True, stop=True)
            return last

        def turn(eng, out, src):
            for h in range(H):
                last = eng.transpose(out[:, h, :], src[:, h, :], c.ident[:, :])
            return last

        def wide(col):
            return col.unsqueeze(2).to_broadcast(four)

        @block.sync
        def _(sp):
            sp.dma_start(dn[:, :], dn_norm).then_inc(dn_in, 16)
            tokens = kept.rearrange("(a h) p t -> p a h t", h=H)
            with sp.Fori(0, NT // 2) as i:
                for p in range(2):
                    sp.wait_ge(e["in_free"], i * 2 + (p + 1))
                    here = bass.ds(i * (2 * P) + p * P, P)
                    for a in range(4):
                        sp.dma_start(qkvz[:, p, a, :, :], tokens[:, a, :, here]).then_inc(ins[p], 16)
                    for dst, row in ((g_row, R_DECAY), (b_row, R_BETA)):
                        sp.dma_start(dst[:, p, :, :], rows_dram[row:row + H, here].unsqueeze(0).to_broadcast(four)).then_inc(ins[p], 16)

        @block.tensor
        def _(pe):
            def gram(t, p):
                q, k, v = (qkvz[:, p, n, :, :] for n in range(3))
                pe.wait_ge(ins[p], (t // 2) * 96 + 96 if isinstance(t, int) else t * 48 + (96 if p == 0 else 48))
                pe.wait_ge(e["xy"], t * XY + 1)
                each(pe, p0, k, k)
                each(pe, p1, k, q).then_inc(e["gram"], 1)
                turn(pe, p2, k)
                turn(pe, p3, v).then_inc(e["turned"], 1)

            def turn_a(t):
                pe.wait_ge(e["nat"], t + 1)
                pe.wait_ge(e["kvb"], t + 1)
                turn(pe, p3, nAT).then_inc(e["nA"], 1)

            def level(t, p, l):
                pe.wait_ge(e["xy"], t * XY + (2 * l + 1))
                each(pe, p2, nAT, X).then_inc(e["m_done"], 1)
                pe.wait_ge(e["m_copied"], t * ND + l)
                if l < ND:
                    each(pe, p0, Y[:, p, :, :], M)
                each(pe, p1, M, Y[:, p, :, :]).then_inc(e["t_done"], 1)

            def read_state(t, p):
                pe.wait_ge(e["S_ready"], t + 1)
                pe.wait_ge(e["o_done"], t + 1)
                each(pe, q0, qkvz[:, p, 1, :, :], S)
                each(pe, q1, qkvz[:, p, 0, :, :], S).then_inc(e["ks"], 1)

            def new_values(t, p):
                pe.wait_ge(e["r"], t + 1)
                pe.wait_ge(e["xy"], t * XY + (XY + 1))
                pe.wait_ge(e["stored"], t + 1)
                each(pe, q2, Y[:, p, :, :], R).then_inc(e["vn"], 1)

            def use_values(t, p):
                pe.wait_ge(e["vn_copied"], t + 1)
                each(pe, q3, PT[:, p, :, :], v_new)
                each(pe, q0, Kd[:, p, :, :], v_new).then_inc(e["pv"], 1)

            def turn_o(t):
                pe.wait_ge(e["on_done"], t + 1)
                turn(pe, q2, on).then_inc(e["o_turned"], 1)

            def before(t, p):
                gram(t, p)
                turn_a(t)
                for l in range(1, LEVELS):
                    level(t, p, l)

            def both(t, p):
                read_state(t, p)
                gram(t + 1, 1 - p)
                new_values(t, p)
                turn_a(t + 1)
                use_values(t, p)
                for l in range(1, LEVELS):
                    level(t + 1, 1 - p, l)
                    if l == 3:
                        turn_o(t)

            def within(t, p):
                read_state(t, p)
                new_values(t, p)
                use_values(t, p)
                turn_o(t)

            rounds(pe, NT, lambda: before(0, 0), both, lambda: within(NT - 1, 1))

        @block.scalar
        def _(act):
            def decay(t, p):
                act.wait_ge(e["dif_done"], t + 1)
                act.wait_ge(e["masked"], t + 1)
                act.activation(E[:, :, :], dif[:, :, :], ACT.Exp)
                act.wait_ge(e["in_free"], t + 1)
                act.activation(smallx[:, p, :], small[:, p, :], ACT.Exp).then_inc(e["expd"], 1)

            def copy_m(t, l):
                act.wait_ge(e["m_done"], t * ND + l)
                act.activation(M[:, :, :], p2[:, :, :], ACT.Copy).then_inc(e["m_copied"], 1)

            def copy_values(t):
                act.wait_ge(e["vn"], t + 1)
                act.wait_ge(e["S_ready"], t + 1)
                act.activation(v_new[:, :, :], q2[:, :, :], ACT.Copy).then_inc(e["vn_copied"], 1)

            def deviation(t):
                act.wait_ge(e["ssq_done"], t + 1)
                act.wait_ge(e["rs_done"], t + 1)
                act.activation(sd[:, :], ssq[:, :], ACT.Sqrt, scale=1.0 / P, bias=c.eps[:, 0:1]).then_inc(e["sd_done"], 1)

            def before(t, p):
                decay(t, p)
                for l in range(1, LEVELS):
                    copy_m(t, l)

            def both(t, p):
                decay(t + 1, 1 - p)
                copy_values(t)
                for l in range(1, LEVELS):
                    copy_m(t + 1, l)
                    if l == 1:
                        deviation(t)

            def within(t, p):
                copy_values(t)
                deviation(t)

            rounds(act, NT, lambda: before(0, 0), both, lambda: within(NT - 1, 1))

        @block.gpsimd
        def _(pool):
            pool.sem_inc(e["masked"], 1)
            pool.sem_inc(e["s_decayed"], 1)

            def masks(t, p):
                pool.wait_ge(e["expd"], t + 1)
                pool.wait_ge(e["v_step"], t + 1)
                pool.tensor_tensor(Em[:, :, :], E[:, :, :], c.uppereq[:, :].unsqueeze(1).to_broadcast(four), ALU.mult)
                pool.tensor_tensor(W1[:, :, :], E[:, :, :], b_row[:, p, :, :], ALU.mult).then_inc(e["w1_done"], 1)
                pool.wait_ge(e["w1_done"], t + 1)
                pool.tensor_tensor(W[:, :, :], W1[:, :, :], c.upper[:, :].unsqueeze(1).to_broadcast(four), ALU.mult).then_inc(e["masked"], 1)

            def identities(t, p):
                pool.wait_ge(e["xy"], t * XY + 1)
                pool.wait_ge(e["in_free"], t + 1)
                pool.sem_inc(e["alone"], 1)
                eye = c.ident[:, :].unsqueeze(1).to_broadcast(four)
                pool.tensor_copy(X[:, :, :], eye)
                pool.tensor_copy(Y[:, p, :, :], eye).then_inc(e["init"], 1)

            def decay_state(t, p):
                pool.wait_ge(e["expd"], t + 1)
                pool.wait_ge(e["S_ready"], t + 1)
                pool.tensor_tensor(Sdec[:, :, :], S[:, :, :], wide(smallx[:, p, 2 * H:]), ALU.mult).then_inc(e["s_decayed"], 1)

            def square(t):
                pool.wait_ge(e["o_done"], t + 2)
                pool.wait_ge(e["rs_done"], t + 1)
                pool.tensor_tensor(osq[:, :, :], o[:, :, :], o[:, :, :], ALU.mult).then_inc(e["osq_done"], 1)

            def before(t, p):
                identities(t, p)
                masks(t, p)

            def both(t, p):
                decay_state(t, p)
                identities(t + 1, 1 - p)
                masks(t + 1, 1 - p)
                square(t)

            def within(t, p):
                decay_state(t, p)
                square(t)

            rounds(pool, NT, lambda: before(0, 0), both, lambda: within(NT - 1, 1))

        @block.vector
        def _(dve):
            dve.sem_inc(e["in_free"], 2)
            dve.sem_inc(e["xy"], 1)
            dve.sem_inc(e["o_done"], 1)
            dve.sem_inc(e["stored"], 1)
            dve.sem_inc(e["rs_done"], 1)
            dve.sem_inc(e["v_step"], 1)
            dve.memset(S[:, :, :], 0.0).then_inc(e["S_ready"], 1)
            dve.wait_ge(dn_in, 16)

            def differences(t, p):
                dve.wait_ge(ins[p], (t // 2) * 96 + 96 if isinstance(t, int) else t * 48 + (96 if p == 0 else 48))
                dve.wait_ge(e["masked"], t + 1)
                here = c.cols[:, bass.ds(t, 1), :].rearrange("p a r -> p (a r)") if not isinstance(t, int) else c.cols[:, t, :]
                dve.tensor_copy(beta[:, p, :], here[:, R_BETA:R_BETA + H])
                dve.tensor_copy(small[:, p, 0:H], here[:, R_DECAY:R_DECAY + H]).then_inc(e["small_in"], 1)
                dve.tensor_copy(small[:, p, 2 * H:], g_row[:, p, :, P - 1])
                dve.wait_ge(e["small_in"], t * 2 + 1)
                dve.tensor_tensor(small[:, p, H:2 * H], g_row[:, p, :, P - 1], small[:, p, 0:H], ALU.subtract).then_inc(e["small_in"], 1)
                for h in range(H):
                    last = dve.tensor_scalar(dif[:, h, :], g_row[:, p, h, :], small[:, p, h:h + 1], 0.0, ALU.subtract, ALU.min)
                last.then_inc(e["dif_done"], 1)

            def attention_parts(t, p):
                dve.wait_ge(e["expd"], t + 1)
                dve.wait_ge(e["gram"], t + 1)
                dve.wait_ge(e["masked"], t + 2)
                dve.scalar_tensor_tensor(out=PT[:, p, :, :], in0=p1[:, :, :], scalar=SCALE, in1=Em[:, :, :], op0=ALU.mult, op1=ALU.mult)
                dve.scalar_tensor_tensor(out=nAT[:, :, :], in0=p0[:, :, :], scalar=-1.0, in1=W[:, :, :], op0=ALU.mult, op1=ALU.mult).then_inc(e["nat"], 1)
                dve.wait_ge(e["nat"], t + 1)
                dve.sem_inc(e["v_step"], 1)

            def key_value_parts(t, p):
                dve.wait_ge(e["turned"], t + 1)
                dve.scalar_tensor_tensor(out=nbeg[:, p, :], in0=beta[:, p, :], scalar=-1.0, in1=smallx[:, p, 0:H], op0=ALU.mult, op1=ALU.mult)
                dve.tensor_scalar(qscale[:, p, :], smallx[:, p, 0:H], SCALE, None, ALU.mult)
                dve.tensor_tensor(Kd[:, p, :, :], p2[:, :, :], wide(smallx[:, p, H:2 * H]), ALU.mult)
                dve.tensor_tensor(Vb[:, p, :, :], p3[:, :, :], wide(beta[:, p, :]), ALU.mult).then_inc(e["kvb"], 1)

            def first_level(t, p):
                dve.wait_ge(e["nA"], t + 1)
                dve.wait_ge(e["init"], t + 1)
                dve.sem_inc(e["alone"], 1)
                mask = lambda m, l: m[:, l, :].bitcast(U32).unsqueeze(1).to_broadcast(four)
                dve.copy_predicated(X[:, :, :], mask(c.below, 0), p3[:, :, :]).then_inc(e["xy"], 1)
                dve.copy_predicated(Y[:, p, :, :], mask(c.above, 0), nAT[:, :, :]).then_inc(e["xy"], 1)

            def level(t, p, l):
                mask = lambda m, l: m[:, l, :].bitcast(U32).unsqueeze(1).to_broadcast(four)
                dve.wait_ge(e["t_done"], t * ND + l)
                dve.wait_ge(e["xy"], t * XY + (2 * l + 1))
                dve.sem_inc(e["alone"], 1)
                if l < ND:
                    dve.copy_predicated(X[:, :, :], mask(c.below, l), p0[:, :, :]).then_inc(e["xy"], 1)
                dve.copy_predicated(Y[:, p, :, :], mask(c.above, l), p1[:, :, :]).then_inc(e["xy"], 1)

            def residual(t, p):
                dve.wait_ge(e["ks"], t + 1)
                dve.wait_ge(e["kvb"], t + 1)
                dve.tensor_tensor(Rt[:, :, :], q0[:, :, :], wide(nbeg[:, p, :]), ALU.mult).then_inc(e["r_half"], 1)
                dve.wait_ge(e["r_half"], t + 1)
                dve.tensor_tensor(R[:, :, :], Rt[:, :, :], Vb[:, p, :, :], ALU.add).then_inc(e["r"], 1)

            def next_state(t):
                dve.wait_ge(e["pv"], t + 1)
                dve.wait_ge(e["s_decayed"], t + 2)
                dve.tensor_tensor(S[:, :, :], q0[:, :, :], Sdec[:, :, :], ALU.add).then_inc(e["S_ready"], 1)

            def output(t, p):
                dve.tensor_tensor(oq[:, :, :], q1[:, :, :], wide(qscale[:, p, :]), ALU.mult).then_inc(e["oq_done"], 1)
                dve.wait_ge(e["oq_done"], t + 1)
                dve.tensor_tensor(o[:, :, :], q3[:, :, :], oq[:, :, :], ALU.add).then_inc(e["o_done"], 1)

            def squares(t):
                dve.wait_ge(e["osq_done"], t + 1)
                dve.tensor_reduce(ssq[:, :], osq[:, :, :], AX.X, ALU.add).then_inc(e["ssq_done"], 1)

            def normalise(t):
                dve.wait_ge(e["sd_done"], t + 1)
                dve.reciprocal(rs[:, :], sd[:, :]).then_inc(e["rs_done"], 1)
                dve.wait_ge(e["rs_done"], t + 2)
                dve.tensor_tensor(on[:, :, :], o[:, :, :], wide(rs[:, :]), ALU.mult).then_inc(e["on_done"], 1)

            def store(t, p):
                dve.wait_ge(e["o_turned"], t + 1)
                here = slice(t * P, (t + 1) * P) if isinstance(t, int) else bass.ds(t * P, P)
                dve.scalar_tensor_tensor(out=oT[:, :, here], in0=q2[:, :, :], scalar=dn[:, 0:1], in1=qkvz[:, p, 3, :, :],
                                         op0=ALU.mult, op1=ALU.mult).then_inc(e["stored"], 1)
                dve.wait_ge(e["stored"], t + 2)
                dve.sem_inc(e["in_free"], 1)

            def before(t, p):
                differences(t, p)
                attention_parts(t, p)
                key_value_parts(t, p)
                first_level(t, p)
                for l in range(1, LEVELS):
                    level(t, p, l)

            def both(t, p):
                differences(t + 1, 1 - p)
                residual(t, p)
                attention_parts(t + 1, 1 - p)
                key_value_parts(t + 1, 1 - p)
                next_state(t)
                first_level(t + 1, 1 - p)
                output(t, p)
                between = {1: lambda: squares(t), 2: lambda: normalise(t), 3: lambda: store(t, p)}
                for l in range(1, LEVELS):
                    level(t + 1, 1 - p, l)
                    if l in between:
                        between[l]()

            def within(t, p):
                residual(t, p)
                next_state(t)
                output(t, p)
                squares(t)
                normalise(t)
                store(t, p)

            rounds(dve, NT, lambda: before(0, 0), both, lambda: within(NT - 1, 1))


def output_and_router(nc, c, merged, x, w_out, nf_row, w_router, b_router, x2_dram, h2_dram):
    NR = N_GRP + N_EXP
    with Phase(nc, "out") as ph:
        wo, wr = ph.sb("wo", [P, KD, D]), ph.sb("wr", [P, KD, NR])
        nf, br = ph.sb("nf", [P, D]), ph.sb("br", [P, NR])
        mT, xt = ph.sb("mT", [P, 2, KD, P]), ph.sb("xt", [P, 2, D])
        x2, h2, junk = ph.sb("x2", [P, 2, D]), ph.sb("h2", [P, 2, D]), ph.sb("junk", [P, D])
        h2T = ph.sb("h2T", [P, 2, KD, P])
        ss, sd, rs = ph.sb("ss", [P, 2]), ph.sb("sd", [P, 2]), ph.sb("rs", [P, 2])
        px = ph.ps("px", [P, 2, D])
        pt = ph.ps("pt", [P, D])
        pr = ph.ps("pr", [P, 2, G])
        const_in, w_in, ins = ph.sem("const_in"), ph.sem("w_in"), ph.sems("ins", 2)
        x2_out, h2_out = ph.sems("x2_out", 2), ph.sems("h2_out", 2)
        names = ("in_free", "mT_free", "product", "x2_ready", "squared", "sd_done", "rs_done", "h2_ready", "turned", "copied", "routed", "logits", "x2_free", "h2_free")
        e = {n: ph.sem(n) for n in names}
        block = ph.block()

        @block.sync
        def _(sp):
            sp.dma_start(wo[:, :, :], w_out).then_inc(w_in, 16)
            with sp.Fori(0, NT // 2) as i:
                for p in range(2):
                    sp.wait_ge(e["mT_free"], i * 2 + (p + 1))
                    sp.wait_ge(e["in_free"], i * 2 + (p + 1))
                    sp.dma_start(mT[:, p, :, :], merged.rearrange("k p t -> p k t")[:, :, bass.ds(i * (2 * P) + p * P, P)]).then_inc(ins[p], 16)
                    sp.dma_start(xt[:, p, :], x[i * 2 + p]).then_inc(ins[p], 16)

        @block.tensor
        def _(pe):
            pe.sem_inc(e["mT_free"], 2)
            pe.wait_ge(w_in, 16)
            pe.wait_ge(const_in, 48)

            def product(t, p):
                pe.wait_ge(ins[p], 32 + (t // 2) * 32 if isinstance(t, int) else t * 16 + (32 if p == 0 else 16))
                pe.wait_ge(e["in_free"], t + 1)
                for half in range(2):
                    for k in range(KD):
                        last = pe.matmul(px[:, p, half * G:(half + 1) * G], mT[:, p, k, :], wo[:, k, half * G:(half + 1) * G],
                                         start=(k == 0), stop=(k == KD - 1))
                last.then_inc(e["product"], 1)
                pe.wait_ge(e["product"], t + 1)
                pe.sem_inc(e["mT_free"], 1)

            def route(t, p):
                pe.wait_ge(e["h2_ready"], t + 1)
                pe.wait_ge(e["copied"], t + 1)
                for k in range(KD):
                    last = pe.transpose(pt[:, k * P:(k + 1) * P], h2[:, p, k * P:(k + 1) * P], c.ident[:, :])
                last.then_inc(e["turned"], 1)
                pe.wait_ge(e["copied"], t + 2)
                pe.wait_ge(e["logits"], t + 1)
                for k in range(KD):
                    last = pe.matmul(pr[:, p, 0:NR], h2T[:, p, k, :], wr[:, k, :], start=(k == 0), stop=(k == KD - 1))
                last.then_inc(e["routed"], 1)

            def both(t, p):
                product(t + 1, 1 - p)
                route(t, p)

            rounds(pe, NT, lambda: product(0, 0), both, lambda: route(NT - 1, 1))

        @block.scalar
        def _(act):
            act.sem_inc(e["copied"], 1)
            with act.Fori(0, NT // 2) as i:
                for p in range(2):
                    n = i * 2 + (p + 1)
                    act.wait_ge(e["x2_ready"], n)
                    act.wait_ge(e["rs_done"], n)
                    act.wait_ge(e["sd_done"], n)
                    act.activation(junk[:, :], x2[:, p, :], ACT.Square, accum_out=ss[:, p:p + 1]).then_inc(e["squared"], 1)
                    act.wait_ge(e["squared"], n)
                    act.activation(sd[:, p:p + 1], ss[:, p:p + 1], ACT.Sqrt, scale=1.0 / D, bias=c.eps[:, 0:1]).then_inc(e["sd_done"], 1)
                    act.wait_ge(e["turned"], n)
                    act.wait_ge(e["logits"], n)
                    act.activation(h2T[:, p, :, :].rearrange("p k t -> p (k t)"), pt[:, :], ACT.Copy).then_inc(e["copied"], 1)

        @block.vector
        def _(dve):
            for n in ("in_free", "rs_done"):
                dve.sem_inc(e[n], 2)
            dve.sem_inc(e["sd_done"], 1)
            dve.sem_inc(e["logits"], 1)
            dve.wait_ge(const_in, 48)

            def add(t, p):
                dve.wait_ge(e["product"], t + 1)
                dve.wait_ge(ins[p], 32 + (t // 2) * 32 if isinstance(t, int) else t * 16 + (32 if p == 0 else 16))
                dve.wait_ge(e["x2_free"], t + 1)
                dve.tensor_tensor(x2[:, p, :], px[:, p, :], xt[:, p, :], ALU.add).then_inc(e["x2_ready"], 1)
                dve.wait_ge(e["x2_ready"], t + 1)
                dve.sem_inc(e["in_free"], 1)

            def scale(t, p):
                dve.wait_ge(e["sd_done"], t + 2)
                dve.reciprocal(rs[:, p:p + 1], sd[:, p:p + 1]).then_inc(e["rs_done"], 1)
                dve.wait_ge(e["rs_done"], t + 3)
                dve.wait_ge(e["h2_free"], t + 1)
                dve.scalar_tensor_tensor(out=h2[:, p, :], in0=x2[:, p, :], scalar=rs[:, p:p + 1], in1=nf[:, :], op0=ALU.mult,
                                         op1=ALU.mult).then_inc(e["h2_ready"], 1)

            def keep(t, p):
                dve.wait_ge(e["routed"], t + 1)
                out = tile_of(c.logits, t)
                out = out if isinstance(t, int) else out.rearrange("p a n -> p (a n)")
                dve.tensor_tensor(out, pr[:, p, 0:NR], br[:, :], ALU.add).then_inc(e["logits"], 1)

            def first():
                add(0, 0)
                scale(0, 0)

            def both(t, p):
                add(t + 1, 1 - p)
                keep(t, p)
                scale(t + 1, 1 - p)

            rounds(dve, NT, first, both, lambda: keep(NT - 1, 1))

        @block.gpsimd
        def _(pool):
            pool.sem_inc(e["x2_free"], 2)
            pool.sem_inc(e["h2_free"], 2)
            pool.dma_start(nf[:, :], nf_row.to_broadcast([P, D])).then_inc(const_in, 16)
            pool.dma_start(br[:, :], b_router.to_broadcast([P, NR])).then_inc(const_in, 16)
            pool.dma_start(wr[:, :, :], w_router).then_inc(const_in, 16)
            with pool.Fori(0, NT // 2) as i:
                for p in range(2):
                    pool.wait_ge(e["h2_ready"], i * 2 + (p + 1))
                    pool.dma_start(x2_dram[i * 2 + p], x2[:, p, :]).then_inc(x2_out[p], 16)
                    pool.dma_start(h2_dram[i * 2 + p], h2[:, p, :]).then_inc(h2_out[p], 16)
                    pool.wait_ge(x2_out[p], i * 16 + 16)
                    pool.wait_ge(h2_out[p], i * 16 + 16)
                    pool.wait_ge(e["turned"], i * 2 + (p + 1))
                    pool.sem_inc(e["x2_free"], 1)
                    pool.sem_inc(e["h2_free"], 1)


def dispatch(nc, c, table):
    NR = N_GRP + N_EXP
    with Phase(nc, "route") as ph:
        f = lambda n, *sh: ph.sb(n, [P, *sh])
        gmax, gsum, pg, m1, m2, low, tx, den = (f(n, NT) for n in ("gmax", "gsum", "pg", "m1", "m2", "low", "tx", "den"))
        eg, geq, gv, goh, pen = (f(n, NT, N_GRP) for n in ("eg", "geq", "gv", "goh", "pen"))
        em, em2, eq, val, oh1, oh2, both, rank, weighed = (
            f(n, NT, N_EXP) for n in ("em", "em2", "eq", "val", "oh1", "oh2", "both", "rank", "weighed"))
        base = f("base", NT + 1, N_EXP)
        padded, pend, pstart, ones = (f(n, N_EXP) for n in ("padded", "pend", "pstart", "ones"))
        count_i, pend_i = ph.sb("count_i", [P, N_EXP], I32), ph.sb("pend_i", [P, N_EXP], I32)
        ends, blocks_f = ph.sb("ends", [1, N_EXP]), ph.sb("blocks_f", [1, N_EXP])
        iota_g, iota_e, destf = f("iota_g", N_GRP), f("iota_e", N_EXP), f("destf", NT, 2)
        lo, hi, pos = (ph.sb(n, [P, NT, 2], I32) for n in ("lo", "hi", "pos"))
        tokens, zero = ph.sb("tokens", [P, NT], I32), ph.sb("zero", [P, NB], I32)
        starts, over, owner = ph.sb("starts", [1, NB]), ph.sb("over", [1, NB, N_EXP]), ph.sb("owner", [1, NB])
        within, total = ph.ps("within", [P, NT, N_EXP]), ph.ps("total", [P, NT, N_EXP])
        step, act_done, iotas, zeroed, zero_in, ranked, placed, scattered, counted, loaded = (
            ph.sem(n) for n in ("step", "act_done", "iotas", "zeroed", "zero_in", "ranked", "placed", "scattered", "counted", "loaded"))
        block = ph.block()

        @block.gpsimd
        def _(pool):
            pool.memset(zero[:, :], 0).then_inc(zeroed, 1)
            for out, pat, mult in ((iota_g, [[1, N_GRP]], 0), (iota_e, [[1, N_EXP]], 0), (starts, [[BLK, NB]], 0)):
                pool.iota(out[:, :], pattern=pat, base=0, channel_multiplier=mult, allow_small_or_imprecise_dtypes=True).then_inc(iotas, 1)
            pool.iota(tokens[:, :], pattern=[[P, NT]], base=0, channel_multiplier=1).then_inc(iotas, 1)
            pool.wait_ge(placed, 1)
            pool.wait_ge(zero_in, 16)
            pool.wait_ge(iotas, 4)
            for s in range(2):
                for t in range(NT):
                    pool.indirect_dma_start(out=table, out_offset=bass.IndirectOffsetOnAxis(ap=pos[:, t, s:s + 1], axis=0),
                                            in_=tokens[:, t:t + 1], in_offset=None).then_inc(scattered, 16)
            pool.wait_ge(scattered, 16 * 2 * NT)

        @block.sync
        def _(sp):
            sp.wait_ge(zeroed, 1)
            sp.dma_start(table.rearrange("(p b) a -> p (b a)", b=NB), zero[:, :]).then_inc(zero_in, 16)
            sp.wait_ge(scattered, 16 * 2 * NT)
            sp.dma_start(c.place_token[:, :], table.rearrange("(p b) a -> p (b a)", b=NB)).then_inc(loaded, 16)
            sp.wait_ge(loaded, 16)

        @block.scalar
        def _(act):
            act.wait_ge(step, 2)
            act.activation(eg[:, :, :], eg[:, :, :], ACT.Exp).then_inc(act_done, 1)
            act.wait_ge(counted, 1)
            act.activation(tx[:, :], tx[:, :], ACT.Exp).then_inc(act_done, 1)

        @block.tensor
        def _(pe):
            pe.wait_ge(ranked, 1)
            pe.matmul(within[:, :, :], c.upper[:, :], both[:, :, :], start=True, stop=True)
            pe.matmul(total[:, :, :], c.ones[:, :], both[:, :, :], start=True, stop=True).then_inc(ranked, 1)

        @block.vector
        def _(dve):
            st = Chain(dve, step)

            def do(ins):
                st.did(ins)
                st.wait()

            def wide(ap, n):
                return ap.unsqueeze(2).to_broadcast([P, NT, n])

            def over_tiles(ap, n):
                return ap.unsqueeze(1).to_broadcast([P, NT, n])

            def first_of(eq_, val_, iota, out, n):
                do(dve.scalar_tensor_tensor(out=val_[:, :, :], in0=eq_[:, :, :], scalar=-99.0, in1=over_tiles(iota[:, :], n), op0=ALU.mult, op1=ALU.add))
                do(dve.tensor_reduce(low[:, :], val_[:, :, :], AX.X, ALU.min))
                do(dve.tensor_tensor(out[:, :, :], val_[:, :, :], wide(low[:, :], n), ALU.is_equal))

            g_log, e_log = c.logits[:, :, 0:N_GRP], c.logits[:, :, N_GRP:NR]
            do(dve.tensor_reduce(gmax[:, :], g_log, AX.X, ALU.max))
            do(dve.tensor_tensor(eg[:, :, :], g_log, wide(gmax[:, :], N_GRP), ALU.subtract))
            do(dve.tensor_tensor(geq[:, :, :], g_log, wide(gmax[:, :], N_GRP), ALU.is_equal))
            dve.wait_ge(iotas, 4)
            first_of(geq, gv, iota_g, goh, N_GRP)
            do(dve.tensor_scalar(pen[:, :, :], goh[:, :, :], 1.0, BIG, ALU.subtract, ALU.mult))
            four_d = "p t (g e) -> p t g e"
            do(dve.tensor_tensor(em[:, :, :].rearrange(four_d, g=N_GRP), e_log.rearrange(four_d, g=N_GRP),
                                 pen[:, :, :].unsqueeze(3).to_broadcast([P, NT, N_GRP, PER_GRP]), ALU.add))
            do(dve.tensor_reduce(m1[:, :], em[:, :, :], AX.X, ALU.max))
            do(dve.tensor_tensor(eq[:, :, :], em[:, :, :], wide(m1[:, :], N_EXP), ALU.is_equal))
            first_of(eq, val, iota_e, oh1, N_EXP)
            do(dve.scalar_tensor_tensor(out=em2[:, :, :], in0=oh1[:, :, :], scalar=-2.0 * BIG, in1=em[:, :, :], op0=ALU.mult, op1=ALU.add))
            do(dve.tensor_reduce(m2[:, :], em2[:, :, :], AX.X, ALU.max))
            do(dve.tensor_tensor(eq[:, :, :], em2[:, :, :], wide(m2[:, :], N_EXP), ALU.is_equal))
            first_of(eq, val, iota_e, oh2, N_EXP)
            do(dve.tensor_tensor(both[:, :, :], oh1[:, :, :], oh2[:, :, :], ALU.add))
            dve.sem_inc(ranked, 1)
            do(dve.tensor_tensor(tx[:, :], m2[:, :], m1[:, :], ALU.subtract))
            dve.sem_inc(counted, 1)
            dve.wait_ge(act_done, 2)
            do(dve.tensor_reduce(gsum[:, :], eg[:, :, :], AX.X, ALU.add))
            do(dve.scalar_tensor_tensor(out=den[:, :], in0=tx[:, :], scalar=1.0, in1=gsum[:, :], op0=ALU.add, op1=ALU.mult))
            do(dve.reciprocal(c.gates[:, :, 0], den[:, :]))
            do(dve.tensor_tensor(c.gates[:, :, 1], c.gates[:, :, 0], tx[:, :], ALU.mult))
            dve.wait_ge(ranked, 2)
            do(dve.memset(base[:, 0, :], 0.0))
            for t in range(NT):
                do(dve.tensor_tensor(base[:, t + 1, :], base[:, t, :], total[:, t, :], ALU.add))
            do(dve.tensor_tensor(rank[:, :, :], within[:, :, :], base[:, 0:NT, :], ALU.add))
            do(dve.tensor_scalar(padded[:, :], base[:, NT, :], float(BLK - 1), None, ALU.add))
            do(dve.tensor_copy(count_i[:, :], padded[:, :]))
            do(dve.tensor_scalar(count_i[:, :], count_i[:, :], 7, 7, ALU.logical_shift_right, ALU.logical_shift_left))
            do(dve.tensor_copy(padded[:, :], count_i[:, :]))
            do(dve.memset(ones[:, :], 1.0))
            do(dve.tensor_tensor_scan(pend[:, :], ones[:, :], padded[:, :], 0.0, ALU.mult, ALU.add))
            do(dve.tensor_copy(pend_i[:, :], pend[:, :]))
            do(dve.tensor_tensor(pstart[:, :], pend[:, :], padded[:, :], ALU.subtract))
            do(dve.tensor_tensor(rank[:, :, :], rank[:, :, :], over_tiles(pstart[:, :], N_EXP), ALU.add))
            for s, oh in enumerate((oh1, oh2)):
                do(dve.tensor_tensor(weighed[:, :, :], oh[:, :, :], rank[:, :, :], ALU.mult))
                do(dve.tensor_reduce(destf[:, :, s], weighed[:, :, :], AX.X, ALU.add))
            do(dve.tensor_copy(c.dest[:, :, :], destf[:, :, :]))
            do(dve.tensor_scalar(lo[:, :, :], c.dest[:, :, :], BLK - 1, 6, ALU.bitwise_and, ALU.logical_shift_left))
            do(dve.tensor_scalar(hi[:, :, :], c.dest[:, :, :], 7, None, ALU.logical_shift_right))
            do(dve.tensor_tensor(pos[:, :, :], lo[:, :, :], hi[:, :, :], ALU.bitwise_or))
            dve.sem_inc(placed, 1)
            do(dve.tensor_tensor(over[:, :, :], starts[:, :].unsqueeze(2).to_broadcast([1, NB, N_EXP]),
                                 pend[0:1, :].unsqueeze(1).to_broadcast([1, NB, N_EXP]), ALU.is_ge))
            do(dve.tensor_reduce(owner[:, :], over[:, :, :], AX.X, ALU.add))
            do(dve.tensor_scalar(owner[:, :], owner[:, :], float(N_EXP - 1), None, ALU.min))
            do(dve.tensor_copy(c.block_expert[:, :], owner[:, :]))
            do(dve.tensor_scalar(count_i[0:1, :], pend_i[0:1, :], 7, None, ALU.logical_shift_right))
            do(dve.memset(ends[:, :], 2.0))
            do(dve.tensor_copy(blocks_f[:, :], count_i[0:1, :]))
            do(dve.tensor_scalar(ends[:, SLOTS:], blocks_f[:, 0:N_EXP - SLOTS], 2.0, None, ALU.add))
            do(dve.tensor_copy(c.blocks_before[:, :], ends[:, :]))
            do(dve.tensor_scalar(c.last_step[:, :], pend_i[0:1, N_EXP - 1:N_EXP], BLK, None, ALU.subtract))
            do(dve.tensor_scalar(c.last_step[:, :], c.last_step[:, :], 9, None, ALU.logical_shift_right))


def experts(nc, c, h2_rows, w13, w2, y_dram):
    KE = DE // P
    with Phase(nc, "moe") as ph:
        wa, wb = ph.sb("wa", [P, SLOTS, KD, 2 * DE]), ph.sb("wb", [P, SLOTS, KE, D])
        idx = ph.sb("idx", [P, SLOTS], I32)
        xg, xT = ph.sb("xg", [P, SLOTS, D]), ph.sb("xT", [P, 2, D])
        act1, prod, prodT = ph.sb("act1", [P, 2, DE]), ph.sb("prod", [P, 2, DE]), ph.sb("prodT", [P, 2, DE])
        y = ph.sb("y", [P, 2, D])
        tx = ph.ps("tx", [P, 2, G])
        pu = ph.ps("pu", [P, 2, G])
        tp = ph.ps("tp", [P, G])
        py = ph.ps("py", [P, 2, G])
        wa_in, wb_in, x_in, y_out = ph.sems("wa_in", SLOTS), ph.sems("wb_in", SLOTS), ph.sems("x_in", SLOTS), ph.sems("y_out", 2)
        names = ("idx_ready", "x_turned", "xa", "xv", "up", "silu", "prod", "p_turned", "p_copied", "down", "ya", "yv", "y_free", "alone")
        e = {n: ph.sem(n) for n in names}
        none, cleared, none_ready = ph.sb("none", [P, D]), ph.sem("cleared"), ph.sem("none_ready")
        block = ph.block()

        def last_step(eng):
            return eng.value_load(c.last_step[0:1, 0:1], min_val=2 * T // BLK // SLOTS - 1, max_val=NB // SLOTS - 1)

        @block.sync
        def _(sp):
            with sp.Fori(0, N_EXP // SLOTS) as i:
                for p in range(SLOTS):
                    ex = i * SLOTS + p
                    done = sp.value_load(c.blocks_before[0:1, bass.ds(ex, 1)], min_val=2, max_val=NB + 2)
                    sp.wait_ge(e["up"], done)
                    sp.dma_start(wa[:, p, :, :], w13[bass.ds(ex, 1)].rearrange("a p k n -> p (a k) n")).then_inc(wa_in[p], 16)
                    sp.wait_ge(e["down"], done)
                    sp.dma_start(wb[:, p, :, :], w2[bass.ds(ex, 1)].rearrange("a p k n -> p (a k) n")).then_inc(wb_in[p], 16)

        @block.gpsimd
        def _(pool):
            def gather(t, n):
                pool.wait_ge(e["x_turned"], t + 1)
                pool.sem_inc(e["alone"], 1)
                pool.tensor_copy(idx[:, n:n + 1], c.place_token[:, bass.ds(t, 1)]).then_inc(e["idx_ready"], 1)
                pool.wait_ge(e["idx_ready"], t + 1)
                pool.sem_inc(e["alone"], 1)
                pool.indirect_dma_start(out=xg[:, n, :], out_offset=None, in_=h2_rows,
                                        in_offset=bass.IndirectOffsetOnAxis(ap=idx[:, n:n + 1], axis=0)).then_inc(x_in[n], 16)

            last = last_step(pool)
            pool.memset(none[:, :], 0.0).then_inc(none_ready, 1)
            for n in range(SLOTS):
                gather(n, n)
            with pool.Fori(1, NB // SLOTS) as i:
                with pool.If(i < last + 1):
                    for n in range(SLOTS):
                        gather(i * SLOTS + n, n)

        @block.tensor
        def _(pe):
            pe.sem_inc(e["x_turned"], SLOTS)
            for n in ("up", "p_turned", "down"):
                pe.sem_inc(e[n], 2)
            for n in range(1, SLOTS):
                pe.sem_inc(wa_in[n], 16)
                pe.sem_inc(wb_in[n], 16)
            last = last_step(pe)

            def expert_of(t):
                here = c.block_expert[0:1, t:t + 1] if isinstance(t, int) else c.block_expert[0:1, bass.ds(t, 1)]
                return pe.value_load(here, min_val=0, max_val=N_EXP - 1)

            def slot_of(ex, arrived):
                pe.wait_ge(arrived[0], ex // SLOTS * 16 + 16)
                for n in range(1, SLOTS):
                    pe.wait_ge(arrived[n], (ex + (SLOTS - n)) // SLOTS * 16 + 16)
                return ex % SLOTS

            def turn_x(t, n):
                pe.wait_ge(x_in[n], t * (16 // SLOTS) + (16 - n * (16 // SLOTS)))
                pe.wait_ge(e["xa"], t + 1)
                pe.wait_ge(e["xv"], t + 1)
                for k in range(KD):
                    done = pe.transpose(tx[:, k // 4, k % 4 * P:(k % 4 + 1) * P], xg[:, n, k * P:(k + 1) * P], c.ident[:, :])
                done.then_inc(e["x_turned"], 1)

            def up(t, p):
                ex = expert_of(t)
                pe.wait_ge(e["xa"], t + 2)
                pe.wait_ge(e["xv"], t + 2)
                slot = slot_of(ex, wa_in)
                pe.wait_ge(e["prod"], t + 1)
                for k in range(KD):
                    last = pe.matmul(pu[:, p, :], xT[:, p, k * P:(k + 1) * P], wa[:, bass.ds(slot, 1), k, :].rearrange("p a n -> p (a n)"), start=(k == 0), stop=(k == KD - 1))
                last.then_inc(e["up"], 1)

            def turn_prod(t, p):
                pe.wait_ge(e["prod"], t + 3)
                pe.wait_ge(e["p_copied"], t + 1)
                for k in range(KE):
                    last = pe.transpose(tp[:, k * P:(k + 1) * P], prod[:, p, k * P:(k + 1) * P], c.ident[:, :])
                last.then_inc(e["p_turned"], 1)

            def down(t, p):
                ex = expert_of(t)
                pe.wait_ge(e["p_copied"], t + 2)
                slot = slot_of(ex, wb_in)
                pe.wait_ge(e["ya"], t + 1)
                pe.wait_ge(e["yv"], t + 1)
                for cols in range(2):
                    for k in range(KE):
                        last = pe.matmul(py[:, cols, :], prodT[:, p, k * P:(k + 1) * P],
                                         wb[:, bass.ds(slot, 1), k, cols * G:(cols + 1) * G].rearrange("p a n -> p (a n)"),
                                         start=(k == 0), stop=(k == KE - 1))
                last.then_inc(e["down"], 1)

            def both(t, n):
                up(t + 1, 1 - n % 2)
                turn_prod(t, n % 2)
                turn_x(t + 2, (n + 2) % SLOTS)
                down(t, n % 2)

            turn_x(0, 0)
            up(0, 0)
            turn_x(1, 1)
            with pe.Fori(1, NB // SLOTS) as i:
                with pe.If(i < last + 1):
                    for n in range(SLOTS):
                        both(i * SLOTS - (SLOTS - n), n)
            both(last * SLOTS, 0)
            both(last * SLOTS + 1, 1)
            up(last * SLOTS + 3, 1)
            turn_prod(last * SLOTS + 2, 0)
            down(last * SLOTS + 2, 0)
            turn_prod(last * SLOTS + 3, 1)
            down(last * SLOTS + 3, 1)

        @block.scalar
        def _(act):
            act.sem_inc(e["xa"], 1)
            act.sem_inc(e["p_copied"], 1)
            act.sem_inc(e["ya"], 1)
            last = last_step(act)

            def copy_x(t, p):
                act.wait_ge(e["x_turned"], t + (SLOTS + 1))
                act.wait_ge(e["up"], t + 1)
                act.activation(xT[:, p, 0:G], tx[:, 0, :], ACT.Copy).then_inc(e["xa"], 1)

            def silu(t, p):
                act.wait_ge(e["up"], t + 3)
                act.wait_ge(e["prod"], t + 1)
                act.activation(act1[:, p, :], pu[:, p, 0:DE], ACT.Silu).then_inc(e["silu"], 1)

            def copy_prod(t, p):
                act.wait_ge(e["p_turned"], t + 3)
                act.wait_ge(e["down"], t + 1)
                act.activation(prodT[:, p, :], tp[:, 0:DE], ACT.Copy).then_inc(e["p_copied"], 1)

            def copy_y(t, p):
                act.wait_ge(e["down"], t + 3)
                act.wait_ge(e["y_free"], t + 1)
                act.activation(y[:, p, 0:G], py[:, 0, :], ACT.Copy).then_inc(e["ya"], 1)
                act.wait_ge(e["ya"], t + 2)
                act.wait_ge(e["yv"], t + 2)
                act.sem_inc(e["alone"], 1)
                act.dma_start(y_dram[t], y[:, p, :]).then_inc(y_out[p], 16)

            def both(t, n):
                p = n % 2
                silu(t + 1, 1 - p)
                copy_prod(t, p)
                copy_x(t + 2, p)
                copy_y(t, p)

            act.wait_ge(none_ready, 1)
            copy_x(0, 0)
            silu(0, 0)
            copy_x(1, 1)
            with act.Fori(1, NB // SLOTS) as i:
                with act.If(i < last + 1):
                    for n in range(SLOTS):
                        both(i * SLOTS - (SLOTS - n), n)
                    act.sem_inc(cleared, 16 * SLOTS)
                with act.If(last < i):
                    for n in range(SLOTS):
                        act.dma_start(y_dram[i * SLOTS + n], none[:, :]).then_inc(cleared, 16)
            both(last * SLOTS, 0)
            both(last * SLOTS + 1, 1)
            silu(last * SLOTS + 3, 1)
            copy_prod(last * SLOTS + 2, 0)
            copy_y(last * SLOTS + 2, 0)
            copy_prod(last * SLOTS + 3, 1)
            copy_y(last * SLOTS + 3, 1)
            for p in range(2):
                act.wait_ge(y_out[p], last * (8 * SLOTS) + (8 * SLOTS + 16))
            act.wait_ge(cleared, (NB - SLOTS) * 16)
            act.sem_inc(e["alone"], 1)

        @block.vector
        def _(dve):
            dve.sem_inc(e["xv"], 1)
            dve.sem_inc(e["yv"], 1)
            dve.sem_inc(e["prod"], 2)
            for p in range(2):
                dve.sem_inc(y_out[p], 16)
            last = last_step(dve)

            def copy_x(t, p):
                dve.wait_ge(e["x_turned"], t + (SLOTS + 1))
                dve.wait_ge(e["up"], t + 1)
                dve.tensor_copy(xT[:, p, G:], tx[:, 1, :]).then_inc(e["xv"], 1)

            def multiply(t, p):
                dve.wait_ge(e["silu"], t + 1)
                dve.wait_ge(e["p_turned"], t + 1)
                dve.tensor_tensor(prod[:, p, :], pu[:, p, DE:], act1[:, p, :], ALU.mult).then_inc(e["prod"], 1)

            def copy_y(t, p):
                dve.wait_ge(e["down"], t + 3)
                dve.wait_ge(y_out[p], t * 8 + (16 if p == 0 else 8))
                dve.sem_inc(e["y_free"], 1)
                dve.tensor_copy(y[:, p, G:], py[:, 1, :]).then_inc(e["yv"], 1)

            def both(t, n):
                p = n % 2
                multiply(t + 1, 1 - p)
                copy_x(t + 2, p)
                copy_y(t, p)

            copy_x(0, 0)
            multiply(0, 0)
            copy_x(1, 1)
            with dve.Fori(1, NB // SLOTS) as i:
                with dve.If(i < last + 1):
                    for n in range(SLOTS):
                        both(i * SLOTS - (SLOTS - n), n)
            both(last * SLOTS, 0)
            both(last * SLOTS + 1, 1)
            multiply(last * SLOTS + 3, 1)
            copy_y(last * SLOTS + 2, 0)
            copy_y(last * SLOTS + 3, 1)


def combine(nc, c, x2_dram, y_rows, nl_row, out):
    with Phase(nc, "comb") as ph:
        nl = ph.sb("nl", [P, D])
        dest = ph.sb("dest", [P, 2, 2], I32)
        gate = ph.sb("gate", [P, 2, 2])
        x2, ys = ph.sb("x2", [P, 2, D]), ph.sb("ys", [P, 2, 2, D])
        one, sum_, res, junk = ph.sb("one", [P, 2, D]), ph.sb("sum", [P, 2, D]), ph.sb("res", [P, 2, D]), ph.sb("junk", [P, 2, D])
        ss, sd, rs = ph.sb("ss", [P, 2]), ph.sb("sd", [P, 2]), ph.sb("rs", [P, 2])
        nl_in, x_in, y_in, stored = ph.sem("nl_in"), ph.sems("x_in", 2), ph.sems("y_in", 2), ph.sems("stored", 2)
        names = ("free", "dest_ready", "gate_ready", "half", "summed", "squared", "sd_done", "rs_done", "ready", "alone")
        e = {n: ph.sem(n) for n in names}
        block = ph.block()

        @block.sync
        def _(sp):
            sp.dma_start(nl[:, :], nl_row.to_broadcast([P, D])).then_inc(nl_in, 16)

            def load(t, p):
                sp.wait_ge(e["free"], t + 1)
                sp.dma_start(x2[:, p, :], x2_dram[t]).then_inc(x_in[p], 16)

            def store(t, p):
                sp.wait_ge(e["ready"], t + 1)
                sp.dma_start(out[t], res[:, p, :]).then_inc(stored[p], 16)

            def both(t, p):
                load(t + 1, 1 - p)
                store(t, p)

            rounds(sp, NT, lambda: load(0, 0), both, lambda: store(NT - 1, 1))
            for p in range(2):
                sp.wait_ge(stored[p], NT * 8 + 16)

        @block.gpsimd
        def _(pool):
            with pool.Fori(0, NT // 2) as i:
                for p in range(2):
                    t = i * 2 + p
                    pool.wait_ge(e["free"], t + 1)
                    pool.sem_inc(e["alone"], 1)
                    pool.tensor_copy(dest[:, p, :], c.dest[:, bass.ds(t, 1), :].rearrange("p a s -> p (a s)")).then_inc(e["dest_ready"], 1)
                    pool.wait_ge(e["dest_ready"], t + 1)
                    pool.sem_inc(e["alone"], 1)
                    for s in range(2):
                        pool.indirect_dma_start(out=ys[:, p, s, :], out_offset=None, in_=y_rows,
                                                in_offset=bass.IndirectOffsetOnAxis(ap=dest[:, p, s:s + 1], axis=0)).then_inc(y_in[p], 16)

        @block.scalar
        def _(act):
            with act.Fori(0, NT // 2) as i:
                for p in range(2):
                    n = i * 2 + (p + 1)
                    act.wait_ge(e["summed"], n)
                    act.activation(junk[:, p, :], sum_[:, p, :], ACT.Square, accum_out=ss[:, p:p + 1]).then_inc(e["squared"], 1)
                    act.wait_ge(e["squared"], n)
                    act.activation(sd[:, p:p + 1], ss[:, p:p + 1], ACT.Sqrt, scale=1.0 / D, bias=c.eps[:, 0:1]).then_inc(e["sd_done"], 1)

        @block.vector
        def _(dve):
            dve.sem_inc(e["free"], 2)
            for p in range(2):
                dve.sem_inc(stored[p], 16)
            dve.wait_ge(nl_in, 16)

            def add(t, p, i):
                dve.wait_ge(x_in[p], i * 16 + 16)
                dve.wait_ge(y_in[p], i * 32 + 32)
                dve.tensor_copy(gate[:, p, :], tile_of(c.gates, t).rearrange("p a s -> p (a s)")).then_inc(e["gate_ready"], 1)
                dve.wait_ge(e["gate_ready"], t + 1)
                dve.scalar_tensor_tensor(out=one[:, p, :], in0=ys[:, p, 0, :], scalar=gate[:, p, 0:1], in1=x2[:, p, :], op0=ALU.mult,
                                         op1=ALU.add).then_inc(e["half"], 1)
                dve.wait_ge(e["half"], t + 1)
                dve.scalar_tensor_tensor(out=sum_[:, p, :], in0=ys[:, p, 1, :], scalar=gate[:, p, 1:2], in1=one[:, p, :], op0=ALU.mult,
                                         op1=ALU.add).then_inc(e["summed"], 1)
                dve.wait_ge(e["summed"], t + 1)
                dve.sem_inc(e["free"], 1)

            def finish(t, p, i):
                dve.wait_ge(e["sd_done"], t + 1)
                dve.reciprocal(rs[:, p:p + 1], sd[:, p:p + 1]).then_inc(e["rs_done"], 1)
                dve.wait_ge(e["rs_done"], t + 1)
                dve.wait_ge(stored[p], i * 16 + 16)
                dve.scalar_tensor_tensor(out=res[:, p, :], in0=sum_[:, p, :], scalar=rs[:, p:p + 1], in1=nl[:, :], op0=ALU.mult,
                                         op1=ALU.mult).then_inc(e["ready"], 1)

            with dve.Fori(0, NT // 2) as i:
                add(i * 2, 0, i)
                add(i * 2 + 1, 1, i)
                finish(i * 2, 0, i)
                finish(i * 2 + 1, 1, i)


class Constants:
    pass


def build(nc, a):
    rows_dram = nc.dram_tensor("gate_rows", (R_ALL, T), F32, kind="Internal").ap()
    kept = nc.dram_tensor("kept", (4 * H, P, T), F32, kind="Internal").ap()
    merged = nc.dram_tensor("merged", (KD, P, T), F32, kind="Internal").ap()
    with ExitStack() as ctx:
        c = Constants()

        def sb(name, shape, dt=F32):
            return ctx.enter_context(nc.sbuf_tensor(name, shape, dt))

        c.ident, c.ones, c.eps = sb("ident", [P, P]), sb("ones", [P, P]), sb("eps", [P, 1])
        c.negtri, c.upper, c.uppereq = sb("negtri", [P, P]), sb("upper", [P, P]), sb("uppereq", [P, P])
        c.below, c.above = sb("below", [P, LEVELS, P]), sb("above", [P, LEVELS, P])
        c.cols = sb("cols", [P, NT, R_ALL])
        constants(nc, c)
        with ExitStack() as mixing:
            c.hT = mixing.enter_context(nc.sbuf_tensor("hT", [P, KD, T], F32))
            oT = mixing.enter_context(nc.sbuf_tensor("oT", [P, KC, T], F32))
            norm_and_transpose(nc, c, a["x"].rearrange("(t p) d -> t p d", p=P), a["nm_col"])
            narrow_rows(nc, c, a["w_narrow"], a["sm_bias"], a["a_log"], rows_dram)
            conformer(nc, c, oT, a["w_blocks"], a["dw_w"], a["dw_b"], a["ln_g"], a["ln_b"])
            gated_merge(nc, c, oT, a["w_blocks"], GATE_C, a["w_mix"], 2, merged, True)
            forgetting_attention(nc, c, oT, a["w_blocks"], rows_dram)
            gated_merge(nc, c, oT, a["w_blocks"], GATE_B, a["w_mix"], 1, merged, False)
            for base, n, conv, norm in ((Q_A, 2 * H, True, True), (V_A, H, True, False), (Z_A, H, False, False)):
                short_conv(nc, c, a["w_blocks"], a["short_w"], base, n, kept, conv, norm)
            delta_rule(nc, c, oT, kept, rows_dram, a["dn_norm"])
            gated_merge(nc, c, oT, a["w_blocks"], GATE_A, a["w_mix"], 0, merged, False)
        x2_dram = nc.dram_tensor("x2", (NT, P, D), F32, kind="Internal").ap()
        h2_dram = nc.dram_tensor("h2", (NT, P, D), F32, kind="Internal").ap()
        y_dram = nc.dram_tensor("y_blocks", (NB, P, D), F32, kind="Internal").ap()
        table = nc.dram_tensor("place_table", (NB * P, 1), I32, kind="Internal").ap()
        c.logits, c.gates = sb("logits", [P, NT, N_GRP + N_EXP]), sb("gates", [P, NT, 2])
        c.dest, c.block_expert = sb("dest", [P, NT, 2], I32), sb("block_expert", [1, NB], I32)
        c.blocks_before, c.last_step = sb("blocks_before", [1, N_EXP], I32), sb("last_step", [1, 1], I32)
        c.place_token = sb("place_token", [P, NB], I32)
        x = a["x"].rearrange("(t p) d -> t p d", p=P)
        output_and_router(nc, c, merged, x, a["w_out"], a["nf_row"], a["w_router"], a["b_router"], x2_dram, h2_dram)
        dispatch(nc, c, table)
        experts(nc, c, h2_dram.rearrange("t p d -> (t p) d"), a["w13"], a["w2"], y_dram)
        combine(nc, c, x2_dram, y_dram.rearrange("b p d -> (b p) d"), a["nl_row"], a["out"])


def lay_out(i):
    f = np.float32
    g = {k: np.asarray(v) for k, v in i.items()}
    w_in = g["w_in"][0]
    sizes = (512, 512, 512, 512, H, H, 512, 512, 512, H, 1024, D, D, D)
    at = np.cumsum((0,) + sizes)
    wide = [w_in[:, at[n]:at[n + 1]] for n in (0, 1, 2, 3, 6, 7, 8, 10, 11, 12, 13)]
    narrow = np.zeros((D, R_ALL), f)
    for row, n in ((R_BETA, 4), (R_DECAY, 5), (R_FORGET, 9)):
        narrow[:, row:row + H] = w_in[:, at[n]:at[n + 1]]

    def blocks(w):
        k, n = w.shape
        return np.ascontiguousarray(w.reshape(k // P, P, n // P, P).transpose(2, 1, 0, 3))

    def rows(w):
        return np.ascontiguousarray(w.reshape(w.shape[0] // P, P, -1).transpose(1, 0, 2))

    def cols(v):
        return np.ascontiguousarray(v.reshape(-1, P).T)

    sm_bias, a_log = np.zeros((R_ALL, 1), f), np.zeros((R_ALL, 1), f)
    sm_bias[R_DECAY:R_DECAY + H, 0] = g["dn_dt_bias"][0]
    sm_bias[R_FORGET:R_FORGET + H, 0] = g["fox_bias"][0]
    a_log[R_DECAY:R_DECAY + H, 0] = g["dn_a_log"][0]
    w13 = np.concatenate([g["expert_w1"][0], g["expert_w3"][0]], axis=-1)
    return {
        "x": np.ascontiguousarray(g["x"].reshape(T, D)),
        "nm_col": cols(g["norm_mix"][0]),
        "w_blocks": np.concatenate([blocks(w) for w in wide]),
        "w_narrow": rows(narrow),
        "sm_bias": sm_bias,
        "a_log": a_log,
        "short_w": np.ascontiguousarray(g["conv_qkv"][0].reshape(W_SHORT, 12, P).transpose(2, 1, 0)),
        "dw_w": np.ascontiguousarray(g["conv_dw"][0].reshape(W_CONV, KC, P).transpose(2, 1, 0)),
        "dw_b": cols(g["conv_dw_b"][0]),
        "ln_g": cols(g["conv_ln_g"][0]),
        "ln_b": cols(g["conv_ln_b"][0]),
        "dn_norm": cols(g["dn_norm"][0]),
        "w_mix": np.concatenate([blocks(g[n][0]) for n in ("w_a", "w_b", "w_c")]),
        "w_out": rows(g["w_out"][0]),
        "nf_row": g["norm_ffn"].reshape(1, D),
        "w_router": rows(np.concatenate([g["router_group_w"][0], g["router_expert_w"][0]], axis=1)),
        "b_router": np.concatenate([g["router_group_b"], g["router_expert_b"]], axis=1),
        "w13": np.ascontiguousarray(w13.reshape(N_EXP, KD, P, 2 * DE).transpose(0, 2, 1, 3)),
        "w2": np.ascontiguousarray(g["expert_w2"][0].reshape(N_EXP, DE // P, P, D).transpose(0, 2, 1, 3)),
        "nl_row": g["norm_final"].reshape(1, D),
    }


def kernel(**inputs):
    import concourse.bacc as _bacc
    from concourse.bass_utils import run_bass_kernel_spmd as _run

    nc = _bacc.Bacc("TRN2", target_bir_lowering=False, num_devices=1)
    arrays = {f"in_{n}_dram": v for n, v in lay_out(inputs).items()}
    a = {n[3:-5]: nc.dram_tensor(n, v.shape, mybir.dt.from_np(v.dtype), kind="ExternalInput").ap() for n, v in arrays.items()}
    a["out"] = nc.dram_tensor("out_0_dram", (NT, P, D), F32, kind="ExternalOutput").ap()
    build(nc, a)
    r = _run(nc, [arrays], core_ids=[0])
    return r.results[0]["out_0_dram"].reshape(1, T, D)
```

```python
from contextlib import ExitStack

import numpy as np

import concourse.bass as bass
from concourse import mybir

ALU = mybir.AluOpType
ACT = mybir.ActivationFunctionType
AX = mybir.AxisListType
F32 = mybir.dt.float32
I32 = mybir.dt.int32
U8 = mybir.dt.uint8
U32 = mybir.dt.uint32
F32R = mybir.dt.float32r

P = 128
T = 2048
D = 1024
KD = D // P
NT = T // P
G = 512
NG = T // G
GT = G // P
H = 4
KC = 4
NPAD = 64
N_EXP = 32
N_GRP = 4
PER_GRP = N_EXP // N_GRP
DE = 256
BLK = 128
NB = 2 * T // BLK + N_EXP
SLOTS = 4
W_CONV = 31
LEVELS = 7
W_SHORT = 4
EPS = 1e-6
BIG = 1e30
Q_A, K_A, V_A, SHORT_BLOCKS = 0, 4, 8, 12
STEP, S_CONV, S_GATE, S_Z, S_Q, S_K, S_V = 12, 1, 2, 8, 9, 10, 11
R_BETA, R_DECAY, R_FORGET, R_ALL = 0, 32, 64, 96


class Phase:

    def __init__(self, nc, name):
        self.nc, self.name, self.ctx, self.used = nc, name, ExitStack(), []

    def __enter__(self):
        self.ctx.__enter__()
        return self

    def __exit__(self, *a):
        self.ctx.__exit__(*a)
        if a[0] is None:
            self.nc.clear_and_free_semaphores(self.used)
            self.nc.all_engine_barrier()

    def sb(self, name, shape, dt=F32):
        return self.ctx.enter_context(self.nc.sbuf_tensor(f"{self.name}_{name}", shape, dt))

    def ps(self, name, shape, dt=F32):
        return self.ctx.enter_context(self.nc.psum_tensor(f"{self.name}_{name}", shape, dt))

    def sem(self, name):
        self.used.append(self.nc.alloc_semaphore(f"{self.name}_{name}"))
        return self.used[-1]

    def sems(self, name, n):
        return [self.sem(f"{name}{i}") for i in range(n)]

    def block(self):
        return self.ctx.enter_context(self.nc.Block())


class Chain:

    def __init__(self, eng, sem, per=0, round_=None):
        self.eng, self.sem, self.per, self.round, self.n = eng, sem, per, round_, 0

    def did(self, ins):
        ins.then_inc(self.sem, 1)
        self.n += 1
        return self.n

    def wait(self, n=None):
        n = self.n if n is None else n
        self.eng.wait_ge(self.sem, n if self.round is None else self.round * self.per + n)

    def end(self):
        assert self.n == self.per, (self.n, self.per)


def rounds(eng, n, first, both, last, ahead=1):
    first()
    loop = (n - ahead) // 2
    with eng.Fori(0, loop) as i:
        both(i * 2, 0)
        both(i * 2 + 1, 1)
    if (n - ahead) % 2:
        both(2 * loop, 0)
    last()


def tile_of(ap, t):
    return ap[:, t] if isinstance(t, int) else ap[:, bass.ds(t, 1)]


def constants(nc, c):
    with Phase(nc, "const") as ph:
        made = ph.sem("made")
        block = ph.block()

        @block.gpsimd
        def _(pool):
            st = Chain(pool, made)
            st.did(pool.memset(c.ones[:, :], 1.0))
            st.did(pool.memset(c.eps[:, :], EPS))
            st.did(pool.memset(c.ident[:, :], 0.0))
            st.wait()
            st.did(pool.affine_select(out=c.ident[:, :], in_=c.ident[:, :], compare_op=ALU.not_equal, fill=1.0,
                                      base=0, pattern=[[-1, P]], channel_multiplier=1))
            st.wait()


def make_masks(pool, made, c):
    st = Chain(pool, made)
    st.did(pool.memset(c.negtri[:, :], 0.0))
    st.wait()
    st.did(pool.affine_select(out=c.negtri[:, :], in_=c.negtri[:, :], compare_op=ALU.is_ge, fill=-BIG,
                              base=0, pattern=[[-1, P]], channel_multiplier=1))
    for m in (c.below, c.above):
        st.did(pool.memset(m[:, :, :], 1.0))
    st.did(pool.memset(c.upper[:, :], 1.0))
    st.did(pool.memset(c.past[:, :], 0.0))
    st.wait()
    st.did(pool.affine_select(out=c.upper[:, :], in_=c.upper[:, :], compare_op=ALU.is_gt, fill=0.0,
                              base=0, pattern=[[1, P]], channel_multiplier=-1))
    st.did(pool.affine_select(out=c.past[:, :], in_=c.past[:, :], compare_op=ALU.is_ge, fill=-BIG,
                              base=0, pattern=[[1, P]], channel_multiplier=-1))
    for l in range(LEVELS):
        n = 1 << l
        for m, row_lo, row_hi, col in ((c.below, n, 2 * n, (n - 1, -1)), (c.above, 0, n, (-n, 1))):
            v = m[:, l, :].rearrange("p (b s) -> p b s", s=2 * n)
            nb = P // (2 * n)
            for base, pat, mult in ((-row_lo, [[-2 * n, nb], [0, 2 * n]], 1),
                                    (row_hi - 1, [[2 * n, nb], [0, 2 * n]], -1),
                                    (col[0], [[0, nb], [col[1], 2 * n]], 0)):
                st.did(pool.affine_select(out=v, in_=v, compare_op=ALU.is_ge, fill=0.0, base=base,
                                          pattern=pat, channel_multiplier=mult))
                st.wait()
    st.wait()


def norm_and_transpose(nc, c, x, gain):
    with Phase(nc, "norm") as ph:
        xt = ph.sb("xt", [P, 2, D])
        xn = ph.sb("xn", [P, 2, D])
        junk = ph.sb("junk", [P, 2, D])
        h = ph.sb("h", [P, 2, KD, P])
        ss = ph.sb("ss", [P, 2])
        sd = ph.sb("sd", [P, 2])
        rs = ph.sb("rs", [P, 2])
        gcol = ph.sb("gcol", [P, KD])
        tp = ph.ps("tp", [P, 2, D])
        x_in = ph.sems("x_in", 2)
        g_in = ph.sem("g_in")
        x_free, xn_free, tp_free = ph.sem("x_free"), ph.sem("xn_free"), ph.sem("tp_free")
        squares, sd_ready, recip, xn_ready, turned = (ph.sem(n) for n in ("squares", "sd_ready", "recip", "xn_ready", "turned"))
        h_free, h_done, hi_done = ph.sem("h_free"), ph.sem("h_done"), ph.sem("hi_done")
        block = ph.block()

        @block.sync
        def _(sp):
            sp.dma_start(gcol[:, :], gain).then_inc(g_in, 16)
            with sp.Fori(0, NT // 2) as i:
                for p in range(2):
                    sp.wait_ge(x_free, i * 2 + (p + 1))
                    sp.dma_start(xt[:, p, :], x[i * 2 + p]).then_inc(x_in[p], 16)

        @block.scalar
        def _(act):
            def deviations(i):
                for p in range(2):
                    act.wait_ge(x_in[p], i * 16 + 16)
                    act.activation(junk[:, p, :], xt[:, p, :], ACT.Square, accum_out=ss[:, p:p + 1]).then_inc(squares, 1)
                for p in range(2):
                    act.wait_ge(squares, i * 2 + (p + 1))
                    act.wait_ge(x_free, i * 2 + (p + 1))
                    act.activation(sd[:, p:p + 1], ss[:, p:p + 1], ACT.Sqrt, scale=1.0 / D, bias=c.eps[:, 0:1]).then_inc(sd_ready, 1)

            def high_parts(i):
                for p in range(2):
                    act.wait_ge(h_done, i * 2 + (p + 1))
                    act.activation(c.h_hi[:, :, bass.ds(i * (2 * P) + p * P, P)], h[:, p, :, :], ACT.Copy).then_inc(hi_done, 1)

            deviations(0)
            with act.Fori(0, NT // 2 - 1) as i:
                deviations(i + 1)
                high_parts(i)
            high_parts(NT // 2 - 1)

        @block.gpsimd
        def _(pool):
            pool.sem_inc(h_free, 2)
            with pool.Fori(0, NT // 2) as i:
                for p in range(2):
                    here = bass.ds(i * (2 * P) + p * P, P)
                    pool.wait_ge(hi_done, i * 2 + (p + 1))
                    pool.tensor_tensor(c.h_lo[:, :, here], h[:, p, :, :], c.h_hi[:, :, here].bitcast(F32), ALU.subtract).then_inc(h_free, 1)

        @block.vector
        def _(dve):
            dve.sem_inc(x_free, 2)
            dve.wait_ge(g_in, 16)

            def scaled(i):
                for p in range(2):
                    dve.wait_ge(sd_ready, i * 2 + (p + 1))
                    dve.reciprocal(rs[:, p:p + 1], sd[:, p:p + 1]).then_inc(recip, 1)
                for p in range(2):
                    dve.wait_ge(recip, i * 2 + (p + 1))
                    dve.wait_ge(xn_free, i * 2 + (p + 1))
                    dve.tensor_scalar(xn[:, p, :], xt[:, p, :], rs[:, p:p + 1], None, ALU.mult).then_inc(x_free, 1)
                    dve.wait_ge(x_free, i * 2 + (p + 3))
                    dve.sem_inc(xn_ready, 1)

            def gained(i):
                for p in range(2):
                    dve.wait_ge(turned, i * 2 + (p + 1))
                    dve.wait_ge(h_free, i * 2 + (p + 1))
                    dve.tensor_tensor(h[:, p, :, :], tp[:, p, :].rearrange("p (k t) -> p k t", t=P),
                                      gcol[:, :].unsqueeze(2).to_broadcast([P, KD, P]), ALU.mult).then_inc(tp_free, 1)
                    dve.wait_ge(tp_free, i * 2 + (p + 3))
                    dve.sem_inc(h_done, 1)

            scaled(0)
            with dve.Fori(0, NT // 2 - 1) as i:
                scaled(i + 1)
                gained(i)
            gained(NT // 2 - 1)

        @block.tensor
        def _(pe):
            pe.sem_inc(xn_free, 2)
            pe.sem_inc(tp_free, 2)
            with pe.Fori(0, NT // 2) as i:
                for p in range(2):
                    pe.wait_ge(xn_ready, i * 2 + (p + 1))
                    pe.wait_ge(tp_free, i * 2 + (p + 1))
                    for k in range(KD):
                        last = pe.transpose(tp[:, p, k * P:(k + 1) * P], xn[:, p, k * P:(k + 1) * P], c.ident[:, :])
                    last.then_inc(turned, 1)
                    pe.wait_ge(turned, i * 2 + (p + 1))
                    pe.sem_inc(xn_free, 1)


def narrow_rows(nc, c, w_narrow, sm_bias, a_log, rows_dram):
    with Phase(nc, "narrow") as ph:
        w = ph.sb("w", [P, KD, R_ALL])
        w_hi, w_lo = ph.sb("w_hi", [P, KD, R_ALL], F32R), ph.sb("w_lo", [P, KD, R_ALL], F32R)
        bias, coef, sign = ph.sb("bias", [R_ALL, 1]), ph.sb("coef", [R_ALL, 1]), ph.sb("sign", [R_ALL, 1])
        u, mag, sp, keep, cum = (ph.sb(n, [R_ALL, T]) for n in ("u", "mag", "sp", "keep", "cum"))
        out = ph.ps("out", [P, NG, G])
        turned = ph.ps("turned", [P, NT, P])
        w_in, b_in, stored, hi_done, lo_done = (ph.sem(n) for n in ("w_in", "b_in", "stored", "hi_done", "lo_done"))
        projected, dve_done, act_done, cols_turned = (ph.sem(n) for n in ("projected", "dve_done", "act_done", "cols_turned"))
        block = ph.block()

        @block.sync
        def _(sp_):
            sp_.dma_start(w[:, :, :], w_narrow).then_inc(w_in, 16)
            sp_.dma_start(bias[:, :], sm_bias).then_inc(b_in, 16)
            sp_.dma_start(coef[:, :], a_log).then_inc(b_in, 16)
            sp_.wait_ge(act_done, 5)
            sp_.dma_start(rows_dram, cum[:, :]).then_inc(stored, 16)
            sp_.wait_ge(stored, 16)

        @block.tensor
        def _(pe):
            pe.wait_ge(lo_done, 1)
            for g in range(NG):
                tok = slice(g * G, (g + 1) * G)
                last = split_products(pe, out[0:R_ALL, g, :], lambda k: w_hi[:, k, :], lambda k: w_lo[:, k, :],
                                      lambda k: c.h_hi[:, k, tok], lambda k: c.h_lo[:, k, tok], KD)
            last.then_inc(projected, 1)
            pe.wait_ge(act_done, 5)
            for t in range(NT):
                last = pe.transpose(turned[:, t, 0:R_ALL], cum[:, t * P:(t + 1) * P], c.ident[0:R_ALL, 0:R_ALL])
            last.then_inc(cols_turned, 1)

        @block.scalar
        def _(act):
            act.wait_ge(w_in, 16)
            act.activation(w_hi[:, :, :], w[:, :, :], ACT.Copy).then_inc(hi_done, 1)
            act.wait_ge(b_in, 32)
            act.activation(coef[R_DECAY:R_DECAY + 32, :], coef[R_DECAY:R_DECAY + 32, :], ACT.Exp).then_inc(act_done, 1)
            act.wait_ge(dve_done, 3)
            act.activation(mag[:, :], u[:, :], ACT.Abs).then_inc(act_done, 1)
            act.wait_ge(act_done, 2)
            act.activation(mag[:, :], mag[:, :], ACT.Exp, scale=-1.0).then_inc(act_done, 1)
            act.wait_ge(act_done, 3)
            act.activation(sp[:, :], mag[:, :], ACT.Ln, bias=c.ones[0:R_ALL, 0:1]).then_inc(act_done, 1)
            act.wait_ge(dve_done, 6)
            act.activation(cum[R_BETA:R_BETA + H, :], out[R_BETA:R_BETA + H, :, :].rearrange("p g t -> p (g t)"), ACT.Sigmoid).then_inc(act_done, 1)

        @block.gpsimd
        def _(pool):
            pool.wait_ge(hi_done, 1)
            pool.tensor_tensor(w_lo[:, :, :], w[:, :, :], w_hi[:, :, :].bitcast(F32), ALU.subtract).then_inc(lo_done, 1)

        @block.vector
        def _(dve):
            st = Chain(dve, dve_done)
            dve.wait_ge(b_in, 32)
            dve.wait_ge(act_done, 1)
            dve.memset(sign[:, :], 1.0)
            dve.memset(keep[:, :], 1.0)
            st.did(dve.tensor_scalar(coef[R_DECAY:R_DECAY + 32, :], coef[R_DECAY:R_DECAY + 32, :], -1.0, None, ALU.mult))
            st.wait()
            dve.memset(coef[R_FORGET:R_ALL, :], -1.0)
            dve.memset(sign[R_FORGET:R_ALL, :], -1.0)
            dve.memset(coef[0:32, :], -1.0)
            st.did(dve.memset(keep[R_DECAY:R_DECAY + 32, :].rearrange("p (t c) -> p t c", c=P)[:, :, 0:1], 0.0))
            st.wait()
            dve.wait_ge(projected, 1)
            st.did(dve.tensor_scalar(u[:, :], out[0:R_ALL, :, :].rearrange("p g t -> p (g t)"), bias[:, 0:1], sign[:, 0:1], ALU.add, ALU.mult))
            st.wait()
            dve.wait_ge(act_done, 4)
            st.did(dve.scalar_tensor_tensor(out=u[:, :], in0=u[:, :], scalar=0.0, in1=sp[:, :], op0=ALU.max, op1=ALU.add))
            st.wait()
            st.did(dve.tensor_scalar(u[:, :], u[:, :], coef[:, 0:1], None, ALU.mult))
            st.wait()
            st.did(dve.tensor_tensor_scan(cum[:, :], keep[:, :], u[:, :], 0.0, ALU.mult, ALU.add))
            dve.wait_ge(cols_turned, 1)
            st.did(dve.tensor_copy(c.cols[:, :, :], turned[:, :, 0:R_ALL]))
            st.wait()


def split_products(eng, out, w_hi, w_lo, x_hi, x_lo, n):
    for k in range(n):
        eng.matmul(out, w_hi(k), x_hi(k), start=(k == 0), stop=False)
        eng.matmul(out, w_hi(k), x_lo(k), start=False, stop=False)
        last = eng.matmul(out, w_lo(k), x_hi(k), start=False, stop=(k == n - 1))
    return last


def project_blocks(nc, c, w_blocks, dw_w, dw_b, wide):
    PAD = W_CONV - 1
    N = KC * STEP
    with Phase(nc, "proj") as ph:
        raw = ph.sb("raw", [P, 2, KD, P])
        w_hi, w_lo = ph.sb("w_hi", [P, 2, KD, P], F32R), ph.sb("w_lo", [P, 2, KD, P], F32R)
        taps, tap_b = ph.sb("taps", [P, KC, W_CONV]), ph.sb("tap_b", [P, KC])
        z, acc = ph.sb("z", [P, PAD + T]), ph.sb("acc", [P, T])
        res = ph.sb("res", [P, 2, T])
        pp = ph.ps("pp", [P, 2, NG, G])
        w_in, stored = ph.sems("w_in", 2), ph.sems("stored", 2)
        names = ("taps_in", "hi_done", "lo_done", "projected", "drained", "gate_ready", "gated", "conv_step", "conv_done",
                 "conv_stored", "acc_free", "out_free")
        (taps_in, hi_done, lo_done, projected, drained, gate_ready, gated, conv_step, conv_done,
         conv_stored, acc_free, out_free) = (ph.sem(n) for n in names)
        block = ph.block()

        @block.sync
        def _(sp):
            sp.dma_start(taps[:, :, :], dw_w).then_inc(taps_in, 16)
            sp.dma_start(tap_b[:, :], dw_b).then_inc(taps_in, 16)
            with sp.Fori(0, N // 2) as i:
                for p in range(2):
                    sp.wait_ge(lo_done, i * 2 + (p + 1))
                    sp.dma_start(raw[:, p, :, :], w_blocks[i * 2 + (SHORT_BLOCKS + p)]).then_inc(w_in[p], 16)

        @block.tensor
        def _(pe):
            pe.sem_inc(projected, 2 * NG)
            with pe.Fori(0, N // 2) as i:
                for p in range(2):
                    pe.wait_ge(lo_done, i * 2 + (p + 3))
                    for g in range(NG):
                        pe.wait_ge(drained, i * (2 * NG) + (p * NG + g + 1))
                        tok = slice(g * G, (g + 1) * G)
                        split_products(pe, pp[:, p, g, :], lambda k: w_hi[:, p, k, :], lambda k: w_lo[:, p, k, :],
                                       lambda k: c.h_hi[:, k, tok], lambda k: c.h_lo[:, k, tok], KD).then_inc(projected, 1)

        @block.scalar
        def _(act):
            act.sem_inc(drained, 2 * NG)

            def high_part(j, s):
                n, p = j * STEP + s, s % 2
                act.wait_ge(w_in[p], j * (8 * STEP) + (s // 2 * 16 + 16))
                act.wait_ge(projected, n * NG + NG)
                act.activation(w_hi[:, p, :, :], raw[:, p, :, :], ACT.Copy).then_inc(hi_done, 1)

            def drain(j, s):
                n, p = j * STEP + s, s % 2
                if s == 0:
                    act.wait_ge(conv_done, j + 1)
                if s >= 2:
                    act.wait_ge(out_free, j * (STEP - 2) + (s - 1))
                if s == 1:
                    act.wait_ge(drained, n * NG + 2 * NG)
                for g in range(NG):
                    act.wait_ge(projected, n * NG + (g + 1 + 2 * NG))
                    if s == 0:
                        act.activation(z[:, PAD + g * G:PAD + (g + 1) * G], pp[:, p, g, :], ACT.Sigmoid).then_inc(drained, 1)
                    elif s == 1:
                        act.wait_ge(gated, j * NG + (g + 1))
                        act.sem_inc(drained, 1)
                    else:
                        func = ACT.Sigmoid if s < S_Z else ACT.Silu if s == S_Z else ACT.Copy
                        scale = float(P) ** -0.5 if s == S_Q else 1.0
                        act.activation(res[:, p, g * G:(g + 1) * G], pp[:, p, g, :], func, scale=scale).then_inc(drained, 1)

            def step(j, last):
                for s in range(STEP):
                    if not (last and s == STEP - 1):
                        high_part(j, s + 1)
                    drain(j, s)

            high_part(0, 0)
            with act.Fori(0, KC - 1) as j:
                step(j, False)
            step(KC - 1, True)

        @block.gpsimd
        def _(pool):
            pool.sem_inc(lo_done, 2)
            pool.sem_inc(out_free, 2)
            pool.sem_inc(acc_free, 1)

            def low_part(j, s):
                p = s % 2
                pool.wait_ge(hi_done, j * STEP + (s + 1))
                pool.tensor_tensor(w_lo[:, p, :, :], raw[:, p, :, :], w_hi[:, p, :, :].bitcast(F32), ALU.subtract).then_inc(lo_done, 1)

            def store(j, s):
                n, p = j * STEP + s, s % 2
                pool.wait_ge(drained, n * NG + 3 * NG)
                pool.dma_start(wide[n], res[:, p, :]).then_inc(stored[p], 16)
                pool.wait_ge(stored[p], j * (8 * (STEP - 2)) + ((s - 2) // 2 * 16 + 16))
                pool.sem_inc(out_free, 1)

            def store_conv(j):
                pool.wait_ge(conv_done, j + 2)
                pool.dma_start(wide[j * STEP + S_CONV], acc[:, :]).then_inc(conv_stored, 16)
                pool.wait_ge(conv_stored, j * 16 + 16)
                pool.sem_inc(acc_free, 1)

            def step(j, last):
                for s in range(STEP):
                    if not (last and s == STEP - 1):
                        low_part(j, s + 1)
                    if s >= 2:
                        store(j, s)
                    if s == STEP // 2:
                        store_conv(j)

            low_part(0, 0)
            with pool.Fori(0, KC - 1) as j:
                step(j, False)
            step(KC - 1, True)

        @block.vector
        def _(dve):
            dve.sem_inc(conv_done, 1)
            dve.memset(z[:, 0:PAD], 0.0)
            dve.wait_ge(taps_in, 32)
            with dve.Fori(0, KC) as j:
                st = Chain(dve, conv_step, W_CONV, j)
                for g in range(NG):
                    dve.wait_ge(projected, j * (STEP * NG) + (NG + g + 1 + 2 * NG))
                    dve.wait_ge(drained, j * (STEP * NG) + (g + 1 + 2 * NG))
                    part = z[:, PAD + g * G:PAD + (g + 1) * G]
                    dve.tensor_tensor(part, pp[:, 1, g, :], part, ALU.mult).then_inc(gated, 1)
                dve.wait_ge(gated, j * NG + NG)
                dve.wait_ge(acc_free, j + 1)
                for k in range(W_CONV):
                    tap, src = taps[:, bass.ds(j, 1), k:k + 1].rearrange("p a b -> p (a b)"), z[:, k:k + T]
                    if k == 0:
                        st.did(dve.tensor_scalar(acc[:, :], src, tap, tap_b[:, bass.ds(j, 1)], ALU.mult, ALU.add))
                    else:
                        st.did(dve.scalar_tensor_tensor(out=acc[:, :], in0=src, scalar=tap, in1=acc[:, :], op0=ALU.mult, op1=ALU.add))
                    st.wait()
                st.end()
                dve.sem_inc(conv_done, 1)


def conformer_norm(nc, c, oT, wide, ln_g, ln_b):
    with Phase(nc, "ln") as ph:
        mean_w = ph.sb("mean_w", [P, P])
        g_col, b_col = ph.sb("g_col", [P, KC]), ph.sb("b_col", [P, KC])
        sq = ph.sb("sq", [P, KC, G])
        logs, rs = ph.sb("logs", [P, 2, G]), ph.sb("rs", [P, 2, G])
        mu, var = ph.ps("mu", [P, NG, G]), ph.ps("var", [P, NG, G])
        x_in, cols_in, w_ready, mu_done, var_done, centred, squared, logs_ready, scaled, rs_ready, act_done = (
            ph.sem(n) for n in ("x_in", "cols_in", "w_ready", "mu_done", "var_done", "centred", "squared", "logs_ready", "scaled", "rs_ready", "act_done"))
        block = ph.block()

        @block.sync
        def _(sp):
            sp.dma_start(oT[:, :, :], wide.rearrange("(j s) p t -> p j s t", s=STEP)[:, :, S_CONV, :]).then_inc(x_in, 16)
            sp.dma_start(g_col[:, :], ln_g).then_inc(cols_in, 16)
            sp.dma_start(b_col[:, :], ln_b).then_inc(cols_in, 16)

        @block.gpsimd
        def _(pool):
            pool.memset(mean_w[:, :], 1.0 / (KC * P)).then_inc(w_ready, 1)

        @block.tensor
        def _(pe):
            pe.wait_ge(w_ready, 1)
            pe.wait_ge(x_in, 16)
            for g in range(NG):
                for j in range(KC):
                    last = pe.matmul(mu[:, g, :], mean_w[:, :], oT[:, j, g * G:(g + 1) * G], start=(j == 0), stop=(j == KC - 1))
                last.then_inc(mu_done, 1)
            for g in range(NG):
                pe.wait_ge(squared, g + 1)
                for j in range(KC):
                    last = pe.matmul(var[:, g, :], mean_w[:, :], sq[:, j, :], start=(j == 0), stop=(j == KC - 1))
                last.then_inc(var_done, 1)

        @block.scalar
        def _(act):
            act.wait_ge(cols_in, 32)
            for g in range(NG):
                act.wait_ge(centred, g + 1)
                if g:
                    act.wait_ge(var_done, g)
                act.activation(sq[:, :, :], oT[:, :, g * G:(g + 1) * G], ACT.Square).then_inc(squared, 1)
                act.wait_ge(var_done, g + 1)
                if g >= 2:
                    act.wait_ge(scaled, g - 1)
                act.activation(logs[:, g % 2, :], var[:, g, :], ACT.Ln, bias=c.eps[:, 0:1]).then_inc(logs_ready, 1)
                act.wait_ge(logs_ready, g + 1)
                act.activation(rs[:, g % 2, :], logs[:, g % 2, :], ACT.Exp, scale=-0.5).then_inc(rs_ready, 1)
            for g in range(NG):
                act.wait_ge(scaled, g + 1)
                for j in range(KC):
                    part = oT[:, j, g * G:(g + 1) * G]
                    act.activation(part, part, ACT.Silu, scale=g_col[:, j:j + 1], bias=b_col[:, j:j + 1])

        @block.vector
        def _(dve):
            for g in range(NG):
                part = oT[:, :, g * G:(g + 1) * G]
                dve.wait_ge(mu_done, g + 1)
                dve.tensor_tensor(part, part, mu[:, g, :].unsqueeze(1).to_broadcast([P, KC, G]), ALU.subtract).then_inc(centred, 1)
            for g in range(NG):
                part = oT[:, :, g * G:(g + 1) * G]
                dve.wait_ge(rs_ready, g + 1)
                dve.wait_ge(centred, g + 1)
                dve.wait_ge(squared, g + 1)
                dve.tensor_tensor(part, part, rs[:, g % 2, :].unsqueeze(1).to_broadcast([P, KC, G]), ALU.mult).then_inc(scaled, 1)


def gated_merge(nc, c, oT, wide, w_mix, mix, merged, first):
    with Phase(nc, f"merge{mix}") as ph:
        raw = ph.sb("raw", [P, 2, KC, P])
        w_hi, w_lo = ph.sb("w_hi", [P, 2, KC, P], F32R), ph.sb("w_lo", [P, 2, KC, P], F32R)
        o_hi, o_lo = ph.sb("o_hi", [P, KC, T], F32R), ph.sb("o_lo", [P, KC, T], F32R)
        gate = ph.sb("gate", [P, 2, NG, G])
        py = ph.ps("py", [P, 2, NG, G])
        w_in, gate_in = ph.sems("w_in", 2), ph.sems("gate_in", 2)
        names = ("o_hi_done", "o_lo_done", "hi_done", "lo_done", "y_done", "gated", "summed")
        o_hi_done, o_lo_done, hi_done, lo_done, y_done, gated, summed = (ph.sem(n) for n in names)
        block = ph.block()

        @block.sync
        def _(sp):
            with sp.Fori(0, KD // 2) as i:
                for p in range(2):
                    sp.wait_ge(lo_done, i * 2 + (p + 1))
                    sp.dma_start(raw[:, p, :, :], w_mix[i * 2 + (mix * KD + p)]).then_inc(w_in[p], 16)
                    sp.wait_ge(summed, i * 2 + (p + 1))
                    sp.dma_start(gate[:, p, :, :].rearrange("p g t -> p (g t)"), wide[i * STEP + (S_GATE + 2 * mix + p)]).then_inc(gate_in[p], 16)

        @block.tensor
        def _(pe):
            with pe.Fori(0, KD // 2) as i:
                for p in range(2):
                    pe.wait_ge(lo_done, i * 2 + (p + 3))
                    for g in range(NG):
                        if p == 0:
                            pe.wait_ge(o_lo_done, g + 1)
                        pe.wait_ge(gated, i * (2 * NG) + (p * NG + g + 1))
                        tok = slice(g * G, (g + 1) * G)
                        split_products(pe, py[:, p, g, :], lambda k: w_hi[:, p, k, :], lambda k: w_lo[:, p, k, :],
                                       lambda k: o_hi[:, k, tok], lambda k: o_lo[:, k, tok], KC).then_inc(y_done, 1)

        @block.scalar
        def _(act):
            act.sem_inc(y_done, 2 * NG)

            def high_part(j, p, i):
                act.wait_ge(w_in[p], i * 16 + 16)
                act.wait_ge(y_done, j * NG + NG)
                act.activation(w_hi[:, p, :, :], raw[:, p, :, :], ACT.Copy).then_inc(hi_done, 1)

            high_part(0, 0, 0)
            high_part(1, 1, 0)
            for g in range(NG):
                act.activation(o_hi[:, :, g * G:(g + 1) * G], oT[:, :, g * G:(g + 1) * G], ACT.Copy).then_inc(o_hi_done, 1)
            with act.Fori(1, KD // 2) as i:
                for p in range(2):
                    high_part(i * 2 + p, p, i)

        @block.vector
        def _(dve):
            dve.sem_inc(gated, 2 * NG)
            for g in range(NG):
                tok = slice(g * G, (g + 1) * G)
                dve.wait_ge(o_hi_done, g + 1)
                dve.tensor_tensor(o_lo[:, :, tok], oT[:, :, tok], o_hi[:, :, tok].bitcast(F32), ALU.subtract).then_inc(o_lo_done, 1)
            with dve.Fori(0, KD // 2) as i:
                for p in range(2):
                    dve.wait_ge(gate_in[p], i * 16 + 16)
                    for g in range(NG):
                        n = i * (2 * NG) + (p * NG + g + 1 + 2 * NG)
                        dve.wait_ge(y_done, n)
                        if first:
                            to = merged[:, bass.ds(i * 2 + p, 1), g * G:(g + 1) * G].rearrange("p a t -> p (a t)")
                        else:
                            to = gate[:, p, g, :]
                        dve.tensor_tensor(to, py[:, p, g, :], gate[:, p, g, :], ALU.mult).then_inc(gated, 1)

        @block.gpsimd
        def _(pool):
            pool.sem_inc(lo_done, 2)
            pool.sem_inc(summed, 2)

            def low_part(j, p):
                pool.wait_ge(hi_done, j + 1)
                pool.tensor_tensor(w_lo[:, p, :, :], raw[:, p, :, :], w_hi[:, p, :, :].bitcast(F32), ALU.subtract).then_inc(lo_done, 1)

            def add(j, p):
                pool.wait_ge(gated, j * NG + 3 * NG)
                if first:
                    pool.sem_inc(summed, 1)
                else:
                    to = tile_of(merged, j)
                    have = gate[:, p, :, :].rearrange("p g t -> p (g t)")
                    have = have if isinstance(j, int) else have.unsqueeze(1)
                    pool.tensor_tensor(to, to, have, ALU.add).then_inc(summed, 1)

            low_part(0, 0)
            low_part(1, 1)
            with pool.Fori(0, KD // 2 - 1) as i:
                for p in range(2):
                    low_part(i * 2 + (p + 2), p)
                    add(i * 2 + p, p)
            add(KD - 2, 0)
            add(KD - 1, 1)


def forgetting_attention(nc, c, oT, wide, rows_dram):
    with Phase(nc, "fox") as ph:
        staged = ph.sb("staged", [P, 3, T])
        lost = ph.sb("lost", [P, T])
        qT, kT, v = ph.sb("qT", [P, T]), ph.sb("kT", [P, T]), ph.sb("v", [P, T])
        logits, probs = ph.sb("logits", [P, T]), ph.sb("probs", [P, 2, T])
        mx, nm = ph.sb("mx", [P, 2, NG]), ph.sb("nm", [P, 2])
        dens, den, rden = ph.sb("dens", [P, 2, NG]), ph.sb("den", [P, 2]), ph.sb("rden", [P, 2])
        pT = ph.sb("pT", [P, 2, GT, P])
        on = ph.sb("on", [P, 2, P])
        big = ph.ps("big", [P, NG, G])
        flat = big[:, :, :].rearrange("p g t -> p (g t)")
        turn = ph.ps("turn", [P, 2, GT, P])
        po = ph.ps("po", [P, G])
        pot = ph.ps("pot", [P, G])
        staged_in, lost_in = ph.sem("staged_in"), ph.sem("lost_in")
        names = ("filled", "emptied", "scored", "biased", "nm_ready", "exped", "turned", "t_copied",
                 "pv_done", "on_ready", "o_turned", "o_stored", "v_chain", "heads_done", "t_pv", "lost_free", "waited")
        (filled, emptied, scored, biased, nm_ready, exped, turned, t_copied,
         pv_done, on_ready, o_turned, o_stored, v_chain, heads_done, t_pv, lost_free, waited) = (ph.sem(n) for n in names)
        segs = [i // GT + 1 for i in range(NT)]
        before = [sum(segs[:i]) for i in range(NT + 1)]
        ALL = before[NT]
        masks_made = ph.sem("masks_made")
        block = ph.block()

        @block.sync
        def _(sp):
            with sp.Fori(0, H) as h:
                sp.wait_ge(emptied, h * 6 + 6)
                for n, s in enumerate((S_Q, S_K, S_V)):
                    sp.dma_start(staged[:, n, :], wide[h * STEP + s]).then_inc(staged_in, 16)
                sp.wait_ge(lost_free, h + 1)
                sp.dma_start(lost[:, :], rows_dram[bass.ds(h + R_FORGET, 1), :].to_broadcast([P, T])).then_inc(lost_in, 16)

        @block.gpsimd
        def _(pool):
            make_masks(pool, masks_made, c)

        @block.tensor
        def _(pe):
            pe.wait_ge(masks_made, 2)
            with pe.Fori(0, H) as h:
                pe.wait_ge(staged_in, h * 48 + 48)
                pe.wait_ge(biased, h * ALL + 1)
                for g in range(NG):
                    for t in range(GT * g, GT * (g + 1)):
                        last = pe.transpose(flat[:, t * P:(t + 1) * P], staged[:, 2, t * P:(t + 1) * P], c.ident[:, :])
                    last.then_inc(filled, 1)
                pe.wait_ge(emptied, h * 6 + 12)

                def score(i):
                    pe.wait_ge(biased, h * ALL + (before[i] + 1))
                    for s in range(segs[i]):
                        n = min(G, (i + 1) * P - s * G)
                        diag = s == segs[i] - 1
                        last = pe.matmul(big[:, s, 0:n], qT[:, i * P:(i + 1) * P], kT[:, s * G:s * G + n], start=True, stop=not diag)
                        if diag:
                            last = pe.matmul(big[:, s, n - P:n], c.ident[:, :], c.negtri[:, :], start=False, stop=True)
                        last.then_inc(scored, 1)

                def turn_group(i, s):
                    m = before[i] + s
                    pe.wait_ge(exped, h * ALL + (m + 1))
                    pe.wait_ge(t_copied, h * ALL + (m + 1))
                    for b in range(min(GT, i + 1 - s * GT)):
                        j = s * GT + b
                        last = pe.transpose(turn[:, m % 2, b, :], probs[:, i % 2, j * P:(j + 1) * P], c.ident[:, :])
                    last.then_inc(turned, 1)

                def weigh_group(i, s):
                    m = before[i] + s
                    pe.wait_ge(t_copied, h * ALL + (m + 3))
                    if s == 0:
                        pe.wait_ge(on_ready, h * NT + (i + 1))
                    for b in range(min(GT, i + 1 - s * GT)):
                        j = s * GT + b
                        last = pe.matmul(po[:, 0:P], pT[:, m % 2, b, :], v[:, j * P:(j + 1) * P], start=(j == 0), stop=(j == i))
                    last.then_inc(t_pv, 1)
                    if s == segs[i] - 1:
                        pe.wait_ge(t_pv, h * ALL + (m + 3))
                        pe.sem_inc(pv_done, 1)

                def turn_out(i):
                    pe.wait_ge(on_ready, h * NT + (i + 2))
                    pe.wait_ge(o_stored, h * NT + (i + 1))
                    pe.transpose(pot[:, 0:P], on[:, i % 2, :], c.ident[:, :]).then_inc(o_turned, 1)

                score(0)
                for i in range(NT):
                    if i + 1 < NT:
                        score(i + 1)
                    turn_group(i, 0)
                    for s in range(segs[i]):
                        if s + 1 < segs[i]:
                            turn_group(i, s + 1)
                        weigh_group(i, s)
                    if i:
                        turn_out(i - 1)
                turn_out(NT - 1)

        @block.scalar
        def _(act):
            act.sem_inc(t_copied, 2)
            act.sem_inc(emptied, 6)
            with act.Fori(0, H) as h:
                act.wait_ge(heads_done, h + 1)
                act.wait_ge(staged_in, h * 48 + 48)
                for n, dst in enumerate((qT, kT)):
                    act.activation(dst[:, :], staged[:, n, :], ACT.Copy).then_inc(emptied, 1)
                for g in range(NG):
                    act.wait_ge(filled, h * NG + (g + 1))
                    act.activation(v[:, g * G:(g + 1) * G], big[:, g, :], ACT.Copy).then_inc(emptied, 1)

                def soften(i, s):
                    if s == 0:
                        act.wait_ge(nm_ready, h * NT + (i + 1))
                        if i >= 2:
                            act.wait_ge(turned, h * ALL + before[i - 1])
                    keys = slice(s * G, min((s + 1) * G, (i + 1) * P))
                    act.activation(probs[:, i % 2, keys], logits[:, keys], ACT.Exp, bias=nm[:, i % 2:i % 2 + 1],
                                   accum_out=dens[:, i % 2, s:s + 1]).then_inc(exped, 1)

                soften(0, 0)
                for i in range(NT):
                    for s in range(segs[i]):
                        m = before[i] + s
                        act.wait_ge(turned, h * ALL + (m + 1))
                        act.wait_ge(t_pv, h * ALL + (m + 1))
                        b = min(GT, i + 1 - s * GT)
                        act.activation(pT[:, m % 2, 0:b, :], turn[:, m % 2, 0:b, :], ACT.Copy).then_inc(t_copied, 1)
                        if i + 1 < NT:
                            soften(i + 1, s)
                    if i + 1 < NT and segs[i + 1] > segs[i]:
                        soften(i + 1, segs[i])

        @block.vector
        def _(dve):
            dve.sem_inc(biased, 1)
            dve.sem_inc(heads_done, 1)
            dve.sem_inc(on_ready, 1)
            dve.sem_inc(o_stored, 1)
            dve.sem_inc(lost_free, 1)
            dve.sem_inc(t_pv, 2)
            with dve.Fori(0, H) as h:
                st = Chain(dve, v_chain, 2 * NT, h)

                def bias(i):
                    for s in range(segs[i]):
                        if i and s < segs[i - 1]:
                            dve.wait_ge(exped, h * ALL + (before[i - 1] + s + 1))
                        n = min(G, (i + 1) * P - s * G)
                        dve.wait_ge(scored, h * ALL + (before[i] + s + 1))
                        dve.sem_inc(waited, 1)
                        dve.tensor_tensor_reduce(logits[:, s * G:s * G + n], big[:, s, 0:n], lost[:, s * G:s * G + n], 1.0, -3e38,
                                                 ALU.subtract, ALU.max, mx[:, i % 2, s:s + 1]).then_inc(biased, 1)
                    dve.wait_ge(biased, h * ALL + (before[i + 1] + 1))
                    dve.tensor_reduce(nm[:, i % 2:i % 2 + 1], mx[:, i % 2, 0:segs[i]], AX.X, ALU.max, negate=True).then_inc(nm_ready, 1)

                def finish(i):
                    dve.wait_ge(exped, h * ALL + before[i + 1])
                    st.did(dve.tensor_reduce(den[:, i % 2:i % 2 + 1], dens[:, i % 2, 0:segs[i]], AX.X, ALU.add))
                    st.wait()
                    st.did(dve.reciprocal(rden[:, i % 2:i % 2 + 1], den[:, i % 2:i % 2 + 1]))
                    st.wait()
                    dve.wait_ge(pv_done, h * NT + (i + 1))
                    if i >= 2:
                        dve.wait_ge(o_turned, h * NT + (i - 1))
                    dve.tensor_scalar(on[:, i % 2, :], po[:, 0:P], rden[:, i % 2:i % 2 + 1], None, ALU.mult).then_inc(on_ready, 1)

                def store(i):
                    dve.wait_ge(o_turned, h * NT + (i + 1))
                    dve.tensor_copy(oT[:, bass.ds(h, 1), i * P:(i + 1) * P].rearrange("p a t -> p (a t)"), pot[:, 0:P]).then_inc(o_stored, 1)

                dve.wait_ge(lost_in, h * 16 + 16)
                bias(0)
                for i in range(NT):
                    if i + 1 < NT:
                        bias(i + 1)
                    if i:
                        store(i - 1)
                    finish(i)
                store(NT - 1)
                st.end()
                dve.wait_ge(biased, h * ALL + (ALL + 1))
                dve.sem_inc(lost_free, 1)
                dve.sem_inc(heads_done, 1)


def short_conv(nc, c, w_blocks, short_w, base, n, kept, norm):
    PAD = W_SHORT - 1
    assert n % 2 == 0 and n >= 4
    with Phase(nc, f"short{base}") as ph:
        raw = ph.sb("raw", [P, 2, KD, P])
        w_hi, w_lo = ph.sb("w_hi", [P, 2, KD, P], F32R), ph.sb("w_lo", [P, 2, KD, P], F32R)
        taps = ph.sb("taps", [P, 12, W_SHORT])
        z = ph.sb("z", [P, 2, PAD + T])
        acc, out = ph.sb("acc", [P, T]), ph.sb("out", [P, T])
        pp, pn = ph.ps("pp", [P, NG, G]), ph.ps("pn", [P, NG, G])
        lengths_flat = pn[:, :, :].rearrange("p g t -> p (g t)")
        w_in, stored = ph.sems("w_in", 2), ph.sem("stored")
        names = ("taps_in", "hi_done", "lo_done", "projected", "copied", "dve_done", "conv_done", "z_free", "silu_done", "squared",
                 "lengths_done", "logs_ready", "scales_ready", "done", "pad_ready", "alone")
        (taps_in, hi_done, lo_done, projected, copied, dve_done, conv_done, z_free, silu_done, squared,
         lengths_done, logs_ready, scales_ready, done, pad_ready, alone) = (ph.sem(x) for x in names)
        block = ph.block()

        @block.sync
        def _(sp):
            sp.dma_start(taps[:, :, :], short_w).then_inc(taps_in, 16)
            with sp.Fori(0, n // 2) as i:
                for p in range(2):
                    sp.wait_ge(lo_done, i * 2 + (p + 1))
                    sp.dma_start(raw[:, p, :, :], w_blocks[i * 2 + (base + p)]).then_inc(w_in[p], 16)

        @block.gpsimd
        def _(pool):
            pool.sem_inc(lo_done, 2)
            with pool.Fori(0, n // 2) as i:
                for p in range(2):
                    pool.wait_ge(hi_done, i * 2 + (p + 1))
                    pool.tensor_tensor(w_lo[:, p, :, :], raw[:, p, :, :], w_hi[:, p, :, :].bitcast(F32), ALU.subtract).then_inc(lo_done, 1)

        @block.tensor
        def _(pe):
            pe.sem_inc(projected, 2 * NG)

            def lengths(j):
                pe.wait_ge(squared, j + 1)
                pe.wait_ge(done, j + 1)
                for g in range(NG):
                    last = pe.matmul(pn[:, g, :], c.ones[:, :], acc[:, g * G:(g + 1) * G], start=True, stop=True)
                last.then_inc(lengths_done, 1)

            def project(j, p, first=False):
                pe.wait_ge(lo_done, j + 3)
                for g in range(NG):
                    pe.wait_ge(copied, j * NG + (g + 1))
                    tok = slice(g * G, (g + 1) * G)
                    split_products(pe, pp[:, g, :], lambda k: w_hi[:, p, k, :], lambda k: w_lo[:, p, k, :],
                                   lambda k: c.h_hi[:, k, tok], lambda k: c.h_lo[:, k, tok], KD).then_inc(projected, 1)
                    if norm and g == 2 and not first:
                        lengths(j - 1)

            project(0, 0, first=True)
            with pe.Fori(0, n // 2 - 1) as i:
                project(i * 2 + 1, 1)
                project(i * 2 + 2, 0)
            project(n - 1, 1)
            if norm:
                lengths(n - 1)

        @block.scalar
        def _(act):
            act.sem_inc(copied, NG)

            def high_part(j, p):
                act.wait_ge(w_in[p], (j // 2) * 16 + 16 if isinstance(j, int) else j * 8 + (16 if p == 0 else 8))
                act.wait_ge(projected, j * NG + NG)
                act.activation(w_hi[:, p, :, :], raw[:, p, :, :], ACT.Copy).then_inc(hi_done, 1)

            def copy(j, p, g):
                act.wait_ge(projected, j * NG + (g + 1 + 2 * NG))
                act.activation(z[:, p, PAD + g * G:PAD + (g + 1) * G], pp[:, g, :], ACT.Copy).then_inc(copied, 1)

            def silu(j):
                act.wait_ge(conv_done, j + 1)
                if not isinstance(j, int) or j:
                    act.wait_ge(stored, j * 16)
                act.activation(out[:, :], acc[:, :], ACT.Silu).then_inc(silu_done, 1)
                if norm:
                    act.wait_ge(silu_done, j + 1)
                    act.activation(acc[:, :], out[:, :], ACT.Square).then_inc(squared, 1)

            def roots(j):
                if norm:
                    act.wait_ge(lengths_done, j + 1)
                    act.activation(lengths_flat, lengths_flat, ACT.Ln, bias=c.eps[:, 0:1]).then_inc(logs_ready, 1)
                    act.wait_ge(logs_ready, j + 1)
                    act.activation(lengths_flat, lengths_flat, ACT.Exp, scale=-0.5).then_inc(scales_ready, 1)

            def store(j):
                act.wait_ge(done if norm else silu_done, j + (2 if norm else 1))
                act.sem_inc(alone, 1)
                act.dma_start(kept[j + base], out[:, :]).then_inc(stored, 16)

            def through(j, p, before=True, two_before=True, more=True):
                if more:
                    high_part(j + 1, 1 - p)
                act.wait_ge(z_free, j + 1)
                copy(j, p, 0)
                if two_before:
                    store(j - 2)
                copy(j, p, 1)
                if before:
                    silu(j - 1)
                copy(j, p, 2)
                if before:
                    roots(j - 1)
                copy(j, p, 3)

            high_part(0, 0)
            through(0, 0, before=False, two_before=False)
            through(1, 1, two_before=False)
            if n > 4:
                with act.Fori(1, n // 2 - 1) as i:
                    through(i * 2, 0)
                    through(i * 2 + 1, 1)
            through(n - 2, 0)
            through(n - 1, 1, more=False)
            store(n - 2)
            silu(n - 1)
            roots(n - 1)
            store(n - 1)
            act.wait_ge(stored, n * 16)

        @block.vector
        def _(dve):
            dve.sem_inc(z_free, 2)
            dve.sem_inc(done, 1)
            dve.memset(z[:, :, 0:PAD], 0.0).then_inc(pad_ready, 1)
            dve.wait_ge(pad_ready, 1)
            dve.wait_ge(taps_in, 16)
            with dve.Fori(0, n // 2) as i:
                for p in range(2):
                    j = i * 2 + p
                    st = Chain(dve, dve_done, W_SHORT + (1 if norm else 0), j)
                    dve.wait_ge(copied, j * NG + 2 * NG)
                    for k in range(W_SHORT):
                        tap, src = taps[:, bass.ds(j + base, 1), k:k + 1].rearrange("p a b -> p (a b)"), z[:, p, k:k + T]
                        if k == 0:
                            st.did(dve.tensor_scalar(acc[:, :], src, tap, None, ALU.mult))
                        else:
                            st.did(dve.scalar_tensor_tensor(out=acc[:, :], in0=src, scalar=tap, in1=acc[:, :], op0=ALU.mult, op1=ALU.add))
                        st.wait()
                    dve.sem_inc(z_free, 1)
                    dve.sem_inc(conv_done, 1)
                    if norm:
                        dve.wait_ge(scales_ready, j + 1)
                        st.did(dve.tensor_tensor(out[:, :], out[:, :], lengths_flat, ALU.mult))
                        st.wait()
                        dve.sem_inc(done, 1)
                    else:
                        dve.wait_ge(silu_done, j + 1)
                    st.end()


def delta_rule(nc, c, oT, kept, projected, rows_dram, dn_norm):
    SCALE = float(P) ** -0.5
    ND = LEVELS - 1
    XY = 2 * LEVELS - 1
    with Phase(nc, "delta") as ph:
        four = [P, H, P]
        qkv, z = ph.sb("qkv", [P, 2, 3, H, P]), ph.sb("z", [P, 2, H, P])
        g_row, b_row = ph.sb("g_row", [P, 2, H, P]), ph.sb("b_row", [P, 2, H, P])
        small, smallx = ph.sb("small", [P, 2, 3 * H]), ph.sb("smallx", [P, 2, 3 * H])
        beta, nbeg, qscale = ph.sb("beta", [P, 2, H]), ph.sb("nbeg", [P, 2, H]), ph.sb("qscale", [P, 2, H])
        dif, E, W, nAT, X, M, R, Rt, v_new, S, Sdec, oq, o, osq, on = (
            ph.sb(n, four) for n in ("dif", "E", "W", "nAT", "X", "M", "R", "Rt", "v_new", "S", "Sdec", "oq", "o", "osq", "on"))
        PT, Kd, Vb, Y = (ph.sb(n, [P, 2, H, P]) for n in ("PT", "Kd", "Vb", "Y"))
        ssq, sd, rs = (ph.sb(n, [P, H]) for n in ("ssq", "sd", "rs"))
        dn = ph.sb("dn", [P, 1])
        p0, p1, p2, p3, q0, q1, q2, q3 = (ph.ps(f"bank{n}", four) for n in range(8))
        ins, z_in, dn_in = ph.sems("ins", 2), ph.sems("z_in", 2), ph.sem("dn_in")
        names = ("in_free", "gram", "turned", "small_in", "dif_done", "expd", "masked", "was_read", "init", "init_y", "kd", "v_step", "nat", "kvb", "nA",
                 "S_ready", "ks", "r_half", "r", "vn", "vn_copied", "pv", "s_decayed", "oq_done",
                 "o_done", "alone", "osq_done", "ssq_done", "sd_done", "rs_done", "on_done", "o_turned", "stored", "nbeg_done")
        e = {n: ph.sem(n) for n in names}
        xy, m_done, m_copied, t_done = (ph.sems(n, 2) for n in ("xy", "m_done", "m_copied", "t_done"))
        block = ph.block()

        heads_of = [range(0, H // 2), range(H // 2, H)]

        m_bank = [p2, p3]

        def for_x(u):
            return (p0, p1)[u][:, 0:H // 2, :]

        def for_y(u):
            return (p0, p1)[u][:, H // 2:, :]

        def part(ap, u):
            return ap[:, u * H // 2:(u + 1) * H // 2, :]

        def each(eng, out, lhs, rhs, heads=range(H)):
            for n, h in enumerate(heads):
                last = eng.matmul(out[:, n, :], lhs[:, h, :], rhs[:, h, :], start=True, stop=True)
            return last

        def turn(eng, out, src):
            for h in range(H):
                last = eng.transpose(out[:, h, :], src[:, h, :], c.ident[:, :])
            return last

        def wide(col):
            return col.unsqueeze(2).to_broadcast(four)

        @block.sync
        def _(sp):
            sp.dma_start(dn[:, :], dn_norm).then_inc(dn_in, 16)
            tokens = kept.rearrange("(a h) p t -> p a h t", h=H)
            z_blocks = projected.rearrange("(h s) p t -> p h s t", s=STEP)[:, :, S_Z, :]
            with sp.Fori(0, NT // 2) as i:
                for p in range(2):
                    sp.wait_ge(e["was_read"], i * 2 + (p + 1))
                    here = bass.ds(i * (2 * P) + p * P, P)
                    for a in range(3):
                        sp.dma_start(qkv[:, p, a, :, :], tokens[:, a, :, here]).then_inc(ins[p], 16)
                    for dst, row in ((g_row, R_DECAY), (b_row, R_BETA)):
                        sp.dma_start(dst[:, p, :, :], rows_dram[row:row + H, here].unsqueeze(0).to_broadcast(four)).then_inc(ins[p], 16)
                    sp.wait_ge(e["in_free"], i * 2 + (p + 1))
                    sp.dma_start(z[:, p, :, :], z_blocks[:, :, here]).then_inc(z_in[p], 16)

        @block.tensor
        def _(pe):
            def gram(t, p):
                q, k, v = (qkv[:, p, n, :, :] for n in range(3))
                pe.wait_ge(ins[p], (t // 2) * 80 + 80 if isinstance(t, int) else t * 40 + (80 if p == 0 else 40))
                for u in range(2):
                    pe.wait_ge(xy[u], t * XY + 1)
                each(pe, p0, k, k)
                each(pe, p1, k, q).then_inc(e["gram"], 1)
                turn(pe, p2, k)
                turn(pe, p3, v).then_inc(e["turned"], 1)

            def turn_a(t):
                pe.wait_ge(e["nat"], t + 1)
                turn(pe, p0, nAT).then_inc(e["nA"], 1)

            def level(t, p, l, between=None):
                if l == 1:
                    pe.wait_ge(e["kvb"], t + 1)
                    pe.wait_ge(e["kd"], t + 1)
                for u in range(2):
                    pe.wait_ge(xy[u], t * XY + (2 * l + 1))
                    each(pe, m_bank[u], nAT, X, heads_of[u]).then_inc(m_done[u], 1)
                if between:
                    between()
                for u in range(2):
                    pe.wait_ge(m_copied[u], t * ND + l)
                    if l < ND:
                        each(pe, for_x(u), Y[:, p, :, :], M, heads_of[u])
                    each(pe, for_y(u), M, Y[:, p, :, :], heads_of[u]).then_inc(t_done[u], 1)

            def read_state(t, p):
                pe.wait_ge(e["S_ready"], t + 1)
                pe.wait_ge(e["o_done"], t + 1)
                each(pe, q0, qkv[:, p, 1, :, :], S)
                each(pe, q1, qkv[:, p, 0, :, :], S).then_inc(e["ks"], 1)

            def new_values(t, p):
                pe.wait_ge(e["r"], t + 1)
                for u in range(2):
                    pe.wait_ge(xy[u], t * XY + (XY + 1))
                pe.wait_ge(e["stored"], t + 1)
                each(pe, q2, Y[:, p, :, :], R).then_inc(e["vn"], 1)

            def use_values(t, p):
                pe.wait_ge(e["vn_copied"], t + 1)
                each(pe, q3, PT[:, p, :, :], v_new)
                each(pe, q0, Kd[:, p, :, :], v_new).then_inc(e["pv"], 1)

            def turn_o(t):
                pe.wait_ge(e["on_done"], t + 1)
                turn(pe, q2, on).then_inc(e["o_turned"], 1)

            def before(t, p):
                gram(t, p)
                turn_a(t)
                for l in range(1, LEVELS):
                    level(t, p, l)

            def both(t, p):
                read_state(t, p)
                gram(t + 1, 1 - p)
                turn_a(t + 1)
                new_values(t, p)
                between = {1: lambda: use_values(t, p), 4: lambda: turn_o(t)}
                for l in range(1, LEVELS):
                    level(t + 1, 1 - p, l, between.get(l))

            def within(t, p):
                read_state(t, p)
                new_values(t, p)
                use_values(t, p)
                turn_o(t)

            rounds(pe, NT, lambda: before(0, 0), both, lambda: within(NT - 1, 1))

        @block.scalar
        def _(act):
            def decay(t, p):
                act.wait_ge(e["dif_done"], t + 1)
                act.wait_ge(e["masked"], t + 1)
                act.activation(E[:, :, :], dif[:, :, :], ACT.Exp)
                act.wait_ge(e["in_free"], t + 1)
                act.activation(smallx[:, p, :], small[:, p, :], ACT.Exp).then_inc(e["expd"], 1)

            def copy_m(t, l):
                for u in range(2):
                    act.wait_ge(m_done[u], t * ND + l)
                    act.activation(part(M, u), m_bank[u][:, 0:H // 2, :], ACT.Copy).then_inc(m_copied[u], 1)

            def key_part(t, p):
                act.wait_ge(e["turned"], t + 1)
                act.wait_ge(e["expd"], t + 1)
                for h in range(H):
                    last = act.activation(Kd[:, p, h, :], p2[:, h, :], ACT.Copy, scale=smallx[:, p, H + h:H + h + 1])
                last.then_inc(e["kd"], 1)

            def copy_values(t):
                act.wait_ge(e["vn"], t + 1)
                act.wait_ge(e["S_ready"], t + 1)
                act.activation(v_new[:, :, :], q2[:, :, :], ACT.Copy).then_inc(e["vn_copied"], 1)

            def deviation(t):
                act.wait_ge(e["ssq_done"], t + 1)
                act.wait_ge(e["rs_done"], t + 1)
                act.activation(sd[:, :], ssq[:, :], ACT.Sqrt, scale=1.0 / P, bias=c.eps[:, 0:1]).then_inc(e["sd_done"], 1)

            def before(t, p):
                decay(t, p)
                key_part(t, p)
                for l in range(1, LEVELS):
                    copy_m(t, l)
                decay(t + 1, 1 - p)

            def both(t, p):
                key_part(t + 1, 1 - p)
                copy_values(t)
                for l in range(1, LEVELS):
                    copy_m(t + 1, l)
                    if l == 3:
                        deviation(t)
                if not (isinstance(t, int) and t + 2 >= NT):
                    decay(t + 2, p)

            def within(t, p):
                copy_values(t)
                deviation(t)

            rounds(act, NT, lambda: before(0, 0), both, lambda: within(NT - 1, 1))

        @block.gpsimd
        def _(pool):
            pool.sem_inc(e["masked"], 1)
            pool.sem_inc(e["s_decayed"], 1)

            def masks(t, p):
                pool.wait_ge(e["expd"], t + 1)
                pool.wait_ge(e["v_step"], t + 1)
                pool.tensor_tensor(W[:, :, :], E[:, :, :], b_row[:, p, :, :], ALU.mult).then_inc(e["masked"], 1)

            def start_y(t, p):
                pool.wait_ge(e["in_free"], t + 1)
                pool.sem_inc(e["alone"], 1)
                pool.tensor_copy(Y[:, p, :, :], c.ident[:, :].unsqueeze(1).to_broadcast(four)).then_inc(e["init_y"], 1)

            def start_x(t):
                for u in range(2):
                    pool.wait_ge(xy[u], t * XY + 1)
                pool.sem_inc(e["alone"], 1)
                pool.tensor_copy(X[:, :, :], c.ident[:, :].unsqueeze(1).to_broadcast(four)).then_inc(e["init"], 1)

            def decay_state(t, p):
                pool.wait_ge(e["expd"], t + 1)
                pool.wait_ge(e["S_ready"], t + 1)
                pool.tensor_tensor(Sdec[:, :, :], S[:, :, :], wide(smallx[:, p, 2 * H:]), ALU.mult).then_inc(e["s_decayed"], 1)

            def square(t):
                pool.wait_ge(e["o_done"], t + 2)
                pool.wait_ge(e["rs_done"], t + 1)
                pool.tensor_tensor(osq[:, :, :], o[:, :, :], o[:, :, :], ALU.mult).then_inc(e["osq_done"], 1)

            def before(t, p):
                start_y(t, p)
                masks(t, p)
                start_x(t)
                start_y(t + 1, 1 - p)
                masks(t + 1, 1 - p)

            def both(t, p):
                start_x(t + 1)
                decay_state(t, p)
                square(t)
                if not (isinstance(t, int) and t + 2 >= NT):
                    start_y(t + 2, p)
                    masks(t + 2, p)

            def within(t, p):
                decay_state(t, p)
                square(t)

            rounds(pool, NT, lambda: before(0, 0), both, lambda: within(NT - 1, 1))

        @block.vector
        def _(dve):
            dve.sem_inc(e["in_free"], 2)
            dve.sem_inc(e["was_read"], 2)
            for u in range(2):
                dve.sem_inc(xy[u], 1)
            dve.sem_inc(e["o_done"], 1)
            dve.sem_inc(e["stored"], 1)
            dve.sem_inc(e["rs_done"], 1)
            dve.sem_inc(e["v_step"], 1)
            dve.memset(S[:, :, :], 0.0).then_inc(e["S_ready"], 1)
            dve.wait_ge(dn_in, 16)

            def differences(t, p):
                dve.wait_ge(ins[p], (t // 2) * 80 + 80 if isinstance(t, int) else t * 40 + (80 if p == 0 else 40))
                dve.wait_ge(e["masked"], t + 1)
                here = c.cols[:, bass.ds(t, 1), :].rearrange("p a r -> p (a r)") if not isinstance(t, int) else c.cols[:, t, :]
                dve.tensor_copy(beta[:, p, :], here[:, R_BETA:R_BETA + H])
                dve.tensor_copy(small[:, p, 0:H], here[:, R_DECAY:R_DECAY + H]).then_inc(e["small_in"], 1)
                dve.tensor_copy(small[:, p, 2 * H:], g_row[:, p, :, P - 1])
                dve.wait_ge(e["small_in"], t * 2 + 1)
                dve.tensor_tensor(small[:, p, H:2 * H], g_row[:, p, :, P - 1], small[:, p, 0:H], ALU.subtract).then_inc(e["small_in"], 1)
                for h in range(H):
                    last = dve.scalar_tensor_tensor(out=dif[:, h, :], in0=g_row[:, p, h, :], scalar=small[:, p, h:h + 1],
                                                    in1=c.past[:, :], op0=ALU.subtract, op1=ALU.add)
                last.then_inc(e["dif_done"], 1)

            def attention_parts(t, p):
                dve.wait_ge(e["expd"], t + 1)
                dve.wait_ge(e["gram"], t + 1)
                dve.wait_ge(e["masked"], t + 2)
                dve.scalar_tensor_tensor(out=nAT[:, :, :], in0=p0[:, :, :], scalar=-1.0, in1=W[:, :, :], op0=ALU.mult, op1=ALU.mult).then_inc(e["nat"], 1)
                dve.scalar_tensor_tensor(out=PT[:, p, :, :], in0=p1[:, :, :], scalar=SCALE, in1=E[:, :, :], op0=ALU.mult, op1=ALU.mult).then_inc(e["v_step"], 1)
                dve.scalar_tensor_tensor(out=nbeg[:, p, :], in0=beta[:, p, :], scalar=-1.0, in1=smallx[:, p, 0:H], op0=ALU.mult, op1=ALU.mult)
                dve.tensor_scalar(qscale[:, p, :], smallx[:, p, 0:H], SCALE, None, ALU.mult).then_inc(e["nbeg_done"], 1)
                dve.wait_ge(e["turned"], t + 1)
                dve.tensor_tensor(Vb[:, p, :, :], p3[:, :, :], wide(beta[:, p, :]), ALU.mult).then_inc(e["kvb"], 1)

            def mask(m, l):
                return m[:, l, :].bitcast(U32).unsqueeze(1).to_broadcast([P, H // 2, P])

            def first_level(t, p):
                dve.wait_ge(e["nA"], t + 1)
                dve.wait_ge(e["init"], t + 1)
                dve.wait_ge(e["init_y"], t + 1)
                dve.sem_inc(e["alone"], 1)
                for u in range(2):
                    dve.copy_predicated(part(X, u), mask(c.below, 0), part(p0, u)).then_inc(xy[u], 1)
                    dve.copy_predicated(part(Y[:, p, :, :], u), mask(c.above, 0), part(nAT, u)).then_inc(xy[u], 1)

            def level(t, p, l):
                for u in range(2):
                    dve.wait_ge(t_done[u], t * ND + l)
                    dve.wait_ge(xy[u], t * XY + (2 * l + 1))
                    dve.sem_inc(e["alone"], 1)
                    if l < ND:
                        dve.copy_predicated(part(X, u), mask(c.below, l), for_x(u)).then_inc(xy[u], 1)
                    dve.copy_predicated(part(Y[:, p, :, :], u), mask(c.above, l), for_y(u)).then_inc(xy[u], 1)

            def residual(t, p):
                dve.wait_ge(e["ks"], t + 1)
                dve.wait_ge(e["kvb"], t + 1)
                dve.wait_ge(e["nbeg_done"], t + 1)
                dve.tensor_tensor(Rt[:, :, :], q0[:, :, :], wide(nbeg[:, p, :]), ALU.mult).then_inc(e["r_half"], 1)
                dve.wait_ge(e["r_half"], t + 1)
                dve.tensor_tensor(R[:, :, :], Rt[:, :, :], Vb[:, p, :, :], ALU.add).then_inc(e["r"], 1)

            def next_state(t):
                dve.wait_ge(e["pv"], t + 1)
                dve.wait_ge(e["s_decayed"], t + 2)
                dve.tensor_tensor(S[:, :, :], q0[:, :, :], Sdec[:, :, :], ALU.add).then_inc(e["S_ready"], 1)

            def output(t, p):
                dve.tensor_tensor(oq[:, :, :], q1[:, :, :], wide(qscale[:, p, :]), ALU.mult).then_inc(e["oq_done"], 1)
                dve.wait_ge(e["oq_done"], t + 1)
                dve.tensor_tensor(o[:, :, :], q3[:, :, :], oq[:, :, :], ALU.add).then_inc(e["o_done"], 1)
                dve.wait_ge(e["o_done"], t + 2)
                dve.sem_inc(e["was_read"], 1)

            def squares(t):
                dve.wait_ge(e["osq_done"], t + 1)
                dve.tensor_reduce(ssq[:, :], osq[:, :, :], AX.X, ALU.add).then_inc(e["ssq_done"], 1)

            def normalise(t):
                dve.wait_ge(e["sd_done"], t + 1)
                dve.reciprocal(rs[:, :], sd[:, :]).then_inc(e["rs_done"], 1)
                dve.wait_ge(e["rs_done"], t + 2)
                dve.tensor_tensor(on[:, :, :], o[:, :, :], wide(rs[:, :]), ALU.mult).then_inc(e["on_done"], 1)

            def store(t, p):
                dve.wait_ge(e["o_turned"], t + 1)
                dve.wait_ge(z_in[p], (t // 2) * 16 + 16 if isinstance(t, int) else t * 8 + (16 if p == 0 else 8))
                here = slice(t * P, (t + 1) * P) if isinstance(t, int) else bass.ds(t * P, P)
                dve.scalar_tensor_tensor(out=oT[:, :, here], in0=q2[:, :, :], scalar=dn[:, 0:1], in1=z[:, p, :, :],
                                         op0=ALU.mult, op1=ALU.mult).then_inc(e["stored"], 1)
                dve.wait_ge(e["stored"], t + 2)
                dve.sem_inc(e["in_free"], 1)

            def before(t, p):
                differences(t, p)
                attention_parts(t, p)
                first_level(t, p)
                for l in range(1, LEVELS):
                    level(t, p, l)
                differences(t + 1, 1 - p)

            def both(t, p):
                residual(t, p)
                attention_parts(t + 1, 1 - p)
                first_level(t + 1, 1 - p)
                between = {1: lambda: (next_state(t), output(t, p)), 2: lambda: squares(t), 3: lambda: normalise(t), 4: lambda: store(t, p)}
                for l in range(1, LEVELS):
                    if l == LEVELS - 1 and not (isinstance(t, int) and t + 2 >= NT):
                        differences(t + 2, p)
                    level(t + 1, 1 - p, l)
                    if l in between:
                        between[l]()

            def within(t, p):
                residual(t, p)
                next_state(t)
                output(t, p)
                squares(t)
                normalise(t)
                store(t, p)

            rounds(dve, NT, lambda: before(0, 0), both, lambda: within(NT - 1, 1))


def output_and_router(nc, c, merged, x, w_out, nf_row, w_router, b_router, x2_dram, h2_dram):
    NR = N_GRP + N_EXP
    with Phase(nc, "out") as ph:
        wo_hi, wo_lo = ph.sb("wo_hi", [P, KD, D], F32R), ph.sb("wo_lo", [P, KD, D], F32R)
        m_hi, m_lo = ph.sb("m_hi", [P, 2, KD, P], F32R), ph.sb("m_lo", [P, 2, KD, P], F32R)
        wr = ph.sb("wr", [P, KD, NR])
        nf, br = ph.sb("nf", [P, D]), ph.sb("br", [P, NR])
        xt = ph.sb("xt", [P, 2, D])
        x2, h2, junk = ph.sb("x2", [P, 2, D]), ph.sb("h2", [P, 2, D]), ph.sb("junk", [P, D])
        h2T = ph.sb("h2T", [P, 2, KD, P])
        ss, sd, rs = ph.sb("ss", [P, 2]), ph.sb("sd", [P, 2]), ph.sb("rs", [P, 2])
        px = ph.ps("px", [P, 2, D])
        pt = ph.ps("pt", [P, D])
        pr = ph.ps("pr", [P, 2, G])
        staged = [x2[:, 0, :], x2[:, 1, :], h2[:, 0, :], h2[:, 1, :]]
        const_in, w_in, ins = ph.sem("const_in"), ph.sems("w_in", 4), ph.sems("ins", 2)
        x2_out, h2_out = ph.sems("x2_out", 2), ph.sems("h2_out", 2)
        names = ("in_free", "wo_hi", "wo_lo", "m_hi", "m_lo", "product", "x2_ready", "squared", "sd_done", "rs_done", "h2_ready", "turned", "copied", "routed", "logits", "x2_free", "h2_free")
        e = {n: ph.sem(n) for n in names}
        block = ph.block()

        @block.sync
        def _(sp):
            for k in range(KD):
                if k >= 4:
                    sp.wait_ge(e["wo_lo"], k - 3)
                sp.dma_start(staged[k % 4], w_out[:, k, :]).then_inc(w_in[k % 4], 16)
            with sp.Fori(0, NT // 2) as i:
                for p in range(2):
                    sp.wait_ge(e["in_free"], i * 2 + (p + 1))
                    sp.dma_start(xt[:, p, :], x[i * 2 + p]).then_inc(ins[p], 16)

        @block.tensor
        def _(pe):
            pe.sem_inc(e["product"], 2)
            pe.wait_ge(e["wo_lo"], KD)
            pe.wait_ge(const_in, 48)

            def product(t, p, half):
                if half == 0:
                    pe.wait_ge(e["m_lo"], t + 1)
                    pe.wait_ge(e["in_free"], t + 1)
                cols = slice(half * G, (half + 1) * G)
                last = split_products(pe, px[:, p, cols], lambda k: m_hi[:, p, k, :], lambda k: m_lo[:, p, k, :],
                                      lambda k: wo_hi[:, k, cols], lambda k: wo_lo[:, k, cols], KD)
                if half == 1:
                    last.then_inc(e["product"], 1)

            def turn(t, p):
                pe.wait_ge(e["h2_ready"], t + 1)
                pe.wait_ge(e["copied"], t + 1)
                for k in range(KD):
                    last = pe.transpose(pt[:, k * P:(k + 1) * P], h2[:, p, k * P:(k + 1) * P], c.ident[:, :])
                last.then_inc(e["turned"], 1)

            def route(t, p):
                pe.wait_ge(e["copied"], t + 2)
                pe.wait_ge(e["logits"], t + 1)
                for k in range(KD):
                    last = pe.matmul(pr[:, p, 0:NR], h2T[:, p, k, :], wr[:, k, :], start=(k == 0), stop=(k == KD - 1))
                last.then_inc(e["routed"], 1)

            def first():
                for half in range(2):
                    product(0, 0, half)

            def both(t, p):
                product(t + 1, 1 - p, 0)
                turn(t, p)
                product(t + 1, 1 - p, 1)
                route(t, p)

            def last():
                turn(NT - 1, 1)
                route(NT - 1, 1)

            rounds(pe, NT, first, both, last)

        @block.scalar
        def _(act):
            act.sem_inc(e["copied"], 1)

            def high_part(t, p):
                act.wait_ge(e["product"], t + 1)
                tile = merged[:, :, t * P:(t + 1) * P] if isinstance(t, int) else merged[:, :, bass.ds(t * P, P)]
                act.activation(m_hi[:, p, :, :], tile, ACT.Copy).then_inc(e["m_hi"], 1)

            def norm_and_copy(t, p):
                act.wait_ge(e["x2_ready"], t + 1)
                act.wait_ge(e["rs_done"], t + 1)
                act.wait_ge(e["sd_done"], t + 1)
                act.activation(junk[:, :], x2[:, p, :], ACT.Square, accum_out=ss[:, p:p + 1]).then_inc(e["squared"], 1)
                act.wait_ge(e["squared"], t + 1)
                act.activation(sd[:, p:p + 1], ss[:, p:p + 1], ACT.Sqrt, scale=1.0 / D, bias=c.eps[:, 0:1]).then_inc(e["sd_done"], 1)
                act.wait_ge(e["turned"], t + 1)
                act.wait_ge(e["logits"], t + 1)
                act.activation(h2T[:, p, :, :].rearrange("p k t -> p (k t)"), pt[:, :], ACT.Copy).then_inc(e["copied"], 1)

            for k in range(KD):
                act.wait_ge(w_in[k % 4], k // 4 * 16 + 16)
                act.activation(wo_hi[:, k, :], staged[k % 4], ACT.Copy).then_inc(e["wo_hi"], 1)
            high_part(0, 0)
            high_part(1, 1)
            with act.Fori(0, NT // 2 - 1) as i:
                for p in range(2):
                    high_part(i * 2 + (p + 2), p)
                    norm_and_copy(i * 2 + p, p)
            norm_and_copy(NT - 2, 0)
            norm_and_copy(NT - 1, 1)

        @block.vector
        def _(dve):
            for n in ("in_free", "rs_done"):
                dve.sem_inc(e[n], 2)
            dve.sem_inc(e["sd_done"], 1)
            dve.sem_inc(e["logits"], 1)
            for k in range(KD):
                dve.wait_ge(e["wo_hi"], k + 1)
                dve.tensor_tensor(wo_lo[:, k, :], staged[k % 4], wo_hi[:, k, :].bitcast(F32), ALU.subtract).then_inc(e["wo_lo"], 1)
            dve.wait_ge(const_in, 48)
            dve.wait_ge(e["wo_lo"], KD)

            def add(t, p):
                dve.wait_ge(e["product"], t + 3)
                dve.wait_ge(ins[p], 16 + (t // 2) * 16 if isinstance(t, int) else t * 8 + (16 if p == 0 else 8))
                dve.wait_ge(e["x2_free"], t + 1)
                dve.tensor_tensor(x2[:, p, :], px[:, p, :], xt[:, p, :], ALU.add).then_inc(e["x2_ready"], 1)
                dve.wait_ge(e["x2_ready"], t + 1)
                dve.sem_inc(e["in_free"], 1)

            def scale(t, p):
                dve.wait_ge(e["sd_done"], t + 2)
                dve.reciprocal(rs[:, p:p + 1], sd[:, p:p + 1]).then_inc(e["rs_done"], 1)
                dve.wait_ge(e["rs_done"], t + 3)
                dve.wait_ge(e["h2_free"], t + 1)
                dve.scalar_tensor_tensor(out=h2[:, p, :], in0=x2[:, p, :], scalar=rs[:, p:p + 1], in1=nf[:, :], op0=ALU.mult,
                                         op1=ALU.mult).then_inc(e["h2_ready"], 1)

            def keep(t, p):
                dve.wait_ge(e["routed"], t + 1)
                out = tile_of(c.logits, t)
                out = out if isinstance(t, int) else out.rearrange("p a n -> p (a n)")
                dve.tensor_tensor(out, pr[:, p, 0:NR], br[:, :], ALU.add).then_inc(e["logits"], 1)

            def first():
                add(0, 0)
                scale(0, 0)

            def both(t, p):
                add(t + 1, 1 - p)
                keep(t, p)
                scale(t + 1, 1 - p)

            rounds(dve, NT, first, both, lambda: keep(NT - 1, 1))

        @block.gpsimd
        def _(pool):
            pool.sem_inc(e["x2_free"], 2)
            pool.sem_inc(e["h2_free"], 2)
            pool.dma_start(nf[:, :], nf_row.to_broadcast([P, D])).then_inc(const_in, 16)
            pool.dma_start(br[:, :], b_router.to_broadcast([P, NR])).then_inc(const_in, 16)
            pool.dma_start(wr[:, :, :], w_router).then_inc(const_in, 16)

            def low_part(t, p):
                pool.wait_ge(e["m_hi"], t + 1)
                tile = merged[:, :, t * P:(t + 1) * P] if isinstance(t, int) else merged[:, :, bass.ds(t * P, P)]
                pool.tensor_tensor(m_lo[:, p, :, :], tile, m_hi[:, p, :, :].bitcast(F32), ALU.subtract).then_inc(e["m_lo"], 1)

            def store(t, p):
                pool.wait_ge(e["h2_ready"], t + 1)
                pool.dma_start(x2_dram[t], x2[:, p, :]).then_inc(x2_out[p], 16)
                pool.dma_start(h2_dram[t], h2[:, p, :]).then_inc(h2_out[p], 16)
                done = t * 8 + (16 if p == 0 else 8)
                pool.wait_ge(x2_out[p], done)
                pool.wait_ge(h2_out[p], done)
                pool.wait_ge(e["turned"], t + 1)
                pool.sem_inc(e["x2_free"], 1)
                pool.sem_inc(e["h2_free"], 1)

            low_part(0, 0)
            low_part(1, 1)
            with pool.Fori(0, NT // 2 - 1) as i:
                for p in range(2):
                    low_part(i * 2 + (p + 2), p)
                    store(i * 2 + p, p)
            store(NT - 2, 0)
            store(NT - 1, 1)


def dispatch(nc, c, table):
    NR = N_GRP + N_EXP
    with Phase(nc, "route") as ph:
        f = lambda n, *sh: ph.sb(n, [P, *sh])
        gmax, gsum, pg, m1, m2, low, tx, den = (f(n, NT) for n in ("gmax", "gsum", "pg", "m1", "m2", "low", "tx", "den"))
        eg, geq, gv, goh, pen = (f(n, NT, N_GRP) for n in ("eg", "geq", "gv", "goh", "pen"))
        em, em2, eq, val, oh1, oh2, both, rank, weighed = (
            f(n, NT, N_EXP) for n in ("em", "em2", "eq", "val", "oh1", "oh2", "both", "rank", "weighed"))
        base = f("base", NT + 1, N_EXP)
        padded, pend, pstart, ones = (f(n, N_EXP) for n in ("padded", "pend", "pstart", "ones"))
        count_i, pend_i = ph.sb("count_i", [P, N_EXP], I32), ph.sb("pend_i", [P, N_EXP], I32)
        ends, blocks_f = ph.sb("ends", [1, N_EXP]), ph.sb("blocks_f", [1, N_EXP])
        iota_g, iota_e, destf = f("iota_g", N_GRP), f("iota_e", N_EXP), f("destf", NT, 2)
        lo, hi, pos = (ph.sb(n, [P, NT, 2], I32) for n in ("lo", "hi", "pos"))
        tokens, zero = ph.sb("tokens", [P, NT], I32), ph.sb("zero", [P, NB], I32)
        starts, over, owner = ph.sb("starts", [1, NB]), ph.sb("over", [1, NB, N_EXP]), ph.sb("owner", [1, NB])
        within, total = ph.ps("within", [P, NT, N_EXP]), ph.ps("total", [P, NT, N_EXP])
        step, act_done, iotas, zeroed, zero_in, ranked, placed, scattered, counted, loaded = (
            ph.sem(n) for n in ("step", "act_done", "iotas", "zeroed", "zero_in", "ranked", "placed", "scattered", "counted", "loaded"))
        block = ph.block()

        @block.gpsimd
        def _(pool):
            pool.memset(zero[:, :], 0).then_inc(zeroed, 1)
            for out, pat, mult in ((iota_g, [[1, N_GRP]], 0), (iota_e, [[1, N_EXP]], 0), (starts, [[BLK, NB]], 0)):
                pool.iota(out[:, :], pattern=pat, base=0, channel_multiplier=mult, allow_small_or_imprecise_dtypes=True).then_inc(iotas, 1)
            pool.iota(tokens[:, :], pattern=[[P, NT]], base=0, channel_multiplier=1).then_inc(iotas, 1)
            pool.wait_ge(placed, 1)
            pool.wait_ge(zero_in, 16)
            pool.wait_ge(iotas, 4)
            for s in range(2):
                for t in range(NT):
                    pool.indirect_dma_start(out=table, out_offset=bass.IndirectOffsetOnAxis(ap=pos[:, t, s:s + 1], axis=0),
                                            in_=tokens[:, t:t + 1], in_offset=None).then_inc(scattered, 16)
            pool.wait_ge(scattered, 16 * 2 * NT)

        @block.sync
        def _(sp):
            sp.wait_ge(zeroed, 1)
            sp.dma_start(table.rearrange("(p b) a -> p (b a)", b=NB), zero[:, :]).then_inc(zero_in, 16)
            sp.wait_ge(scattered, 16 * 2 * NT)
            sp.dma_start(c.place_token[:, :], table.rearrange("(p b) a -> p (b a)", b=NB)).then_inc(loaded, 16)
            sp.wait_ge(loaded, 16)

        @block.scalar
        def _(act):
            act.wait_ge(step, 2)
            act.activation(eg[:, :, :], eg[:, :, :], ACT.Exp).then_inc(act_done, 1)
            act.wait_ge(counted, 1)
            act.activation(tx[:, :], tx[:, :], ACT.Exp).then_inc(act_done, 1)

        @block.tensor
        def _(pe):
            pe.wait_ge(ranked, 1)
            pe.matmul(within[:, :, :], c.upper[:, :], both[:, :, :], start=True, stop=True)
            pe.matmul(total[:, :, :], c.ones[:, :], both[:, :, :], start=True, stop=True).then_inc(ranked, 1)

        @block.vector
        def _(dve):
            st = Chain(dve, step)

            def do(ins):
                st.did(ins)
                st.wait()

            def wide(ap, n):
                return ap.unsqueeze(2).to_broadcast([P, NT, n])

            def over_tiles(ap, n):
                return ap.unsqueeze(1).to_broadcast([P, NT, n])

            def first_of(eq_, val_, iota, out, n):
                do(dve.scalar_tensor_tensor(out=val_[:, :, :], in0=eq_[:, :, :], scalar=-99.0, in1=over_tiles(iota[:, :], n), op0=ALU.mult, op1=ALU.add))
                do(dve.tensor_reduce(low[:, :], val_[:, :, :], AX.X, ALU.min))
                do(dve.tensor_tensor(out[:, :, :], val_[:, :, :], wide(low[:, :], n), ALU.is_equal))

            g_log, e_log = c.logits[:, :, 0:N_GRP], c.logits[:, :, N_GRP:NR]
            do(dve.tensor_reduce(gmax[:, :], g_log, AX.X, ALU.max))
            do(dve.tensor_tensor(eg[:, :, :], g_log, wide(gmax[:, :], N_GRP), ALU.subtract))
            do(dve.tensor_tensor(geq[:, :, :], g_log, wide(gmax[:, :], N_GRP), ALU.is_equal))
            dve.wait_ge(iotas, 4)
            first_of(geq, gv, iota_g, goh, N_GRP)
            do(dve.tensor_scalar(pen[:, :, :], goh[:, :, :], 1.0, BIG, ALU.subtract, ALU.mult))
            four_d = "p t (g e) -> p t g e"
            do(dve.tensor_tensor(em[:, :, :].rearrange(four_d, g=N_GRP), e_log.rearrange(four_d, g=N_GRP),
                                 pen[:, :, :].unsqueeze(3).to_broadcast([P, NT, N_GRP, PER_GRP]), ALU.add))
            do(dve.tensor_reduce(m1[:, :], em[:, :, :], AX.X, ALU.max))
            do(dve.tensor_tensor(eq[:, :, :], em[:, :, :], wide(m1[:, :], N_EXP), ALU.is_equal))
            first_of(eq, val, iota_e, oh1, N_EXP)
            do(dve.scalar_tensor_tensor(out=em2[:, :, :], in0=oh1[:, :, :], scalar=-2.0 * BIG, in1=em[:, :, :], op0=ALU.mult, op1=ALU.add))
            do(dve.tensor_reduce(m2[:, :], em2[:, :, :], AX.X, ALU.max))
            do(dve.tensor_tensor(eq[:, :, :], em2[:, :, :], wide(m2[:, :], N_EXP), ALU.is_equal))
            first_of(eq, val, iota_e, oh2, N_EXP)
            do(dve.tensor_tensor(both[:, :, :], oh1[:, :, :], oh2[:, :, :], ALU.add))
            dve.sem_inc(ranked, 1)
            do(dve.tensor_tensor(tx[:, :], m2[:, :], m1[:, :], ALU.subtract))
            dve.sem_inc(counted, 1)
            dve.wait_ge(act_done, 2)
            do(dve.tensor_reduce(gsum[:, :], eg[:, :, :], AX.X, ALU.add))
            do(dve.scalar_tensor_tensor(out=den[:, :], in0=tx[:, :], scalar=1.0, in1=gsum[:, :], op0=ALU.add, op1=ALU.mult))
            do(dve.reciprocal(c.gates[:, :, 0], den[:, :]))
            do(dve.tensor_tensor(c.gates[:, :, 1], c.gates[:, :, 0], tx[:, :], ALU.mult))
            dve.wait_ge(ranked, 2)
            do(dve.memset(base[:, 0, :], 0.0))
            for t in range(NT):
                do(dve.tensor_tensor(base[:, t + 1, :], base[:, t, :], total[:, t, :], ALU.add))
            do(dve.tensor_tensor(rank[:, :, :], within[:, :, :], base[:, 0:NT, :], ALU.add))
            do(dve.tensor_scalar(padded[:, :], base[:, NT, :], float(BLK - 1), None, ALU.add))
            do(dve.tensor_copy(count_i[:, :], padded[:, :]))
            do(dve.tensor_scalar(count_i[:, :], count_i[:, :], 7, 7, ALU.logical_shift_right, ALU.logical_shift_left))
            do(dve.tensor_copy(padded[:, :], count_i[:, :]))
            do(dve.memset(ones[:, :], 1.0))
            do(dve.tensor_tensor_scan(pend[:, :], ones[:, :], padded[:, :], 0.0, ALU.mult, ALU.add))
            do(dve.tensor_copy(pend_i[:, :], pend[:, :]))
            do(dve.tensor_tensor(pstart[:, :], pend[:, :], padded[:, :], ALU.subtract))
            do(dve.tensor_tensor(rank[:, :, :], rank[:, :, :], over_tiles(pstart[:, :], N_EXP), ALU.add))
            for s, oh in enumerate((oh1, oh2)):
                do(dve.tensor_tensor(weighed[:, :, :], oh[:, :, :], rank[:, :, :], ALU.mult))
                do(dve.tensor_reduce(destf[:, :, s], weighed[:, :, :], AX.X, ALU.add))
            do(dve.tensor_copy(c.dest[:, :, :], destf[:, :, :]))
            do(dve.tensor_scalar(lo[:, :, :], c.dest[:, :, :], BLK - 1, 6, ALU.bitwise_and, ALU.logical_shift_left))
            do(dve.tensor_scalar(hi[:, :, :], c.dest[:, :, :], 7, None, ALU.logical_shift_right))
            do(dve.tensor_tensor(pos[:, :, :], lo[:, :, :], hi[:, :, :], ALU.bitwise_or))
            dve.sem_inc(placed, 1)
            do(dve.tensor_tensor(over[:, :, :], starts[:, :].unsqueeze(2).to_broadcast([1, NB, N_EXP]),
                                 pend[0:1, :].unsqueeze(1).to_broadcast([1, NB, N_EXP]), ALU.is_ge))
            do(dve.tensor_reduce(owner[:, :], over[:, :, :], AX.X, ALU.add))
            do(dve.tensor_scalar(owner[:, :], owner[:, :], float(N_EXP - 1), None, ALU.min))
            do(dve.tensor_copy(c.block_expert[:, :], owner[:, :]))
            do(dve.tensor_scalar(count_i[0:1, :], pend_i[0:1, :], 7, None, ALU.logical_shift_right))
            do(dve.memset(ends[:, :], 2.0))
            do(dve.tensor_copy(blocks_f[:, :], count_i[0:1, :]))
            do(dve.tensor_scalar(ends[:, SLOTS:], blocks_f[:, 0:N_EXP - SLOTS], 2.0, None, ALU.add))
            do(dve.tensor_copy(c.blocks_before[:, :], ends[:, :]))
            do(dve.tensor_scalar(c.last_step[:, :], pend_i[0:1, N_EXP - 1:N_EXP], BLK, None, ALU.subtract))
            do(dve.tensor_scalar(c.last_step[:, :], c.last_step[:, :], 9, None, ALU.logical_shift_right))


def experts(nc, c, h2_rows, w13, w2, y_dram):
    KE = DE // P
    with Phase(nc, "moe") as ph:
        wa, wb = ph.sb("wa", [P, SLOTS, KD, 2 * DE]), ph.sb("wb", [P, SLOTS, KE, D])
        idx = ph.sb("idx", [P, SLOTS], I32)
        xg, xT = ph.sb("xg", [P, SLOTS, D]), ph.sb("xT", [P, 2, D])
        act1, prod, prodT = ph.sb("act1", [P, 2, DE]), ph.sb("prod", [P, 2, DE]), ph.sb("prodT", [P, 2, DE])
        y = ph.sb("y", [P, 2, D])
        tx = ph.ps("tx", [P, 2, G])
        pu = ph.ps("pu", [P, 2, G])
        tp = ph.ps("tp", [P, G])
        py = ph.ps("py", [P, 2, G])
        wa_in, wb_in, x_in, y_out = ph.sems("wa_in", SLOTS), ph.sems("wb_in", SLOTS), ph.sems("x_in", SLOTS), ph.sems("y_out", 2)
        names = ("idx_ready", "x_turned", "xa", "xv", "up", "silu", "prod", "p_turned", "p_copied", "down", "ya", "yv", "y_free", "alone")
        e = {n: ph.sem(n) for n in names}
        none, cleared, none_ready = ph.sb("none", [P, D]), ph.sem("cleared"), ph.sem("none_ready")
        block = ph.block()

        def last_step(eng):
            return eng.value_load(c.last_step[0:1, 0:1], min_val=2 * T // BLK // SLOTS - 1, max_val=NB // SLOTS - 1)

        @block.sync
        def _(sp):
            with sp.Fori(0, N_EXP // SLOTS) as i:
                for p in range(SLOTS):
                    ex = i * SLOTS + p
                    done = sp.value_load(c.blocks_before[0:1, bass.ds(ex, 1)], min_val=2, max_val=NB + 2)
                    sp.wait_ge(wa_in[p], i * 16 + 16)
                    sp.wait_ge(e["up"], done)
                    sp.dma_start(wa[:, p, :, :], w13[bass.ds(ex, 1)].rearrange("a p k n -> p (a k) n")).then_inc(wa_in[p], 16)
                    sp.wait_ge(wb_in[p], i * 16 + 16)
                    sp.wait_ge(e["down"], done)
                    sp.dma_start(wb[:, p, :, :], w2[bass.ds(ex, 1)].rearrange("a p k n -> p (a k) n")).then_inc(wb_in[p], 16)
            for p in range(SLOTS):
                sp.wait_ge(wa_in[p], N_EXP // SLOTS * 16 + 16)
                sp.wait_ge(wb_in[p], N_EXP // SLOTS * 16 + 16)

        @block.gpsimd
        def _(pool):
            def gather(t, n):
                pool.wait_ge(e["x_turned"], t + 1)
                pool.sem_inc(e["alone"], 1)
                pool.tensor_copy(idx[:, n:n + 1], c.place_token[:, bass.ds(t, 1)]).then_inc(e["idx_ready"], 1)
                pool.wait_ge(e["idx_ready"], t + 1)
                pool.sem_inc(e["alone"], 1)
                pool.indirect_dma_start(out=xg[:, n, :], out_offset=None, in_=h2_rows,
                                        in_offset=bass.IndirectOffsetOnAxis(ap=idx[:, n:n + 1], axis=0)).then_inc(x_in[n], 16)

            last = last_step(pool)
            pool.memset(none[:, :], 0.0).then_inc(none_ready, 1)
            for n in range(SLOTS):
                gather(n, n)
            with pool.Fori(1, NB // SLOTS) as i:
                with pool.If(i < last + 1):
                    for n in range(SLOTS):
                        gather(i * SLOTS + n, n)

        @block.tensor
        def _(pe):
            pe.sem_inc(e["x_turned"], SLOTS)
            for n in ("up", "p_turned", "down"):
                pe.sem_inc(e[n], 2)
            for n in range(SLOTS):
                pe.sem_inc(wa_in[n], 16)
                pe.sem_inc(wb_in[n], 16)
            last = last_step(pe)

            def expert_of(t):
                here = c.block_expert[0:1, t:t + 1] if isinstance(t, int) else c.block_expert[0:1, bass.ds(t, 1)]
                return pe.value_load(here, min_val=0, max_val=N_EXP - 1)

            def slot_of(ex, arrived):
                for n in range(SLOTS):
                    pe.wait_ge(arrived[n], (ex + (SLOTS - n)) // SLOTS * 16 + 16)
                return ex % SLOTS

            def turn_x(t, n):
                pe.wait_ge(x_in[n], t * (16 // SLOTS) + (16 - n * (16 // SLOTS)))
                pe.wait_ge(e["xa"], t + 1)
                pe.wait_ge(e["xv"], t + 1)
                for k in range(KD):
                    done = pe.transpose(tx[:, k // 4, k % 4 * P:(k % 4 + 1) * P], xg[:, n, k * P:(k + 1) * P], c.ident[:, :])
                done.then_inc(e["x_turned"], 1)

            def up(t, p):
                ex = expert_of(t)
                pe.wait_ge(e["xa"], t + 2)
                pe.wait_ge(e["xv"], t + 2)
                slot = slot_of(ex, wa_in)
                pe.wait_ge(e["prod"], t + 1)
                for k in range(KD):
                    last = pe.matmul(pu[:, p, :], xT[:, p, k * P:(k + 1) * P], wa[:, bass.ds(slot, 1), k, :].rearrange("p a n -> p (a n)"), start=(k == 0), stop=(k == KD - 1))
                last.then_inc(e["up"], 1)

            def turn_prod(t, p):
                pe.wait_ge(e["prod"], t + 3)
                pe.wait_ge(e["p_copied"], t + 1)
                for k in range(KE):
                    last = pe.transpose(tp[:, k * P:(k + 1) * P], prod[:, p, k * P:(k + 1) * P], c.ident[:, :])
                last.then_inc(e["p_turned"], 1)

            def down(t, p):
                ex = expert_of(t)
                pe.wait_ge(e["p_copied"], t + 2)
                slot = slot_of(ex, wb_in)
                pe.wait_ge(e["ya"], t + 1)
                pe.wait_ge(e["yv"], t + 1)
                for cols in range(2):
                    for k in range(KE):
                        last = pe.matmul(py[:, cols, :], prodT[:, p, k * P:(k + 1) * P],
                                         wb[:, bass.ds(slot, 1), k, cols * G:(cols + 1) * G].rearrange("p a n -> p (a n)"),
                                         start=(k == 0), stop=(k == KE - 1))
                last.then_inc(e["down"], 1)

            def both(t, n):
                up(t + 1, 1 - n % 2)
                turn_prod(t, n % 2)
                turn_x(t + 2, (n + 2) % SLOTS)
                down(t, n % 2)

            turn_x(0, 0)
            up(0, 0)
            turn_x(1, 1)
            with pe.Fori(1, NB // SLOTS) as i:
                with pe.If(i < last + 1):
                    for n in range(SLOTS):
                        both(i * SLOTS - (SLOTS - n), n)
            both(last * SLOTS, 0)
            both(last * SLOTS + 1, 1)
            up(last * SLOTS + 3, 1)
            turn_prod(last * SLOTS + 2, 0)
            down(last * SLOTS + 2, 0)
            turn_prod(last * SLOTS + 3, 1)
            down(last * SLOTS + 3, 1)

        @block.scalar
        def _(act):
            act.sem_inc(e["xa"], 1)
            act.sem_inc(e["p_copied"], 1)
            act.sem_inc(e["ya"], 1)
            last = last_step(act)

            def copy_x(t, p):
                act.wait_ge(e["x_turned"], t + (SLOTS + 1))
                act.wait_ge(e["up"], t + 1)
                act.activation(xT[:, p, 0:G], tx[:, 0, :], ACT.Copy).then_inc(e["xa"], 1)

            def silu(t, p):
                act.wait_ge(e["up"], t + 3)
                act.wait_ge(e["prod"], t + 1)
                act.activation(act1[:, p, :], pu[:, p, 0:DE], ACT.Silu).then_inc(e["silu"], 1)

            def copy_prod(t, p):
                act.wait_ge(e["p_turned"], t + 3)
                act.wait_ge(e["down"], t + 1)
                act.activation(prodT[:, p, :], tp[:, 0:DE], ACT.Copy).then_inc(e["p_copied"], 1)

            def copy_y(t, p):
                act.wait_ge(e["down"], t + 3)
                act.wait_ge(e["y_free"], t + 1)
                act.activation(y[:, p, 0:G], py[:, 0, :], ACT.Copy).then_inc(e["ya"], 1)
                act.wait_ge(e["ya"], t + 2)
                act.wait_ge(e["yv"], t + 2)
                act.sem_inc(e["alone"], 1)
                act.dma_start(y_dram[t], y[:, p, :]).then_inc(y_out[p], 16)

            def both(t, n):
                p = n % 2
                silu(t + 1, 1 - p)
                copy_prod(t, p)
                copy_x(t + 2, p)
                copy_y(t, p)

            act.wait_ge(none_ready, 1)
            copy_x(0, 0)
            silu(0, 0)
            copy_x(1, 1)
            with act.Fori(1, NB // SLOTS) as i:
                with act.If(i < last + 1):
                    for n in range(SLOTS):
                        both(i * SLOTS - (SLOTS - n), n)
                    act.sem_inc(cleared, 16 * SLOTS)
                with act.If(last < i):
                    for n in range(SLOTS):
                        act.dma_start(y_dram[i * SLOTS + n], none[:, :]).then_inc(cleared, 16)
            both(last * SLOTS, 0)
            both(last * SLOTS + 1, 1)
            silu(last * SLOTS + 3, 1)
            copy_prod(last * SLOTS + 2, 0)
            copy_y(last * SLOTS + 2, 0)
            copy_prod(last * SLOTS + 3, 1)
            copy_y(last * SLOTS + 3, 1)
            for p in range(2):
                act.wait_ge(y_out[p], last * (8 * SLOTS) + (8 * SLOTS + 16))
            act.wait_ge(cleared, (NB - SLOTS) * 16)
            act.sem_inc(e["alone"], 1)

        @block.vector
        def _(dve):
            dve.sem_inc(e["xv"], 1)
            dve.sem_inc(e["yv"], 1)
            dve.sem_inc(e["prod"], 2)
            for p in range(2):
                dve.sem_inc(y_out[p], 16)
            last = last_step(dve)

            def copy_x(t, p):
                dve.wait_ge(e["x_turned"], t + (SLOTS + 1))
                dve.wait_ge(e["up"], t + 1)
                dve.tensor_copy(xT[:, p, G:], tx[:, 1, :]).then_inc(e["xv"], 1)

            def multiply(t, p):
                dve.wait_ge(e["silu"], t + 1)
                dve.wait_ge(e["p_turned"], t + 1)
                dve.tensor_tensor(prod[:, p, :], pu[:, p, DE:], act1[:, p, :], ALU.mult).then_inc(e["prod"], 1)

            def copy_y(t, p):
                dve.wait_ge(e["down"], t + 3)
                dve.wait_ge(y_out[p], t * 8 + (16 if p == 0 else 8))
                dve.sem_inc(e["y_free"], 1)
                dve.tensor_copy(y[:, p, G:], py[:, 1, :]).then_inc(e["yv"], 1)

            def both(t, n):
                p = n % 2
                multiply(t + 1, 1 - p)
                copy_x(t + 2, p)
                copy_y(t, p)

            copy_x(0, 0)
            multiply(0, 0)
            copy_x(1, 1)
            with dve.Fori(1, NB // SLOTS) as i:
                with dve.If(i < last + 1):
                    for n in range(SLOTS):
                        both(i * SLOTS - (SLOTS - n), n)
            both(last * SLOTS, 0)
            both(last * SLOTS + 1, 1)
            multiply(last * SLOTS + 3, 1)
            copy_y(last * SLOTS + 2, 0)
            copy_y(last * SLOTS + 3, 1)


def combine(nc, c, x2_dram, y_rows, nl_row, out):
    B = 4
    with Phase(nc, "comb") as ph:
        nl = ph.sb("nl", [P, D])
        dest = ph.sb("dest", [P, B, 2], I32)
        gate = ph.sb("gate", [P, B, 2])
        x2, ys = ph.sb("x2", [P, B, D]), ph.sb("ys", [P, B, 2, D])
        one, sum_, res, junk = ph.sb("one", [P, B, D]), ph.sb("sum", [P, B, D]), ph.sb("res", [P, B, D]), ph.sb("junk", [P, D])
        ss, sd, rs = ph.sb("ss", [P, B]), ph.sb("sd", [P, B]), ph.sb("rs", [P, B])
        nl_in, x_in, y_in, stored = ph.sem("nl_in"), ph.sems("x_in", B), ph.sems("y_in", B), ph.sems("stored", B)
        names = ("free", "dest_ready", "gate_ready", "half", "summed", "squared", "sd_done", "rs_done", "ready", "alone")
        e = {n: ph.sem(n) for n in names}
        block = ph.block()

        @block.sync
        def _(sp):
            sp.dma_start(nl[:, :], nl_row.to_broadcast([P, D])).then_inc(nl_in, 16)

            def load(t, p):
                sp.wait_ge(e["free"], t + 1)
                sp.dma_start(x2[:, p, :], x2_dram[t]).then_inc(x_in[p], 16)

            def store(t, p):
                sp.wait_ge(e["ready"], t + 1)
                sp.dma_start(out[t], res[:, p, :]).then_inc(stored[p], 16)

            for p in range(B):
                load(p, p)
            with sp.Fori(0, NT // B - 1) as i:
                for p in range(B):
                    store(i * B + p, p)
                    load(i * B + (p + B), p)
            for p in range(B):
                store(NT - B + p, p)
            for p in range(B):
                sp.wait_ge(stored[p], NT // B * 16 + 16)

        @block.gpsimd
        def _(pool):
            with pool.Fori(0, NT // B) as i:
                for p in range(B):
                    t = i * B + p
                    pool.wait_ge(e["free"], t + 1)
                    pool.sem_inc(e["alone"], 1)
                    pool.tensor_copy(dest[:, p, :], c.dest[:, bass.ds(t, 1), :].rearrange("p a s -> p (a s)")).then_inc(e["dest_ready"], 1)
                    pool.wait_ge(e["dest_ready"], t + 1)
                    pool.sem_inc(e["alone"], 1)
                    for s in range(2):
                        pool.indirect_dma_start(out=ys[:, p, s, :], out_offset=None, in_=y_rows,
                                                in_offset=bass.IndirectOffsetOnAxis(ap=dest[:, p, s:s + 1], axis=0)).then_inc(y_in[p], 16)

        @block.scalar
        def _(act):
            act.sem_inc(e["sd_done"], 1)
            with act.Fori(0, NT // B) as i:
                for p in range(B):
                    n = i * B + (p + 1)
                    act.wait_ge(e["summed"], n)
                    act.wait_ge(e["sd_done"], n)
                    act.activation(junk[:, :], sum_[:, p, :], ACT.Square, accum_out=ss[:, p:p + 1]).then_inc(e["squared"], 1)
                    act.wait_ge(e["squared"], n)
                    act.activation(sd[:, p:p + 1], ss[:, p:p + 1], ACT.Sqrt, scale=1.0 / D, bias=c.eps[:, 0:1]).then_inc(e["sd_done"], 1)

        @block.vector
        def _(dve):
            dve.sem_inc(e["free"], B)
            for p in range(B):
                dve.sem_inc(stored[p], 16)
            dve.wait_ge(nl_in, 16)

            def add(t, p, i):
                dve.wait_ge(x_in[p], i * 16 + 16)
                dve.wait_ge(y_in[p], i * 32 + 32)
                dve.tensor_copy(gate[:, p, :], tile_of(c.gates, t).rearrange("p a s -> p (a s)")).then_inc(e["gate_ready"], 1)
                dve.wait_ge(e["gate_ready"], t + 1)
                dve.scalar_tensor_tensor(out=one[:, p, :], in0=ys[:, p, 0, :], scalar=gate[:, p, 0:1], in1=x2[:, p, :], op0=ALU.mult,
                                         op1=ALU.add).then_inc(e["half"], 1)
                dve.wait_ge(e["half"], t + 1)
                dve.scalar_tensor_tensor(out=sum_[:, p, :], in0=ys[:, p, 1, :], scalar=gate[:, p, 1:2], in1=one[:, p, :], op0=ALU.mult,
                                         op1=ALU.add).then_inc(e["summed"], 1)
                dve.wait_ge(e["summed"], t + 1)
                dve.sem_inc(e["free"], 1)

            def finish(t, p, i):
                dve.wait_ge(e["sd_done"], t + 2)
                dve.reciprocal(rs[:, p:p + 1], sd[:, p:p + 1]).then_inc(e["rs_done"], 1)
                dve.wait_ge(e["rs_done"], t + 1)
                dve.wait_ge(stored[p], i * 16 + 16)
                dve.scalar_tensor_tensor(out=res[:, p, :], in0=sum_[:, p, :], scalar=rs[:, p:p + 1], in1=nl[:, :], op0=ALU.mult,
                                         op1=ALU.mult).then_inc(e["ready"], 1)

            with dve.Fori(0, NT // B) as i:
                for p in range(B):
                    add(i * B + p, p, i)
                    if p:
                        finish(i * B + (p - 1), p - 1, i)
                finish(i * B + (B - 1), B - 1, i)


class Constants:
    pass


def build(nc, a):
    rows_dram = nc.dram_tensor("gate_rows", (R_ALL, T), F32, kind="Internal").ap()
    kept = nc.dram_tensor("kept", (SHORT_BLOCKS, P, T), F32, kind="Internal").ap()
    wide = nc.dram_tensor("wide", (KC * STEP, P, T), F32, kind="Internal").ap()
    with ExitStack() as ctx:
        c = Constants()

        def sb(name, shape, dt=F32):
            return ctx.enter_context(nc.sbuf_tensor(name, shape, dt))

        c.ident, c.ones, c.eps = sb("ident", [P, P]), sb("ones", [P, P]), sb("eps", [P, 1])
        c.negtri, c.upper, c.past = sb("negtri", [P, P]), sb("upper", [P, P]), sb("past", [P, P])
        c.below, c.above = sb("below", [P, LEVELS, P]), sb("above", [P, LEVELS, P])
        c.cols = sb("cols", [P, NT, R_ALL])
        x2_dram = nc.dram_tensor("x2", (NT, P, D), F32, kind="Internal").ap()
        h2_dram = nc.dram_tensor("h2", (NT, P, D), F32, kind="Internal").ap()
        y_dram = nc.dram_tensor("y_blocks", (NB, P, D), F32, kind="Internal").ap()
        table = nc.dram_tensor("place_table", (NB * P, 1), I32, kind="Internal").ap()
        c.logits, c.gates = sb("logits", [P, NT, N_GRP + N_EXP]), sb("gates", [P, NT, 2])
        c.dest, c.block_expert = sb("dest", [P, NT, 2], I32), sb("block_expert", [1, NB], I32)
        c.blocks_before, c.last_step = sb("blocks_before", [1, N_EXP], I32), sb("last_step", [1, 1], I32)
        c.place_token = sb("place_token", [P, NB], I32)
        x = a["x"].rearrange("(t p) d -> t p d", p=P)
        constants(nc, c)
        with ExitStack() as projecting:
            c.h_hi, c.h_lo = (projecting.enter_context(nc.sbuf_tensor(n, [P, KD, T], F32R)) for n in ("h_hi", "h_lo"))
            norm_and_transpose(nc, c, x, a["nm_col"])
            narrow_rows(nc, c, a["w_narrow"], a["sm_bias"], a["a_log"], rows_dram)
            project_blocks(nc, c, a["w_blocks"], a["dw_w"], a["dw_b"], wide)
            short_conv(nc, c, a["w_blocks"], a["short_w"], Q_A, 2 * H, kept, True)
            short_conv(nc, c, a["w_blocks"], a["short_w"], V_A, H, kept, False)
        with nc.sbuf_tensor("merged", [P, KD, T], F32) as merged:
            with nc.sbuf_tensor("oT", [P, KC, T], F32) as oT:
                conformer_norm(nc, c, oT, wide, a["ln_g"], a["ln_b"])
                gated_merge(nc, c, oT, wide, a["w_mix"], 2, merged, True)
                forgetting_attention(nc, c, oT, wide, rows_dram)
                gated_merge(nc, c, oT, wide, a["w_mix"], 1, merged, False)
                delta_rule(nc, c, oT, kept, wide, rows_dram, a["dn_norm"])
                gated_merge(nc, c, oT, wide, a["w_mix"], 0, merged, False)
            output_and_router(nc, c, merged, x, a["w_out"], a["nf_row"], a["w_router"], a["b_router"], x2_dram, h2_dram)
        dispatch(nc, c, table)
        experts(nc, c, h2_dram.rearrange("t p d -> (t p) d"), a["w13"], a["w2"], y_dram)
        combine(nc, c, x2_dram, y_dram.rearrange("b p d -> (b p) d"), a["nl_row"], a["out"])


def lay_out(i):
    f = np.float32
    g = {k: np.asarray(v) for k, v in i.items()}
    w_in = g["w_in"][0]
    sizes = (512, 512, 512, 512, H, H, 512, 512, 512, H, 1024, D, D, D)
    at = np.cumsum((0,) + sizes)
    wide = [w_in[:, at[n]:at[n + 1]] for n in (0, 1, 2, 3, 6, 7, 8, 10, 11, 12, 13)]
    narrow = np.zeros((D, R_ALL), f)
    for row, n in ((R_BETA, 4), (R_DECAY, 5), (R_FORGET, 9)):
        narrow[:, row:row + H] = w_in[:, at[n]:at[n + 1]]

    def blocks(w):
        k, n = w.shape
        return np.ascontiguousarray(w.reshape(k // P, P, n // P, P).transpose(2, 1, 0, 3))

    def rows(w):
        return np.ascontiguousarray(w.reshape(w.shape[0] // P, P, -1).transpose(1, 0, 2))

    def cols(v):
        return np.ascontiguousarray(v.reshape(-1, P).T)

    z_a, q_b, k_b, v_b, conf, gate_a, gate_b, gate_c = (blocks(w) for w in wide[3:])
    steps = [np.stack([conf[KC + j], conf[j], *gate_a[2 * j:2 * j + 2], *gate_b[2 * j:2 * j + 2], *gate_c[2 * j:2 * j + 2],
                       z_a[j], q_b[j], k_b[j], v_b[j]]) for j in range(KC)]

    sm_bias, a_log = np.zeros((R_ALL, 1), f), np.zeros((R_ALL, 1), f)
    sm_bias[R_DECAY:R_DECAY + H, 0] = g["dn_dt_bias"][0]
    sm_bias[R_FORGET:R_FORGET + H, 0] = g["fox_bias"][0]
    a_log[R_DECAY:R_DECAY + H, 0] = g["dn_a_log"][0]
    w13 = np.concatenate([g["expert_w1"][0], g["expert_w3"][0]], axis=-1)
    return {
        "x": np.ascontiguousarray(g["x"].reshape(T, D)),
        "nm_col": cols(g["norm_mix"][0]),
        "w_blocks": np.concatenate([blocks(w) for w in wide[:3]] + steps),
        "w_narrow": rows(narrow),
        "sm_bias": sm_bias,
        "a_log": a_log,
        "short_w": np.ascontiguousarray(g["conv_qkv"][0].reshape(W_SHORT, 12, P).transpose(2, 1, 0)),
        "dw_w": np.ascontiguousarray(g["conv_dw"][0].reshape(W_CONV, KC, P).transpose(2, 1, 0)),
        "dw_b": cols(g["conv_dw_b"][0]),
        "ln_g": cols(g["conv_ln_g"][0]),
        "ln_b": cols(g["conv_ln_b"][0]),
        "dn_norm": cols(g["dn_norm"][0]),
        "w_mix": np.concatenate([blocks(g[n][0]) for n in ("w_a", "w_b", "w_c")]),
        "w_out": rows(g["w_out"][0]),
        "nf_row": g["norm_ffn"].reshape(1, D),
        "w_router": rows(np.concatenate([g["router_group_w"][0], g["router_expert_w"][0]], axis=1)),
        "b_router": np.concatenate([g["router_group_b"], g["router_expert_b"]], axis=1),
        "w13": np.ascontiguousarray(w13.reshape(N_EXP, KD, P, 2 * DE).transpose(0, 2, 1, 3)),
        "w2": np.ascontiguousarray(g["expert_w2"][0].reshape(N_EXP, DE // P, P, D).transpose(0, 2, 1, 3)),
        "nl_row": g["norm_final"].reshape(1, D),
    }


def kernel(**inputs):
    import concourse.bacc as _bacc
    from concourse.bass_utils import run_bass_kernel_spmd as _run

    nc = _bacc.Bacc("TRN2", target_bir_lowering=False, num_devices=1)
    arrays = {f"in_{n}_dram": v for n, v in lay_out(inputs).items()}
    a = {n[3:-5]: nc.dram_tensor(n, v.shape, mybir.dt.from_np(v.dtype), kind="ExternalInput").ap() for n, v in arrays.items()}
    a["out"] = nc.dram_tensor("out_0_dram", (NT, P, D), F32, kind="ExternalOutput").ap()
    build(nc, a)
    r = _run(nc, [arrays], core_ids=[0])
    return r.results[0]["out_0_dram"].reshape(1, T, D)
```
